# Optimizing a Trainium2 kernel written in Bass

```python
import math
import jax
import jax.numpy as jnp
from jax import lax
import numpy as np

D_MODEL = 1024
BATCH = 1
SEQ = 256
DEPTH = 1
DEC_BATCH = 8
DEC_SEQ = 1
PAST_LEN = 256
PAGE_SIZE = 128

N_HEADS = 16
N_KV_HEADS = 8
HEAD_DIM = 64
ATT_WIDTH = N_HEADS * HEAD_DIM
KV_WIDTH = N_KV_HEADS * HEAD_DIM
Q_BLOCK = 128
FORGET_BIAS_INIT = 3.0
SSM_EXPAND = 2
D_INNER = SSM_EXPAND * D_MODEL
SSM_HEAD_DIM = 64
SSM_HEADS = D_INNER // SSM_HEAD_DIM
SSM_GROUPS = 4
D_STATE = 128
CONV_WIDTH = 4
CONV_DIM = D_INNER + 2 * SSM_GROUPS * D_STATE
SSD_CHUNK = 128
N_EXPERTS = 16
N_EXPERT_GROUPS = 4
EXPERTS_PER_GROUP = N_EXPERTS // N_EXPERT_GROUPS
TOP_K = 2
D_FF_EXPERT = D_MODEL // 2
IN_SIZES = (ATT_WIDTH, KV_WIDTH, KV_WIDTH, N_HEADS, D_INNER, CONV_DIM, SSM_HEADS, D_MODEL, D_MODEL)
IN_DIM = ATT_WIDTH + 2 * KV_WIDTH + N_HEADS + D_INNER + CONV_DIM + SSM_HEADS + 2 * D_MODEL
EPS = 1e-6

kernel_name = 'fox_ssd_gated_moe_adaln_decode_step'

def _block(n, size):
    return size if n % size == 0 else n

def split_cols(p, sizes):
    out, o = [], 0
    for s in sizes:
        out.append(p[..., o:o + s])
        o += s
    return out

def rms_norm(x, g):
    xf = x.astype(jnp.float32)
    y = xf * lax.rsqrt(jnp.mean(xf * xf, axis=-1, keepdims=True) + EPS)
    return y.astype(x.dtype) * g

def forgetting_attention(q, cf_q, qpos, k, v, cf_k):
    b, lq = q.shape[0], q.shape[1]
    lk = k.shape[1]
    r = N_HEADS // N_KV_HEADS
    blk = _block(lq, Q_BLOCK)
    nb = lq // blk
    qb = q.reshape(b, nb, blk, N_KV_HEADS, r, HEAD_DIM).transpose(1, 0, 2, 3, 4, 5)
    cqb = cf_q.reshape(b, nb, blk, N_KV_HEADS, r).transpose(1, 0, 3, 4, 2)
    pb = qpos.reshape(nb, blk)
    ck = cf_k.reshape(b, lk, N_KV_HEADS, r).transpose(0, 2, 3, 1)
    kpos = jnp.arange(lk)
    scale = HEAD_DIM ** -0.5

    def one_block(args):
        qi, ci, pi = args
        s = jnp.einsum('bqgrd,bkgd->bgrqk', qi, k).astype(jnp.float32) * scale
        s = s + ci[..., :, None] - ck[..., None, :]
        s = jnp.where(kpos[None, :] <= pi[:, None], s, -jnp.inf)
        p = jax.nn.softmax(s, axis=-1).astype(v.dtype)
        return jnp.einsum('bgrqk,bkgd->bqgrd', p, v)

    o = lax.map(one_block, (qb, cqb, pb))
    return o.transpose(1, 0, 2, 3, 4, 5).reshape(b, lq, ATT_WIDTH)

def ssd_scan(xs, dt, a, bm, cm, s0, chunk):
    b, l, g, r, p = xs.shape
    nc = l // chunk
    ch = lambda t: t.reshape((b, nc, chunk) + t.shape[2:])
    xd = ch(xs * dt[..., None])
    acs = jnp.cumsum(ch(dt * a), axis=2)
    bm, cm = ch(bm), ch(cm)
    tri = jnp.tril(jnp.ones((chunk, chunk), dtype=bool))[:, :, None, None]
    seg = acs[:, :, :, None] - acs[:, :, None, :]
    lmat = jnp.exp(jnp.where(tri, seg, -jnp.inf))
    cb = jnp.einsum('bctgn,bcsgn->bctsg', cm, bm)
    y_diag = jnp.einsum('bctsg,bctsgr,bcsgrp->bctgrp', cb, lmat, xd)
    decay_end = jnp.exp(acs[:, :, -1:] - acs)
    st = jnp.einsum('bcsgn,bcsgr,bcsgrp->cbgrpn', bm, decay_end, xd)
    cdec = jnp.exp(acs[:, :, -1]).transpose(1, 0, 2, 3)

    def step(s, inp):
        st_c, d_c = inp
        return s * d_c[..., None, None] + st_c, s

    s_fin, s_prev = lax.scan(step, s0, (st, cdec))
    y_off = jnp.einsum('bctgn,bctgr,cbgrpn->bctgrp', cm, jnp.exp(acs), s_prev)
    return (y_diag + y_off).reshape(b, l, g, r, p), s_fin

def mamba2_branch(z, xbc, dtr, ssm0, conv0, w):
    b, l = xbc.shape[0], xbc.shape[1]
    r = SSM_HEADS // SSM_GROUPS
    f32 = jnp.float32
    xa = jnp.concatenate([conv0.astype(xbc.dtype), xbc], axis=1)
    conv = w['conv_b'] + sum(xa[:, i:i + l] * w['conv_w'][i] for i in range(CONV_WIDTH))
    conv_new = xa[:, xa.shape[1] - (CONV_WIDTH - 1):]
    u = jax.nn.silu(conv)
    xs, bm, cm = split_cols(u, (D_INNER, SSM_GROUPS * D_STATE, SSM_GROUPS * D_STATE))
    xs = xs.reshape(b, l, SSM_GROUPS, r, SSM_HEAD_DIM).astype(f32)
    bm = bm.reshape(b, l, SSM_GROUPS, D_STATE).astype(f32)
    cm = cm.reshape(b, l, SSM_GROUPS, D_STATE).astype(f32)
    dt = jax.nn.softplus(dtr.astype(f32) + w['dt_bias'].astype(f32)).reshape(b, l, SSM_GROUPS, r)
    a = -jnp.exp(w['a_log'].astype(f32)).reshape(SSM_GROUPS, r)
    s0 = ssm0.astype(f32).reshape(b, SSM_GROUPS, r, SSM_HEAD_DIM, D_STATE)
    y, s_fin = ssd_scan(xs, dt, a, bm, cm, s0, _block(l, SSD_CHUNK))
    y = y + w['d_skip'].astype(f32).reshape(SSM_GROUPS, r)[..., None] * xs
    y = y.reshape(b, l, D_INNER) * jax.nn.silu(z.astype(f32))
    yg = y.reshape(b, l, SSM_GROUPS, D_INNER // SSM_GROUPS)
    yg = yg * lax.rsqrt(jnp.mean(yg * yg, axis=-1, keepdims=True) + EPS)
    y = yg.reshape(b, l, D_INNER).astype(z.dtype) * w['g_ssm']
    s_new = s_fin.reshape(b, SSM_HEADS, SSM_HEAD_DIM, D_STATE).astype(z.dtype)
    return y, s_new, conv_new

def grouped_moe(h, w_router, b_router, w_gate, w_up, w_down):
    shp = h.shape
    t = h.reshape(-1, shp[-1])
    f32 = jnp.float32
    logits = (t @ w_router).astype(f32) + b_router.astype(f32)
    probs = jax.nn.softmax(logits, axis=-1)
    pg = probs.reshape(-1, N_EXPERT_GROUPS, EXPERTS_PER_GROUP)
    gsel = jnp.argmax(jnp.max(pg, axis=-1), axis=-1)
    pin = jnp.take_along_axis(pg, gsel[:, None, None], axis=1)[:, 0]
    vals, idx = lax.top_k(pin, TOP_K)
    wts = vals / jnp.sum(vals, axis=-1, keepdims=True)
    eid = gsel[:, None] * EXPERTS_PER_GROUP + idx
    comb = jnp.sum(jax.nn.one_hot(eid, N_EXPERTS, dtype=f32) * wts[..., None], axis=1)
    act = jax.nn.silu(jnp.einsum('td,edf->tef', t, w_gate)) * jnp.einsum('td,edf->tef', t, w_up)
    act = act * comb.astype(act.dtype)[..., None]
    y = jnp.einsum('tef,efd->td', act, w_down)
    return y.reshape(shp)

def layer(x, c, past, ssm0, conv0, w, w_router, b_router):
    b, l = x.shape[0], x.shape[1]
    mod = jax.nn.silu(c) @ w['w_mod'] + w['b_mod']
    sh1, sc1, gt1, sh2, sc2, gt2 = [m[:, None, :] for m in jnp.split(mod, 6, axis=-1)]
    h = rms_norm(x, w['g_norm1']) * (1 + sc1) + sh1
    proj = h @ w['w_in']
    q, k, v, fl, z, xbc, dtr, ga, gb = split_cols(proj, IN_SIZES)
    q = rms_norm(q.reshape(b, l, N_HEADS, HEAD_DIM), w['g_q'])
    k = rms_norm(k.reshape(b, l, N_KV_HEADS, HEAD_DIM), w['g_k'])
    v = v.reshape(b, l, N_KV_HEADS, HEAD_DIM)
    logf = jax.nn.log_sigmoid(fl.astype(jnp.float32) + w['b_f'].astype(jnp.float32))
    if past is None:
        k_all, v_all, lf_all = k, v, logf
    else:
        k_all = jnp.concatenate([past[0].astype(k.dtype), k], axis=1)
        v_all = jnp.concatenate([past[1].astype(v.dtype), v], axis=1)
        lf_all = jnp.concatenate([past[2].astype(jnp.float32), logf], axis=1)
    cf = jnp.cumsum(lf_all, axis=1)
    qpos = (k_all.shape[1] - l) + jnp.arange(l)
    o_att = forgetting_attention(q, cf[:, cf.shape[1] - l:], qpos, k_all, v_all, cf)
    y_ssm, ssm_new, conv_new = mamba2_branch(z, xbc, dtr, ssm0, conv0, w)
    m = jax.nn.sigmoid(ga) * (o_att @ w['w_pa']) + jax.nn.sigmoid(gb) * (y_ssm @ w['w_pb'])
    x = x + gt1 * (m @ w['w_o'])
    h2 = rms_norm(x, w['g_norm2']) * (1 + sc2) + sh2
    x = x + gt2 * grouped_moe(h2, w_router, b_router, w['w_gate'], w['w_up'], w['w_down'])
    return x, (k, v, logf.astype(x.dtype), ssm_new, conv_new)

def setup_inputs(seed: int = 0) -> dict:
    key = jax.random.key(seed)
    ks = iter(jax.random.split(key, 48))
    f32 = jnp.float32
    n_pages = PAST_LEN // PAGE_SIZE
    n_pool = (DEC_BATCH * n_pages * 5 + 3) // 4

    def nrm(shape, scale):
        return jax.random.normal(next(ks), shape, f32) * scale

    x_prompt = nrm((BATCH, SEQ, D_MODEL), 1.0)
    x_sample = nrm((DEC_BATCH, DEC_SEQ, D_MODEL), 1.0)
    cache_k = nrm((DEPTH, n_pool, PAGE_SIZE, N_KV_HEADS, HEAD_DIM), 1.0)
    cache_v = nrm((DEPTH, n_pool, PAGE_SIZE, N_KV_HEADS, HEAD_DIM), 1.0)
    cache_logf = jax.nn.log_sigmoid(FORGET_BIAS_INIT + nrm((DEPTH, n_pool, PAGE_SIZE, N_HEADS), 1.0))
    state_ssm = nrm((DEPTH, DEC_BATCH, SSM_HEADS, SSM_HEAD_DIM, D_STATE), 0.1)
    state_conv = nrm((DEPTH, DEC_BATCH, CONV_WIDTH - 1, CONV_DIM), 1.0)
    perm = jax.random.permutation(next(ks), n_pool)
    page_table = perm[:DEC_BATCH * n_pages].reshape(DEC_BATCH, n_pages).astype(jnp.int32)
    c_prompt = nrm((BATCH, D_MODEL), 1.0)
    c_sample = nrm((DEC_BATCH, D_MODEL), 1.0)
    w_mod = nrm((DEPTH, D_MODEL, 6 * D_MODEL), 0.5 * D_MODEL ** -0.5)
    b_mod = nrm((DEPTH, 6 * D_MODEL), 0.02)
    g_norm1 = 1.0 + nrm((DEPTH, D_MODEL), 0.05)
    g_norm2 = 1.0 + nrm((DEPTH, D_MODEL), 0.05)
    w_in = nrm((DEPTH, D_MODEL, IN_DIM), D_MODEL ** -0.5)
    b_f = FORGET_BIAS_INIT + nrm((DEPTH, N_HEADS), 0.5)
    g_q = 1.0 + nrm((DEPTH, HEAD_DIM), 0.05)
    g_k = 1.0 + nrm((DEPTH, HEAD_DIM), 0.05)
    conv_w = nrm((DEPTH, CONV_WIDTH, CONV_DIM), CONV_WIDTH ** -0.5)
    conv_b = nrm((DEPTH, CONV_DIM), 0.02)
    dt0 = jnp.exp(jax.random.uniform(next(ks), (DEPTH, SSM_HEADS), f32, math.log(1e-3), math.log(1e-1)))
    dt_bias = dt0 + jnp.log(-jnp.expm1(-dt0))
    a_log = jnp.log(jax.random.uniform(next(ks), (DEPTH, SSM_HEADS), f32, 1.0, 16.0))
    d_skip = 1.0 + nrm((DEPTH, SSM_HEADS), 0.1)
    g_ssm = 1.0 + nrm((DEPTH, D_INNER), 0.05)
    w_pa = nrm((DEPTH, ATT_WIDTH, D_MODEL), ATT_WIDTH ** -0.5)
    w_pb = nrm((DEPTH, D_INNER, D_MODEL), D_INNER ** -0.5)
    w_o = nrm((DEPTH, D_MODEL, D_MODEL), D_MODEL ** -0.5)
    w_router = nrm((D_MODEL, N_EXPERTS), D_MODEL ** -0.5)
    b_router = nrm((N_EXPERTS,), 0.01)
    w_gate = nrm((DEPTH, N_EXPERTS, D_MODEL, D_FF_EXPERT), D_MODEL ** -0.5)
    w_up = nrm((DEPTH, N_EXPERTS, D_MODEL, D_FF_EXPERT), D_MODEL ** -0.5)
    w_down = nrm((DEPTH, N_EXPERTS, D_FF_EXPERT, D_MODEL), D_FF_EXPERT ** -0.5)
    return {'x_prompt': x_prompt, 'x_sample': x_sample, 'cache_k': cache_k, 'cache_v': cache_v,
            'cache_logf': cache_logf, 'state_ssm': state_ssm, 'state_conv': state_conv,
            'page_table': page_table, 'c_prompt': c_prompt, 'c_sample': c_sample,
            'w_mod': w_mod, 'b_mod': b_mod, 'g_norm1': g_norm1, 'g_norm2': g_norm2, 'w_in': w_in,
            'b_f': b_f, 'g_q': g_q, 'g_k': g_k, 'conv_w': conv_w, 'conv_b': conv_b,
            'dt_bias': dt_bias, 'a_log': a_log, 'd_skip': d_skip, 'g_ssm': g_ssm,
            'w_pa': w_pa, 'w_pb': w_pb, 'w_o': w_o, 'w_router': w_router, 'b_router': b_router,
            'w_gate': w_gate, 'w_up': w_up, 'w_down': w_down}

def reference(x_prompt, x_sample, cache_k, cache_v, cache_logf, state_ssm, state_conv, page_table,
              c_prompt, c_sample, w_mod, b_mod, g_norm1, g_norm2, w_in, b_f, g_q, g_k, conv_w, conv_b,
              dt_bias, a_log, d_skip, g_ssm, w_pa, w_pb, w_o, w_router, b_router, w_gate, w_up, w_down):
    bp = x_prompt.shape[0]
    db = x_sample.shape[0]
    yp, ys = x_prompt, x_sample
    kp, vp, lp, sp, cp = [], [], [], [], []
    kq, vq, lq, sq, cq = [], [], [], [], []
    for l in range(DEPTH):
        w = dict(w_mod=w_mod[l], b_mod=b_mod[l], g_norm1=g_norm1[l], g_norm2=g_norm2[l], w_in=w_in[l],
                 b_f=b_f[l], g_q=g_q[l], g_k=g_k[l], conv_w=conv_w[l], conv_b=conv_b[l],
                 dt_bias=dt_bias[l], a_log=a_log[l], d_skip=d_skip[l], g_ssm=g_ssm[l],
                 w_pa=w_pa[l], w_pb=w_pb[l], w_o=w_o[l], w_gate=w_gate[l], w_up=w_up[l], w_down=w_down[l])
        ssm_zero = jnp.zeros((bp, SSM_HEADS, SSM_HEAD_DIM, D_STATE), x_prompt.dtype)
        conv_zero = jnp.zeros((bp, CONV_WIDTH - 1, CONV_DIM), x_prompt.dtype)
        yp, st = layer(yp, c_prompt, None, ssm_zero, conv_zero, w, w_router, b_router)
        kp.append(st[0]); vp.append(st[1]); lp.append(st[2]); sp.append(st[3]); cp.append(st[4])
        past = (cache_k[l][page_table].reshape(db, -1, N_KV_HEADS, HEAD_DIM),
                cache_v[l][page_table].reshape(db, -1, N_KV_HEADS, HEAD_DIM),
                cache_logf[l][page_table].reshape(db, -1, N_HEADS))
        ys, st = layer(ys, c_sample, past, state_ssm[l], state_conv[l], w, w_router, b_router)
        kq.append(st[0]); vq.append(st[1]); lq.append(st[2]); sq.append(st[3]); cq.append(st[4])
    return (yp, ys,
            jnp.stack(kp), jnp.stack(vp), jnp.stack(lp), jnp.stack(sp), jnp.stack(cp),
            jnp.stack(kq), jnp.stack(vq), jnp.stack(lq), jnp.stack(sq), jnp.stack(cq))


_drawn_inputs = setup_inputs


def setup_inputs(seed=0):
    import zlib

    import numpy as np

    out = dict(_drawn_inputs(seed))
    spreads = {}
    factors = {'g_q': 6.185, 'b_router': 4.135}
    for name, (base, spread) in spreads.items():
        noise = np.random.default_rng([zlib.crc32(name.encode()), seed]).standard_normal(out[name].shape)
        drawn = base * np.exp(spread * noise) if base else spread * noise
        out[name] = jnp.asarray(drawn.astype(out[name].dtype))
    for name, factor in factors.items():
        out[name] = (out[name] * factor).astype(out[name].dtype)
    return out
```

```python
import concourse.bass as bass
from concourse import mybir
from contextlib import ExitStack

F32 = mybir.dt.float32
BF16 = mybir.dt.bfloat16
I32 = mybir.dt.int32
ALU = mybir.AluOpType
ACT = mybir.ActivationFunctionType
AX = mybir.AxisListType

D = 1024
NP, NS = 256, 8
T = NP + NS
NC = NS + 1
KD = D // 128
NH, NKV, HD = 16, 8, 64
PAGE, NPG = 128, 2
KVW = NKV * HD
DI, SH, SG, NST = 2048, 32, 4, 128
CD = DI + 2 * SG * NST
NCB = CD // 128
NXB = DI // 128
HB = SH + NH
NE, EPG, NG, FF = 16, 4, 4, 512
EPS = 1e-6
COL_K, COL_V, COL_F = D, D + KVW, D + 2 * KVW
COL_Z = COL_F + NH
COL_X = COL_Z + DI
COL_DT = COL_X + CD
COL_G = COL_DT + SH
IN_DIM = COL_G + 2 * D
TOK = [(0, 128), (128, 128), (256, NS)]
SW = 256
SLOT = KD * SW
NSLOT = 6
NBANK = 7
BLK = 64
XW = 3 + NP + 4 * NS
XO = XW - 3


def build(nc, t):
    ctx = ExitStack()
    with ctx:
        def sb(name, shape, dt=F32):
            return ctx.enter_context(nc.sbuf_tensor(name, shape, dt))

        def sem(name):
            return ctx.enter_context(nc.semaphore(name))

        ring = sb("weight_ring", [128, NSLOT * SLOT])
        xT = sb("x_residual", [128, KD, T])
        hT = sb("h_normed", [128, KD, T])
        modT = sb("modulation", [128, 6 * KD, NC])
        gsc = sb("norm_gain", [128, KD, NC])
        ident = sb("identity", [128, 128])
        nident = sb("neg_identity", [HB, HB])
        ntri = sb("neg_triangle", [128, 3 * 128 + 1])
        cmask = sb("causal_mask", [128, 384])
        triu = sb("upper_triangle", [128, 128])
        onesf = sb("ones", [128, 128])
        blk = sb("head_blocks", [128, 128])
        striu = sb("strict_upper", [128, 128], BF16)
        onesb = sb("ones_bf", [128, 128], BF16)
        bm8 = sb("sample_rows", [NS, 128])
        bm2 = sb("sample_cols", [128, NS])
        iota = sb("slot_numbers", [128, BLK])
        w4 = sb("first_weights", [128, 4])
        thr = sb("round_limits", [1, 4])
        vm = sb("valid_rows", [128, 3])
        epsc = sb("eps_col", [128, 1])
        vec = sb("vectors", [128, 200])
        gqk = sb("qk_gain", [128, 2])
        hcol = sb("head_cols", [HB, 4])
        brow = sb("router_bias", [NE, 1])
        cT = sb("cond_T", [128, KD, 32])
        wfd = sb("w_forget_dt", [128, KD, HB])
        wr = sb("w_router_sb", [128, KD, NE])
        pgs = sb("pages", [1, NS * NPG], I32)
        rs = sb("rstd", [128, 4, T])
        attT = sb("att_T", [128, KD, T])
        u = sb("conv_out", [128, NCB, T])
        xa = sb("conv_in", [128, 2, XW])
        cacc = sb("conv_sum", [128, 2, XO])
        tails = sb("conv_tails", [128, NCB, 27])
        yq = sb("y_T", [128, 4228])
        yT = yq[:, 0:NXB * T].rearrange("p (c t) -> p c t", c=NXB)
        fd = sb("dt_logf", [HB, T])
        acsT = sb("cums", [HB, NP])
        ex = sb("expand_in", [SH, 2 * NS + 1])
        tokc = sb("token_cols", [128, 7 * 32])
        lft = sb("logf_tok", [128, 3, NH])
        exo = sb("expanded", [128, NXB, 2 * NS + 1])
        sm2 = sb("small", [128, 64])
        fdw = sb("head_work", [HB, 3, T])
        mrow = sb("mod_rows", [128, SW])
        stT = sb("conv_states", [128, NCB, 24])
        zsS = sb("z_samples", [128, NXB, NS])
        ARENA = 14352
        ar = sb("arena", [128, ARENA])
        at = [0]

        def part(n):
            o = at[0]
            at[0] += n
            assert at[0] <= ARENA, at[0]
            return ar[:, o:o + n]

        qkT = part(12 * T).rearrange("p (c t) -> p c t", c=12)
        vtok = part(3 * KVW).rearrange("p (a f) -> p a f", a=3)
        kvf = part(4 * NPG * KVW)
        kvr = kvf.rearrange("p (s g f) -> p s g f", s=4, g=NPG)
        ktb = part(2 * 4 * 257).rearrange("p (s m k) -> p s m k", s=2, m=4)
        pbT = part(4 * 384)
        pb = pbT[:, 0:768].rearrange("p (s k) -> p s k", s=2)
        pT = pbT[:, 768:1536].rearrange("p (s k) -> p s k", s=2)
        vT = pbT[:, 0:4 * T].rearrange("p (c t) -> p c t", c=4)
        ps_s = part(257)
        psT = part(NPG * 144).rearrange("p (g k) -> p g k", g=NPG)
        pn = part(144)
        otok = part(KVW)
        ktok = otok
        lfc = part(NPG * 128).rearrange("p (g k) -> p g k", g=NPG)
        lfn = part(128)
        pnb = part(NS)
        qbd = yq
        xin = kvf[:, 0:3 * D].rearrange("p (a d) -> p a d", a=3)
        vrow = otok[:, 0:256].rearrange("p (a k) -> p a k", a=2)
        crow = ar[:, 0:D]
        csin = ar[:, D:D + CD]
        at[0] = 0
        xd = part(2 * DI).rearrange("p (a f) -> p a f", a=2)
        xef = part(2 * DI)
        xe = xef.rearrange("p (a f) -> p a f", a=2)
        late0 = at[0]
        btok = part(2 * SG * NST).rearrange("p (a f) -> p a f", a=2)
        s1T = part(DI)
        cbm = part(SG * 128).rearrange("p (g k) -> p g k", g=SG)
        wdf = part(2 * 512)
        wd = wdf.rearrange("p (s k) -> p s k", s=2)
        ce = part(2 * 512).rearrange("p (s k) -> p s k", s=2)
        zs = part(2 * T).rearrange("p (s k) -> p s k", s=2)
        ctok = xef[:, 0:512]
        at[0] = late0
        sst = part(2 * 8 * NST).rearrange("p (s k) -> p s k", s=2)
        bc = part(2 * SG * NST)
        prod = part(8 * NST)
        gT = ar[:, 0:16 * T].rearrange("p (c t) -> p c t", c=16)
        mslot = [ring[:, i * 4096:(i + 1) * 4096] for i in range(3)] + \
                [ar[:, 4224 + i * 4096:4224 + (i + 1) * 4096] for i in range(2)] + [yq[:, 0:4096]]

        def blocks(a, b, n):
            return u[:, a:b, :].rearrange("p c t -> p (c t)")[:, 0:n]

        h2tok = blocks(8, 20, 3 * D).rearrange("p (a d) -> p a d", a=3)
        xg = blocks(0, 4, D).rearrange("p (k s) -> p k s", k=KD)
        outs = blocks(4, 8, D)
        aT = blocks(20, 22, 512).rearrange("p (k s) -> p k s", k=4)
        gact = blocks(22, 24, 512)
        sel = ar[:, 0:768].rearrange("p (w a s) -> p w a s", w=2, a=3)
        selT = ar[:, 768:768 + T]
        hact = ar[:, 1100:1100 + 512]
        lgT = ar[:, 2100:2100 + T]

        def rows3(o, n=NE):
            return ar[:, o:o + 3 * n].rearrange("p (a e) -> p a e", a=3)

        lg, cmb, asg, rank, prg = (rows3(2400 + 48 * i) for i in range(5))
        rt = [rows3(2700 + 12 * i, 4) for i in range(12)]
        rw = [ar[:, 2900 + 4 * i:2903 + 4 * i] for i in range(10)]
        cnt = ar[:, 2950:2950 + NE]
        asb = sb("assigned_bf", [128, 3, NE], BF16)
        xrd = sb("extra_rounds", [1, 1], I32)
        Y = attT
        yout = yq[:, 0:3 * D].rearrange("p (a d) -> p a d", a=3)

        banks = [ctx.enter_context(nc.psum_tensor(f"bank{i}", [128, 512], F32)) for i in range(8)]
        sbank = banks[7]

        jobs = [("cT",), ("vecs",), ("mod", 0), ("modt", 0)]
        jobs += [("xt", a, f) for a in range(3) for f in range(2)]
        jobs += [("ssq", 0), ("mod", 1), ("modt", 1), ("cst", 0), ("cst", 1), ("fd",)]
        jobs += [("k", i) for i in range(4)] + [("ft",)] + [("kn", i) for i in range(4)]
        jobs += [("q", i) for i in range(4)] + [("qn", i) for i in range(4)]
        jobs += [("q", i) for i in range(4, 8)] + [("qn", i) for i in range(4, 8)]
        jobs += [("v", i) for i in range(4)]
        jobs += [("kt", a) for a in range(3)] + [("vt", a) for a in range(3)]
        for c in range(8):
            jobs += [("s", c, 0), ("s", c, 1), ("xbc", 3 * c), ("sk", c, 0), ("sk", c, 1),
                     ("xbc", 3 * c + 1), ("ss", c), ("xbc", 3 * c + 2),
                     ("pt", c, 0), ("pt", c, 1), ("o2", c)]
        jobs += [("mod", 2), ("modt", 2), ("sp",), ("mod", 3), ("modt", 3)]
        jobs += [("so", 0), ("sx", 0), ("so", 1), ("sx", 1)]
        jobs += [("ct", i) for i in range(6)] + [("bs", 0), ("bs", 1), ("exp",)]
        jobs += [("bt", a) for a in range(2)]
        for a in range(2):
            jobs += [("xs", a, g) for g in range(4)]
            if a == 1:
                jobs += [("s1", g) for g in range(4)]
            jobs += [("cb", a)]
            for b in range(8):
                jobs += [("ab", a, b)]
                if b >= 1:
                    jobs += [("y", a, b - 1)]
                if a == 0 and b in (2, 5):
                    jobs += [("mod", 4 + b // 5), ("modt", 4 + b // 5)]
            jobs += [("y", a, 7)]
        jobs += [("fs", i) for i in range(4)]
        jobs += [("z", i) for i in range(NXB)]
        for i in range(16):
            jobs += [("g", i), ("ssm", i)]
        jobs += [("pa", i) for i in range(8)] + [("yn", g) for g in range(SG)]
        jobs += [("pb", i) for i in range(8)] + [("o", i) for i in range(8)]
        jobs += [("ssq", 1), ("lr",), ("lt",)] + [("ht", a, f) for a in range(3) for f in range(2)] + [("rk",)]
        late = [("yt", a, f) for a in range(3) for f in range(2)]
        NOBANK = {"ss", "ssm"}

        bank_of, at_bank = {}, [0] * NBANK
        for n, j in enumerate([j for j in jobs + late if j[0] not in NOBANK]):
            b = n % NBANK
            at_bank[b] += 1
            bank_of[j] = (b, at_bank[b])
        at_moe = [0] * NBANK
        for j in jobs:
            if j in bank_of:
                at_moe[bank_of[j][0]] += 1
        bank_filled = [sem(f"bank_filled{i}") for i in range(NBANK)]
        bank_read = [sem(f"bank_read{i}") for i in range(NBANK)]

        def slots_of(j):
            k = j[0]
            if k == "mod":
                return [("mod", 4 * j[1] + i) for i in range(4)]
            if k in ("q", "k", "v", "xbc", "z", "g"):
                base = {"q": 0, "k": COL_K, "v": COL_V, "xbc": COL_X, "z": COL_Z, "g": COL_G}[k]
                return [("in", base + SW * (j[1] // 2))]
            if k in ("pa", "o"):
                return [(k, j[1] // 2)]
            if k == "pb":
                return [(k, j[1] // 2, 0), (k, j[1] // 2, 1)]
            return []

        loads, last_user = [], {}
        for j in jobs:
            for s in slots_of(j):
                if s not in last_user:
                    loads.append(s)
                last_user[s] = j
        slot_at, slot_count, arrived_at = {}, [0] * NSLOT, {}
        for n, s in enumerate(loads):
            r = n % NSLOT
            slot_count[r] += 16 * (4 if s[0] == "pa" else 4 if s[0] == "in" and s[1] < D else 1)
            slot_at[s], arrived_at[s] = r, slot_count[r]
        slot_full = [sem(f"slot_full{i}") for i in range(NSLOT)]

        def slot(s):
            r = slot_at[s]
            return ring[:, r * SLOT:(r + 1) * SLOT].rearrange("p (k n) -> p k n", k=KD)

        small_in = sem("conditions_and_vectors_landed")
        x_in = sem("x_landed")
        st_in = sem("conv_states_landed")
        late_in = sem("small_weights_landed")
        pt_in = sem("page_table_landed")
        lf_in = sem("cached_logf_landed")
        consts = sem("constants_built")
        cond_ready = sem("condition_silu_done")
        sq_ready = sem("x_squared")
        h_ready = sem("h_ready")
        fd_exp = sem("exp_of_head_logits")
        fd_sp = sem("dt_logf_and_sums_ready")
        fd_e = sem("head_decays_ready")
        lfn_ready = sem("new_logf_spread")
        qk_sq = sem("qk_squared")
        qk_ready = sem("qk_normed")
        qbd_zero = sem("sample_queries_zeroed")
        qbd_ready = sem("sample_queries_placed")
        s_max = sem("scores_and_max_ready")
        s_exp = sem("scores_exponentiated")
        p_ready = sem("probs_ready")
        kcol_ready = sem("new_key_placed")
        ss_done = sem("sample_scores_summed")
        ss_max = sem("sample_max_ready")
        ss_exp = sem("sample_scores_exponentiated")
        sp_ready = sem("sample_probs_ready")
        conv_ready = sem("conv_summed")
        u_ready = sem("conv_silu_done")
        bs_out = sem("sample_bc_rows_stored")
        xds_ready = sem("sample_x_dt_ready")
        xe_ready = sem("decayed_xd_ready")
        seg_exp = sem("segment_decays_ready")
        et_ready = sem("exp_of_sums_ready")
        w_ready = sem("weighted_cb_ready")
        ce_ready = sem("decayed_c_ready")
        zg_done = sem("z_gate_applied")
        y_sq = sem("y_squared")
        y_ready = sem("y_normed")
        m_ready = sem("branches_merged")
        bc_full = sem("sample_bc_rows_landed")
        st_dec = sem("state_decayed")
        st_new = sem("state_updated")
        st_prod = sem("state_times_c_ready")
        st_red = sem("state_times_c_summed")
        o_small = sem("small_outputs_stored")
        o_k = sem("k_stored")
        o_tail = sem("conv_states_stored")
        o_y = sem("y_stored")
        asg_ready = sem("assignment_ready")
        rk_exp = sem("router_exp_ready")
        rk_ready = sem("ranks_ready")
        rk_shift = sem("ranks_shifted")
        sel_ready = sem("selection_ready")
        gather_done = sem("gather_done")
        selT_done = sem("selection_transposed")
        selT_ready = sem("selection_T_copied")
        xg_ready = sem("gathered_copied")
        gate_done = sem("gate_product_done")
        up_done = sem("up_product_done")
        silu_ready = sem("gate_silu_ready")
        act_ready = sem("expert_act_ready")
        actT_done = sem("expert_act_transposed")
        actT_ready = sem("expert_act_T_copied")
        down_done = sem("down_product_done")
        out_ready = sem("expert_out_copied")
        comb_filled = sem("combined_bank_filled")
        comb_read = sem("combined_bank_read")
        yfin = sem("y_final_ready")
        dve_step = sem("dve_step")
        act_step = sem("act_step")
        pool_step = sem("pool_step")
        kv_full = [sem(f"cache_page_landed{i}") for i in range(4)]
        st_full = [sem(f"state_landed{i}") for i in range(2)]
        st_out = [sem(f"state_stored{i}") for i in range(2)]
        o_fs = [sem(f"ssm_prompt_stored{i}") for i in range(2)]
        moe_full = [sem(f"expert_matrix_landed{i}") for i in range(6)]

        def stepper(eng, own):
            n = {}

            def link(ins, s=own):
                n[s.name] = n.get(s.name, 0) + 1
                ins.then_inc(s, 1)
                eng.wait_ge(s, n[s.name])
            return link

        def filled(eng, j):
            b, n = bank_of[j]
            eng.wait_ge(bank_filled[b], n)
            return banks[b]

        def release(eng, ins, j):
            b, n = bank_of[j]
            ins.then_inc(bank_read[b], 1)
            eng.wait_ge(bank_read[b], n)

        def read_out(eng, j):
            b, n = bank_of[j]
            eng.wait_ge(bank_read[b], n)

        wmod = t["w_mod"].rearrange("o (k p) n -> p (o k) n", p=128)
        win = t["w_in"].rearrange("o (k p) n -> p (o k) n", p=128)
        wpa = t["w_pa"].rearrange("o (m h s d) n -> (o h) s d m n", h=2, s=2, d=HD)
        wpb = t["w_pb"].rearrange("o (k p) n -> p (o k) n", p=128)
        wo = t["w_o"].rearrange("o (k p) n -> p (o k) n", p=128)
        wg = t["w_gate"].rearrange("o e (k p) n -> (o e) p k n", p=128)
        wu = t["w_up"].rearrange("o e (k p) n -> (o e) p k n", p=128)
        wdn = t["w_down"].rearrange("o e (k p) n -> (o e) p k n", p=128)
        ck = t["cache_k"].rearrange("o g k h d -> (o g) k (h d)")
        cv = t["cache_v"].rearrange("o g k h d -> (o g) k (h d)")
        clf = t["cache_logf"].rearrange("o g k h -> (o g) k h")
        st_d = t["state_ssm"].rearrange("o b (c h) p n -> (o b) (h p) c n", h=2)
        so_d = t["ssm_sample"].rearrange("o b (c h) p n -> (o b) (h p) c n", h=2)
        fs_d = t["ssm_prompt"].rearrange("o b (c h) p n -> (o b) (h p) c n", h=2)
        bc_d = t["bc_scratch"]

        block = ctx.enter_context(nc.Block())

        @block.sync
        def _(sp):
            for n, s in enumerate(loads):
                if n >= NSLOT:
                    b, use = bank_of[last_user[loads[n - NSLOT]]]
                    sp.wait_ge(bank_filled[b], use)
                r, dst, c0 = slot_at[s], slot(s), SW * s[1]
                if s[0] == "mod":
                    sp.dma_start(dst, wmod[:, :, c0:c0 + SW]).then_inc(slot_full[r], 16)
                elif s[0] == "in" and s[1] < D:
                    for q in range(2):
                        for h in range(2):
                            o, c = HD * (2 * q + h), s[1] + HD * (2 * h + q)
                            sp.dma_start(dst[:, :, o:o + HD], win[:, :, c:c + HD]).then_inc(slot_full[r], 16)
                elif s[0] == "in":
                    sp.dma_start(dst, win[:, :, s[1]:s[1] + SW]).then_inc(slot_full[r], 16)
                elif s[0] == "o":
                    sp.dma_start(dst, wo[:, :, c0:c0 + SW]).then_inc(slot_full[r], 16)
                elif s[0] == "pb":
                    sp.dma_start(dst, wpb[:, KD * s[2]:KD * s[2] + KD, c0:c0 + SW]).then_inc(slot_full[r], 16)
                else:
                    dv = dst.rearrange("p (m s) n -> p s m n", s=2)
                    for h in range(2):
                        for q in range(2):
                            sp.dma_start(dv[64 * h:64 * h + 64, q], wpa[h, q, :, :, c0:c0 + SW])\
                              .then_inc(slot_full[r], 16)

            def experts(it, j):
                for i, w in enumerate((wg, wu, wdn)):
                    sp.wait_ge((gate_done, up_done, down_done)[i], it + 1)
                    for e in range(2):
                        s = 2 * i + e
                        sp.dma_start(mslot[s].rearrange("p (k n) -> p k n", k=KD if i < 2 else FF // 128),
                                     w[2 * j + e]).then_inc(moe_full[s], 16)

            b, use = bank_of[("o", 7)]
            sp.wait_ge(bank_filled[b], use)
            for i in range(2):
                sp.wait_ge(st_out[i], 16 * NS)
                sp.wait_ge(o_fs[i], 32)
            with sp.Fori(0, NE // 2) as j:
                experts(j, j)
            sp.wait_ge(rk_ready, 1)
            extra = sp.value_load(xrd[0:1, 0:1], min_val=0, max_val=4)
            with sp.If(extra > 0):
                with sp.Fori(0, extra) as r:
                    with sp.Fori(0, NE // 2) as j:
                        experts(r * 8 + (j + 8), j)
            for a, (t0, n) in enumerate(TOK):
                read_out(sp, ("yt", a, 1))
                if a < 2:
                    dst = t["y_prompt"].rearrange("o q d -> (o q) d")[t0:t0 + n, :]
                else:
                    dst = t["y_sample"].rearrange("b o d -> (b o) d")
                sp.dma_start(dst, yout[0:n, a, :]).then_inc(o_y, 16)
            sp.wait_ge(o_y, 48)
            sp.wait_ge(o_small, 16 * 5)
            sp.wait_ge(o_k, 48)
            sp.wait_ge(o_tail, 16 * 12)

        @block.gpsimd
        def _(pool):
            link = stepper(pool, pool_step)
            g = nc.gpsimd
            link(g.memset(ident[:], 0.0))
            link(g.affine_select(out=ident[:], in_=ident[:], compare_op=ALU.not_equal, fill=1.0, base=0,
                                 pattern=[[-1, 128]], channel_multiplier=1), consts)
            link(g.memset(cT[:], 0.0), consts)
            link(g.memset(onesf[:], 1.0))
            link(g.memset(epsc[:], EPS))
            link(g.memset(blk[:], 0.0))
            link(g.memset(blk[0:64, 0:64], 1.0))
            link(g.memset(blk[64:128, 64:128], 1.0), consts)
            link(g.memset(qbd[:], 0.0), qbd_zero)
            link(g.memset(ntri[:], -1.0))
            link(g.affine_select(out=ntri[:], in_=ntri[:], compare_op=ALU.is_ge, fill=0.0, base=-128,
                                 pattern=[[1, 385]], channel_multiplier=-1))
            link(g.memset(cmask[:], 0.0))
            for o in (0, 256):
                link(g.affine_select(out=cmask[:, o:o + 128], in_=cmask[:, o:o + 128], compare_op=ALU.is_ge,
                                     fill=-1e30, base=0, pattern=[[-1, 128]], channel_multiplier=1))
            link(g.affine_select(out=triu[:], in_=onesf[:], compare_op=ALU.is_ge, fill=0.0, base=0,
                                 pattern=[[1, 128]], channel_multiplier=-1))
            link(g.affine_select(out=bm8[:].rearrange("p (b h) -> p b h", h=NH),
                                 in_=onesf[0:NS, :].rearrange("p (b h) -> p b h", h=NH),
                                 compare_op=ALU.is_equal, fill=0.0, base=0,
                                 pattern=[[1, NS], [0, NH]], channel_multiplier=-1))
            link(g.affine_select(out=bm2[:], in_=onesf[:, 0:NS], compare_op=ALU.is_ge, fill=0.0, base=0,
                                 pattern=[[-NH, NS]], channel_multiplier=1))
            link(g.affine_select(out=bm2[:], in_=bm2[:], compare_op=ALU.is_ge, fill=0.0, base=NH - 1,
                                 pattern=[[NH, NS]], channel_multiplier=-1))
            link(g.memset(onesb[:], 1.0))
            link(g.affine_select(out=striu[:], in_=onesb[:], compare_op=ALU.is_ge, fill=0.0, base=-1,
                                 pattern=[[1, 128]], channel_multiplier=-1))
            link(g.iota(iota[:], pattern=[[1, BLK]], base=0, channel_multiplier=0,
                        allow_small_or_imprecise_dtypes=True))
            link(g.iota(w4[:], pattern=[[-1, 4]], base=4, channel_multiplier=0,
                        allow_small_or_imprecise_dtypes=True))
            link(g.iota(thr[:], pattern=[[BLK, 4]], base=BLK, channel_multiplier=0,
                        allow_small_or_imprecise_dtypes=True))
            link(g.memset(vm[:], 1.0))
            link(g.affine_select(out=vm[:, 2:3], in_=vm[:, 2:3], compare_op=ALU.is_ge, fill=0.0, base=NS - 1,
                                 pattern=[[0, 1]], channel_multiplier=-1))
            link(g.memset(xa[:, :, 0:3], 0.0))
            link(g.memset(psT[:], 0.0))
            link(g.memset(pn[:], 0.0), consts)

            pool.wait_ge(pt_in, 16)

            def page(i):
                return pool.value_load(pgs[0:1, bass.ds(i, 1)], min_val=0, max_val=ck.shape[0] - 1)

            with pool.Fori(0, NS) as b:
                for q in range(NPG):
                    pool.dma_start(lfc[:, q, bass.ds(b * NH, NH)], clf[page(b * NPG + q)]).then_inc(lf_in, 16)
            bk, use = bank_of[("xt", 2, 1)]
            pool.wait_ge(bank_filled[bk], use)
            for kind, cache in enumerate((ck, cv)):
                for b in range(NS):
                    if kind == 1 or b >= 4:
                        bk, use = bank_of[("sk", b - 4, 1) if kind == 0 else ("sk", b + 4, 1) if b < 4 else ("so", 0)]
                        pool.wait_ge(bank_filled[bk], use)
                    with pool.Fori(0, NPG) as q:
                        pool.dma_start(kvr[:, b % 4, bass.ds(q, 1), :].rearrange("p o f -> p (o f)"),
                                       cache[page(q + b * NPG)]).then_inc(kv_full[b % 4], 16)

            for a in range(2):
                read_out(pool, ("xs", a, 3))
                if a == 0:
                    pool.wait_ge(o_tail, 16 * 12)
                e = tokc[:, (4 + a) * 32:(5 + a) * 32]
                link(g.tensor_tensor(xe[:, a, :].rearrange("p (h d) -> p h d", d=HD),
                                     xd[:, a, :].rearrange("p (h d) -> p h d", d=HD),
                                     e.unsqueeze(2).to_broadcast([128, SH, HD]), ALU.mult), xe_ready)
            bk, use = bank_of[("s1", 3)]
            pool.wait_ge(bank_filled[bk], use)
            x3 = xe[:, 0, :].rearrange("p (h d) -> p h d", d=HD)
            link(g.tensor_tensor(x3, x3, tokc[:, 192:224].unsqueeze(2).to_broadcast([128, SH, HD]), ALU.mult), xe_ready)
            for b in range(8):
                pool.wait_ge(et_ready, b + 1)
                c3 = ce[:, b % 2, :].rearrange("p (h k) -> p h k", h=4)
                cv3 = u[:, 20 + b // 2, 128:256].unsqueeze(1).to_broadcast([128, 4, 128])
                link(g.tensor_tensor(c3, c3, cv3, ALU.mult), ce_ready)

            bk, use = bank_of[("fs", 3)]
            pool.wait_ge(bank_filled[bk], use)
            for i in range(2):
                pool.wait_ge(o_fs[i], 32)
            pool.wait_ge(bs_out, 16)
            pool.wait_ge(xds_ready, 1)

            def load_state(i):
                if i >= 2:
                    pool.wait_ge(st_out[i % 2], 16 * (i // 2))
                pool.dma_start(sst[:, i % 2, :].rearrange("p (c n) -> p c n", c=8),
                               st_d[i // 2, :, 8 * (i % 2):8 * (i % 2) + 8, :]).then_inc(st_full[i % 2], 16)

            def load_bc(b):
                pool.dma_start(bc, bc_d[b:b + 1, :].to_broadcast([128, 2 * SG * NST])).then_inc(bc_full, 16)

            load_state(0)
            load_bc(0)
            load_state(1)
            for i in range(2 * NS):
                b, hf = i // 2, i % 2
                s3 = sst[:, i % 2, :].rearrange("p (c n) -> p c n", c=8)
                dec = exo[:, 8 * hf:8 * hf + 8, NS + b:NS + b + 1]
                pool.wait_ge(st_full[i % 2], 16 * (i // 2 + 1))
                link(g.tensor_tensor(s3, s3, dec.to_broadcast([128, 8, NST]), ALU.mult), st_dec)
                pool.wait_ge(st_new, i + 1)
                pool.dma_start(so_d[b, :, 8 * hf:8 * hf + 8, :], s3).then_inc(st_out[i % 2], 16)
                if i:
                    pool.wait_ge(st_red, i)
                s4 = sst[:, i % 2, :].rearrange("p (g c n) -> p g c n", g=2, c=4)
                p4 = prod.rearrange("p (g c n) -> p g c n", g=2, c=4)
                for q in range(2):
                    cr = bc[:, (SG + 2 * hf + q) * NST:(SG + 2 * hf + q + 1) * NST]
                    link(g.tensor_tensor(p4[:, q], s4[:, q], cr.unsqueeze(1).to_broadcast([128, 4, NST]), ALU.mult),
                         st_prod)
                if i + 2 < 2 * NS:
                    load_state(i + 2)
                if hf and b + 1 < NS:
                    load_bc(b + 1)

        @block.scalar
        def _(act):
            link = stepper(act, act_step)
            fn = nc.scalar.activation
            act.sem_inc(out_ready, 1)
            act.dma_start(crow[0:NS, :], t["c_sample"]).then_inc(small_in, 16)
            act.dma_start(crow[NS:NC, :], t["c_prompt"]).then_inc(small_in, 16)
            o = 0
            for name, n in (("b_mod", 48), ("g_norm1", 8), ("g_norm2", 8), ("g_ssm", 16), ("conv_b", 24)):
                act.dma_start(vrow[o:o + n, 0, :], t[name].rearrange("o (k p) -> (o k) p", p=128)).then_inc(small_in, 16)
                o += n
            act.dma_start(vrow[0:96, 1, :], t["conv_w"].rearrange("o w (k p) -> (o w k) p", p=128)).then_inc(small_in, 16)
            xp = t["x_prompt"].rearrange("o q d -> (o q) d")
            act.dma_start(xin[:, 0, :], xp[0:128, :]).then_inc(x_in, 16)
            act.dma_start(xin[:, 1, :], xp[128:256, :]).then_inc(x_in, 16)
            act.dma_start(xin[0:NS, 2, :], t["x_sample"].rearrange("b o d -> (b o) d")).then_inc(x_in, 16)
            act.dma_start(csin[0:24, :], t["state_conv"].rearrange("o b w c -> (o b w) c")).then_inc(st_in, 16)
            act.dma_start(pgs[:], t["page_table"].rearrange("(o b) g -> o (b g)", o=1)).then_inc(pt_in, 16)
            act.dma_start(wfd[:, :, 0:SH], win[:, :, COL_DT:COL_DT + SH]).then_inc(late_in, 16)
            act.dma_start(wfd[:, :, SH:HB], win[:, :, COL_F:COL_F + NH]).then_inc(late_in, 16)
            act.dma_start(wr[:], t["w_router"].rearrange("(k p) e -> p k e", p=128)).then_inc(late_in, 16)
            for h in range(2):
                act.dma_start(gqk[64 * h:64 * h + 64, 0:1], t["g_q"].rearrange("o d -> d o")).then_inc(late_in, 16)
                act.dma_start(gqk[64 * h:64 * h + 64, 1:2], t["g_k"].rearrange("o d -> d o")).then_inc(late_in, 16)
            act.dma_start(hcol[0:SH, 0:1], t["dt_bias"].rearrange("o d -> d o")).then_inc(late_in, 16)
            act.dma_start(hcol[SH:HB, 0:1], t["b_f"].rearrange("o d -> d o")).then_inc(late_in, 16)
            act.dma_start(hcol[0:SH, 1:2], t["a_log"].rearrange("o d -> d o")).then_inc(late_in, 16)
            act.dma_start(hcol[0:SH, 2:3], t["d_skip"].rearrange("o d -> d o")).then_inc(late_in, 16)
            act.dma_start(brow[:], t["b_router"].rearrange("(d o) -> d o", o=1)).then_inc(late_in, 16)
            act.wait_ge(small_in, 16 * 8)
            link(fn(crow[0:NC, :], crow[0:NC, :], ACT.Silu), cond_ready)

            def conv_silu(i):
                act.wait_ge(conv_ready, i + 1)
                link(fn(u[:, i, 0:NP], cacc[:, i % 2, 0:NP], ACT.Silu))
                link(fn(u[:, i, NP:T], cacc[:, i % 2, NP + 3:XO:4], ACT.Silu), u_ready)

            for j in jobs:
                k = j[0]
                if k == "sp":
                    act.wait_ge(ss_max, 1)
                    link(fn(ps_s, sbank[:, 0:257], ACT.Exp, bias=sm2[:, 8:9], accum_out=sm2[:, 9:10]), ss_exp)
                if k == "lt":
                    act.wait_ge(asg_ready, 1)
                    link(fn(lg, lg, ACT.Exp), rk_exp)
                ps = filled(act, j) if k in ("mod", "ssq", "q", "k", "qn", "kn", "v", "kt", "vt", "pt", "o2", "xbc",
                                             "sk", "sp", "so", "ct", "bs", "bt", "s1", "fs", "z", "g", "yn",
                                             "ht") else None
                if k == "mod":
                    if j[1] == 2:
                        conv_silu(NCB - 1)
                    release(act, fn(mrow[:], ps[:, 0:SW], ACT.Copy), j)
                elif k == "ssq":
                    act.wait_ge(consts, 3)
                    release(act, fn(rs[:, 0, :], ps[:, 0:T], ACT.Sqrt, bias=epsc[:], scale=1.0 / D), j)
                elif k == "fd":
                    read_out(act, j)
                    link(fn(fdw[:, 0, :], fd[:], ACT.Abs))
                    link(fn(hcol[0:SH, 1:2], hcol[0:SH, 1:2], ACT.Exp))
                    link(fn(fdw[:, 0, :], fdw[:, 0, :], ACT.Exp, scale=-1.0), fd_exp)
                    act.wait_ge(fd_sp, 1)
                    for c in range(2):
                        cols = slice(128 * c, 128 * c + 128)
                        link(fn(fdw[0:SH, 1, cols], acsT[0:SH, cols], ACT.Exp,
                                bias=acsT[0:SH, 128 * c + 127:128 * c + 128], scale=-1.0))
                    link(fn(fdw[0:SH, 2, 0:128], fdw[0:SH, 2, 0:128], ACT.Exp))
                    link(fn(ex[:, NS:2 * NS], ex[:, NS:2 * NS], ACT.Exp), fd_e)
                elif k == "ft":
                    read_out(act, j)
                    act.dma_start(t["logf_prompt"].rearrange("o b (a p) h -> p (o b a) h", p=128),
                                  lft[:, 0:2, :]).then_inc(o_small, 16)
                    act.dma_start(t["logf_sample"].rearrange("o b q h -> (o b q) h"), lft[0:NS, 2, :])\
                       .then_inc(o_small, 16)
                elif k in ("q", "k"):
                    release(act, fn(qkT[:, j[1] + (8 if k == "k" else 0), :], ps[:, 0:T], ACT.Copy), j)
                elif k in ("qn", "kn"):
                    if k == "qn":
                        act.wait_ge(qk_ready, 1 + j[1] // 4)
                    release(act, fn(rs[:, j[1] % 4, :], ps[:, 0:T], ACT.Sqrt, bias=epsc[:], scale=1.0 / HD), j)
                elif k == "v":
                    release(act, fn(vT[:, j[1], :], ps[:, 0:T], ACT.Copy), j)
                elif k in ("kt", "vt"):
                    a, (t0, n) = j[1], TOK[j[1]]
                    o, kind = (ktok[0:n, :], "k") if k == "kt" else (vtok[0:n, a, :], "v")
                    if k == "kt" and a:
                        act.wait_ge(o_k, 16 * a)
                    release(act, fn(o, ps[0:n, :], ACT.Copy), j)
                    dst = t[f"{kind}_prompt" if a < 2 else f"{kind}_sample"].rearrange("o b q h d -> (o b q) (h d)")
                    act.dma_start(dst[t0:t0 + n, :] if a < 2 else dst, o).then_inc(o_k if k == "kt" else o_small, 16)
                elif k == "s":
                    p = j[2]
                    act.wait_ge(s_max, 2 * j[1] + p + 1)
                    for q, (lo, hi) in enumerate(((0, 128), (128, 384))):
                        link(fn(pb[:, p, lo:hi], pb[:, p, lo:hi], ACT.Exp, bias=sm2[:, 4 * p + q:4 * p + q + 1],
                                accum_out=sm2[:, 4 * p + 2 + q:4 * p + 3 + q]), s_exp if q else act_step)
                elif k == "pt":
                    release(act, fn(pT[:, j[2], :], ps[:, 0:384], ACT.Copy), j)
                elif k == "o2":
                    release(act, fn(attT[:, j[1], 0:NP], ps[:, 0:NP], ACT.Copy), j)
                elif k == "xbc":
                    i = j[1]
                    if i >= 2:
                        act.wait_ge(conv_ready, i - 1)
                    link(fn(xa[:, i % 2, 3:3 + NP], ps[:, 0:NP], ACT.Copy))
                    release(act, fn(xa[:, i % 2, 3 + NP + 3:XW:4], ps[:, NP:T], ACT.Copy), j)
                    if i:
                        conv_silu(i - 1)
                elif k == "sk":
                    b, q = j[1], j[2]
                    release(act, fn(ktb[:, b % 2, :, 128 * q:128 * q + 128],
                                    ps.rearrange("p (m k) -> p m k", m=4), ACT.Copy), j)
                elif k == "sp":
                    for q in range(NPG):
                        link(fn(psT[:, q, 0:128], ps[:, 128 * q:128 * q + 128], ACT.Copy))
                    release(act, fn(pn[0:NS, 0:128], ps[0:NS, 256:384], ACT.Copy), j)
                elif k == "so":
                    act.wait_ge(o_k, 48)
                    release(act, fn(otok[:], ps[:], ACT.Copy), j)
                elif k == "ct":
                    i = j[1]
                    act.wait_ge(*((o_tail, 32 * i) if i else (o_small, 16 * 5)))
                    release(act, fn(ctok[0:27, :], ps[0:27, :], ACT.Copy), j)
                    act.dma_start(t["conv_sample"].rearrange("o b w c -> (o b w) c")[:, 512 * i:512 * i + 512],
                                  ctok[0:24, :]).then_inc(o_tail, 16)
                    act.dma_start(t["conv_prompt"].rearrange("o b w c -> (o b w) c")[:, 512 * i:512 * i + 512],
                                  ctok[24:27, :]).then_inc(o_tail, 16)
                elif k == "bs":
                    release(act, fn(wdf[0:NS, 512 * j[1]:512 * j[1] + 512], ps[0:NS, :], ACT.Copy), j)
                    if j[1]:
                        act.dma_start(bc_d, wdf[0:NS, :]).then_inc(bs_out, 16)
                elif k == "bt":
                    release(act, fn(btok[:, j[1], :], ps[:], ACT.Copy), j)
                elif k == "s1":
                    release(act, fn(s1T[:, 512 * j[1]:512 * j[1] + 512], ps[:], ACT.Copy), j)
                elif k == "ab":
                    a, b = j[1], j[2]
                    if a == 1:
                        filled(act, j)
                        if b >= 2:
                            filled(act, ("y", 1, b - 2))
                        link(fn(ce[:, b % 2, :], banks[bank_of[j][0]][:], ACT.Exp), et_ready)
                    read_out(act, j)
                    link(fn(wd[:, b % 2, :], wd[:, b % 2, :], ACT.Exp), seg_exp)
                elif k == "fs":
                    i = j[1]
                    if i >= 2:
                        act.wait_ge(o_fs[i % 2], 16)
                    release(act, fn(wd[:, i % 2, :], ps[:], ACT.Copy), j)
                    act.dma_start(fs_d[0, :, 4 * i:4 * i + 4, :], wd[:, i % 2, :].rearrange("p (c n) -> p c n", c=4))\
                       .then_inc(o_fs[i % 2], 16)
                elif k == "z":
                    i = j[1]
                    if i >= 2:
                        act.wait_ge(zg_done, i - 1)
                    release(act, fn(zs[:, i % 2, :], ps[:, 0:T], ACT.Silu), j)
                elif k == "g":
                    release(act, fn(gT[:, j[1], :], ps[:, 0:T], ACT.Sigmoid), j)
                elif k == "yn":
                    release(act, fn(rs[:, j[1], :], ps[:, 0:T], ACT.Sqrt, bias=epsc[:], scale=SG / DI), j)
                elif k == "ht":
                    a, f, n = j[1], j[2], TOK[j[1]][1]
                    release(act, fn(h2tok[0:n, a, 512 * f:512 * f + 512], ps[0:n, :], ACT.Copy), j)

            def experts(it):
                act.wait_ge(selT_done, it + 2)
                act.wait_ge(comb_filled, it * 8 + 1)
                fn(selT, banks[4][:, 0:T], ACT.Copy).then_inc(selT_ready, 1)
                act.wait_ge(gate_done, it + 2)
                act.wait_ge(act_ready, it + 1)
                fn(gact, banks[2][:], ACT.Silu).then_inc(silu_ready, 1)
                act.wait_ge(actT_done, it + 1)
                fn(aT.rearrange("p k s -> p (k s)"), banks[5][:], ACT.Copy).then_inc(actT_ready, 1)
                act.wait_ge(down_done, it + 2)
                for q in range(2):
                    ins = fn(outs[:, 512 * q:512 * q + 512], banks[q][:], ACT.Copy)
                ins.then_inc(out_ready, 1)

            with act.Fori(0, NE // 2) as j:
                experts(j)
            act.wait_ge(rk_ready, 1)
            extra = act.value_load(xrd[0:1, 0:1], min_val=0, max_val=4)
            with act.If(extra > 0):
                with act.Fori(0, extra) as r:
                    with act.Fori(0, NE // 2) as j:
                        experts(r * 8 + (j + 8))
            for j in late:
                ps, (a, f), n = filled(act, j), j[1:], TOK[j[1]][1]
                release(act, fn(yout[0:n, a, 512 * f:512 * f + 512], ps[0:n, :], ACT.Copy), j)

        @block.vector
        def _(dve):
            link = stepper(dve, dve_step)
            v = nc.vector
            for s in (act_ready, comb_read):
                dve.sem_inc(s, 1)
            norm_of = ((48, 8, 0), (56, 32, 24))

            def squares(i):
                link(v.tensor_tensor(u[:, 0:KD, :], xT[:], xT[:], ALU.mult), sq_ready)

            def normed(i):
                gv, sc, sh = norm_of[i]
                link(v.reciprocal(rs[:, 0, :], rs[:, 0, :]))
                link(v.tensor_tensor(u[:, 0:KD, :], xT[:], rs[:, 0:1, :].to_broadcast([128, KD, T]), ALU.mult))
                link(v.scalar_tensor_tensor(gsc[:], modT[:, sc:sc + KD, :], 1.0,
                                            vec[:, gv:gv + KD].unsqueeze(2).to_broadcast([128, KD, NC]),
                                            ALU.add, ALU.mult))
                for c in range(KD):
                    v.tensor_scalar(hT[:, c, 0:NP], u[:, c, 0:NP], gsc[:, c, NS:NC], modT[:, sh + c, NS:NC],
                                    ALU.mult, ALU.add)
                link(v.tensor_tensor(hT[:, :, NP:T], u[:, 0:KD, NP:T], gsc[:, :, 0:NS], ALU.mult))
                link(v.tensor_tensor(hT[:, :, NP:T], hT[:, :, NP:T], modT[:, sh:sh + KD, 0:NS], ALU.add), h_ready)

            def weigh(a, b):
                dve.wait_ge(seg_exp, 8 * a + b + 1)
                w3 = wd[:, b % 2, :].rearrange("p (h k) -> p h k", h=4)
                link(v.tensor_tensor(w3, w3, cbm[:, b // 2:b // 2 + 1, :].to_broadcast([128, 4, 128]), ALU.mult), w_ready)

            def state_sum(i):
                dve.wait_ge(st_prod, 2 * i + 2)
                b, hf = i // 2, i % 2
                link(v.tensor_reduce(yT[:, 8 * hf:8 * hf + 8, NP + b], prod.rearrange("p (c n) -> p c n", c=8),
                                     AX.X, ALU.add), st_red)

            def first_max(src, m, best, tmp):
                m3 = m.unsqueeze(2).to_broadcast([128, 3, 4])
                link(v.tensor_reduce(m, src, AX.X, ALU.max))
                link(v.tensor_tensor(best, src, m3, ALU.is_equal))
                link(v.tensor_tensor(best, best, w4[:].unsqueeze(1).to_broadcast([128, 3, 4]), ALU.mult))
                link(v.tensor_reduce(tmp, best, AX.X, ALU.max))
                link(v.tensor_tensor(best, best, tmp.unsqueeze(2).to_broadcast([128, 3, 4]), ALU.is_equal))

            def route():
                m16 = rw[0].unsqueeze(2).to_broadcast([128, 3, NE])
                link(v.tensor_reduce(rw[0], lg, AX.X, ALU.max))
                link(v.tensor_tensor(lg, lg, m16, ALU.subtract), asg_ready)
                dve.wait_ge(rk_exp, 1)
                link(v.tensor_reduce(rw[1], lg, AX.X, ALU.add))
                link(v.reciprocal(rw[1], rw[1]))
                link(v.tensor_tensor(lg, lg, rw[1].unsqueeze(2).to_broadcast([128, 3, NE]), ALU.mult))
                lg4 = lg.rearrange("p a (g e) -> p a g e", g=NG)
                gm, og, pin, o1, o2, we = rt[0], rt[1], rt[2], rt[3], rt[4], rt[5]
                link(v.tensor_reduce(gm, lg4, AX.X, ALU.max))
                first_max(gm, rw[2], og, rw[3])
                pg4 = prg.rearrange("p a (g e) -> p a g e", g=NG)
                og4 = og.unsqueeze(3).to_broadcast([128, 3, NG, EPG])
                link(v.tensor_tensor(pg4, lg4, og4, ALU.mult))
                link(v.tensor_reduce(pin, prg.rearrange("p a (g e) -> p a e g", g=NG), AX.X, ALU.add))
                first_max(pin, rw[4], o1, rw[3])
                link(v.scalar_tensor_tensor(pin, o1, -4.0, pin, ALU.mult, ALU.add))
                first_max(pin, rw[5], o2, rw[3])
                link(v.tensor_tensor(rw[6], rw[4], rw[5], ALU.add))
                link(v.reciprocal(rw[6], rw[6]))
                link(v.tensor_tensor(rw[4], rw[4], rw[6], ALU.mult))
                link(v.tensor_tensor(rw[5], rw[5], rw[6], ALU.mult))
                link(v.tensor_tensor(we, o1, rw[4].unsqueeze(2).to_broadcast([128, 3, 4]), ALU.mult))
                link(v.tensor_tensor(pin, o2, rw[5].unsqueeze(2).to_broadcast([128, 3, 4]), ALU.mult))
                link(v.tensor_tensor(we, we, pin, ALU.add))
                link(v.tensor_tensor(o1, o1, o2, ALU.add))
                link(v.tensor_tensor(o1, o1, vm[:].unsqueeze(2).to_broadcast([128, 3, 4]), ALU.mult))
                link(v.tensor_tensor(we, we, vm[:].unsqueeze(2).to_broadcast([128, 3, 4]), ALU.mult))
                for dst, e4 in ((cmb, we), (asg, o1)):
                    for a in range(3):
                        link(v.tensor_tensor(dst[:, a, :].rearrange("p (g e) -> p g e", g=NG),
                                             og[:, a, :].unsqueeze(2).to_broadcast([128, NG, EPG]),
                                             e4[:, a, :].unsqueeze(1).to_broadcast([128, NG, EPG]), ALU.mult))
                link(v.tensor_copy(asb[:], asg), asg_ready)

            for j in jobs:
                k = j[0]
                if k == "cT":
                    ps = filled(dve, j)
                    dve.wait_ge(consts, 2)
                    release(dve, v.tensor_copy(cT[:, :, 0:NC], ps[:, 0:KD * NC].rearrange("p (k c) -> p k c", k=KD)), j)
                elif k == "vecs":
                    ps = filled(dve, j)
                    release(dve, v.tensor_copy(vec[:], ps[:, 0:200]), j)
                elif k == "modt":
                    ps, o = filled(dve, j), KD * j[1]
                    for q in range(2):
                        ins = v.tensor_tensor(modT[:, o + q:o + KD:2, :],
                                              ps[:, 128 * q:128 * q + 128].rearrange("p (i c) -> p i c", i=4)[:, :, 0:NC],
                                              vec[:, o + q:o + KD:2].unsqueeze(2).to_broadcast([128, 4, NC]), ALU.add)
                        if q:
                            release(dve, ins, j)
                        else:
                            link(ins)
                    if j[1] == 1:
                        normed(0)
                elif k == "xt":
                    ps, a, f, (t0, n) = filled(dve, j), j[1], j[2], TOK[j[1]]
                    release(dve, v.tensor_copy(xT[:, 4 * f:4 * f + 4, t0:t0 + n],
                                               ps[:, 0:4 * n].rearrange("p (q t) -> p q t", q=4)), j)
                    if a == 2 and f == 1:
                        squares(0)
                elif k == "ssq":
                    read_out(dve, j)
                    if j[1] == 1:
                        normed(1)
                elif k == "cst":
                    ps = filled(dve, j)
                    release(dve, v.tensor_copy(stT[:, 12 * j[1]:12 * j[1] + 12, :],
                                               ps[:, 0:288].rearrange("p (c s) -> p c s", c=12)), j)
                elif k == "fd":
                    ps = filled(dve, j)
                    dve.wait_ge(late_in, 16 * 12)
                    w0, w1, w2 = fdw[:, 0, :], fdw[:, 1, :], fdw[:, 2, :]
                    release(dve, v.tensor_scalar(fd[:], ps[0:HB, 0:T], hcol[:, 0:1], None, ALU.add), j)
                    link(v.tensor_scalar(gqk[:, 0:1], gqk[:, 0:1], HD ** -0.5, None, ALU.mult))
                    link(v.tensor_scalar(nident[:], ident[0:HB, 0:HB], -1.0, None, ALU.mult))
                    dve.wait_ge(fd_exp, 1)
                    link(v.tensor_scalar(w1, w0, 2.0, None, ALU.add))
                    link(v.reciprocal(w1, w1))
                    link(v.tensor_tensor(w0, w0, w1, ALU.mult))
                    link(v.tensor_tensor(w1, w0, w0, ALU.mult))
                    link(v.tensor_scalar(w2, w1, 1.0 / 15, None, ALU.mult))
                    for c in (13, 11, 9, 7, 5, 3):
                        link(v.scalar_tensor_tensor(w2, w2, 1.0 / c, w1, ALU.add, ALU.mult))
                    link(v.scalar_tensor_tensor(w2, w2, 1.0, w0, ALU.add, ALU.mult))
                    link(v.tensor_scalar(w1[0:SH], fd[0:SH, :], 0.0, None, ALU.max))
                    link(v.scalar_tensor_tensor(fd[0:SH, :], w2[0:SH], 2.0, w1[0:SH], ALU.mult, ALU.add))
                    link(v.tensor_scalar(w1[SH:HB], fd[SH:HB, :], 0.0, None, ALU.min))
                    link(v.scalar_tensor_tensor(fd[SH:HB, :], w2[SH:HB], -2.0, w1[SH:HB], ALU.mult, ALU.add))
                    link(v.tensor_scalar(hcol[0:SH, 1:2], hcol[0:SH, 1:2], -1.0, None, ALU.mult))
                    link(v.tensor_scalar(w0[0:SH], fd[0:SH, :], hcol[0:SH, 1:2], None, ALU.mult))
                    for c in range(2):
                        cols = slice(128 * c, 128 * c + 128)
                        link(v.tensor_tensor_scan(acsT[0:SH, cols], onesf[0:SH, :], w0[0:SH, cols], 0.0,
                                                  ALU.mult, ALU.add))
                        link(v.tensor_tensor_scan(acsT[SH:HB, cols], onesf[SH:HB, :], fd[SH:HB, cols],
                                                  acsT[SH:HB, 127:128] if c else 0.0, ALU.mult, ALU.add))
                    link(v.tensor_scalar(w2[0:SH, 0:128], onesf[0:SH, :], acsT[0:SH, 255:256], None, ALU.mult))
                    link(v.tensor_copy(ex[:, 0:NS], fd[0:SH, NP:T]))
                    link(v.tensor_copy(ex[:, 2 * NS:2 * NS + 1], hcol[0:SH, 2:3]))
                    link(v.tensor_copy(ex[:, NS:2 * NS], w0[0:SH, NP:T]), fd_sp)
                elif k == "ft":
                    ps = filled(dve, j)
                    v.tensor_copy(tokc[:, 0:64].rearrange("p (a h) -> p a h", a=2),
                                  ps[:, 0:96].rearrange("p (a h) -> p a h", a=2)[:, :, 0:SH])
                    v.tensor_copy(tokc[:, 64:224], ps[:, 144:304])
                    v.tensor_copy(lft[:, 0:2, :], ps[:, 0:96].rearrange("p (a h) -> p a h", a=2)[:, :, SH:HB])
                    release(dve, v.tensor_copy(lft[0:NS, 2, :], ps[0:NS, 96 + SH:96 + HB]), j)
                    dve.wait_ge(consts, 4)
                    link(v.tensor_tensor(lfn[0:NS, :].rearrange("p (b h) -> p b h", b=NS),
                                         lft[0:NS, 2:3, :].to_broadcast([NS, NS, NH]),
                                         bm8[:].rearrange("p (b h) -> p b h", b=NS), ALU.mult), lfn_ready)
                elif k in ("kn", "qn"):
                    c0 = 8 if k == "kn" else 4 * (j[1] // 4)
                    base = j[1] - j[1] % 4
                    if j[1] % 4 == 0:
                        for i in range(4):
                            read_out(dve, (k[0], base + i))
                        link(v.tensor_tensor(u[:, 0:4, :], qkT[:, c0:c0 + 4, :], qkT[:, c0:c0 + 4, :], ALU.mult), qk_sq)
                    elif j[1] % 4 == 3:
                        for i in range(4):
                            read_out(dve, (k, base + i))
                        link(v.reciprocal(rs[:], rs[:]))
                        col = gqk[:, 1:2] if k == "kn" else gqk[:, 0:1]
                        link(v.scalar_tensor_tensor(qkT[:, c0:c0 + 4, :], qkT[:, c0:c0 + 4, :], col, rs[:],
                                                    ALU.mult, ALU.mult), qk_ready)
                        if j == ("qn", 7):
                            dve.wait_ge(qbd_zero, 1)
                            for h in range(2):
                                dst = qbd[64 * h:64 * h + 64, 2 * h:2 * h + 4224]\
                                    .rearrange("p (b m x) -> p b m x", b=NS, m=4)[:, :, :, 0:2]
                                qs = qkT[64 * h:64 * h + 64, 0:8, NP:T].rearrange("p (m s) b -> p b m s", s=2)
                                link(v.tensor_copy(dst, qs), qbd_ready)
                elif k == "s":
                    ps, p = filled(dve, j), j[2]
                    release(dve, v.tensor_tensor(pb[:, p, :], ps[:, 0:384], cmask[:], ALU.add), j)
                    for q, (lo, hi) in enumerate(((0, 128), (128, 384))):
                        link(v.tensor_reduce(sm2[:, 4 * p + q:4 * p + q + 1], pb[:, p, lo:hi], AX.X, ALU.max, negate=True),
                             s_max if q else dve_step)
                elif k == "pt":
                    p = j[2]
                    dve.wait_ge(s_exp, 2 * j[1] + p + 1)
                    link(v.reciprocal(sm2[:, 4 * p + 2:4 * p + 4], sm2[:, 4 * p + 2:4 * p + 4]))
                    for q, (lo, hi) in enumerate(((0, 128), (128, 384))):
                        link(v.tensor_scalar(pb[:, p, lo:hi], pb[:, p, lo:hi], sm2[:, 4 * p + 2 + q:4 * p + 3 + q], None,
                                             ALU.mult), p_ready if q else dve_step)
                elif k == "xbc":
                    i, x = j[1], xa[:, j[1] % 2, :]
                    read_out(dve, j)
                    xs4 = x[:, 3 + NP:XW].rearrange("p (b w) -> p b w", w=4)
                    link(v.tensor_copy(xs4[:, :, 0:3], stT[:, i, :].rearrange("p (b w) -> p b w", w=3)))
                    link(v.tensor_copy(tails[:, i, 0:24].rearrange("p (b w) -> p b w", w=3), xs4[:, :, 1:4]))
                    link(v.tensor_copy(tails[:, i, 24:27], x[:, NP:NP + 3]))
                    if i >= 2:
                        dve.wait_ge(u_ready, i - 1)
                    acc = cacc[:, i % 2, :]
                    link(v.tensor_scalar(acc, x[:, 0:XO], vec[:, 104 + i:105 + i], vec[:, 80 + i:81 + i], ALU.mult, ALU.add))
                    for w in range(1, 4):
                        link(v.scalar_tensor_tensor(acc, x[:, w:w + XO], vec[:, 104 + 24 * w + i:105 + 24 * w + i], acc,
                                                    ALU.mult, ALU.add), conv_ready if w == 3 else dve_step)
                elif k == "sk" and j[2] == 1:
                    filled(dve, j)
                    link(v.tensor_copy(ktb[:, j[1] % 2, :, 256], qkT[:, 8:12, NP + j[1]]), kcol_ready)
                elif k == "sp":
                    dve.wait_ge(ss_done, 1)
                    link(v.tensor_reduce(sm2[:, 8:9], sbank[:, 0:257], AX.X, ALU.max, negate=True), ss_max)
                    dve.wait_ge(ss_exp, 1)
                    link(v.reciprocal(sm2[:, 9:10], sm2[:, 9:10]))
                    link(v.tensor_scalar(ps_s, ps_s, sm2[:, 9:10], None, ALU.mult))
                    link(v.tensor_scalar(pnb, bm2[:], ps_s[:, 256:257], None, ALU.mult), sp_ready)
                elif k == "sx":
                    ps, hf = filled(dve, j), j[1]
                    for m in range(4):
                        for h in range(2):
                            x = 4 * m + 2 * h
                            ins = v.tensor_copy(
                                attT[64 * h:64 * h + 64, 2 * m:2 * m + 2, NP + 4 * hf:NP + 4 * hf + 4].rearrange("p s b -> p b s"),
                                ps[64 * h:64 * h + 64, 128 * m:128 * m + 128].rearrange("p (b x) -> p b x", b=4)[:, :, x:x + 2])
                    release(dve, ins, j)
                elif k == "exp":
                    ps = filled(dve, j)
                    release(dve, v.tensor_copy(exo[:], ps[:, 0:NXB * 17].rearrange("p (c k) -> p c k", c=NXB)), j)
                    link(v.tensor_tensor(exo[:, :, 0:NS], exo[:, :, 0:NS], u[:, 0:NXB, NP:T], ALU.mult), xds_ready)
                elif k == "xs":
                    ps, a, g = filled(dve, j), j[1], j[2]
                    dve.wait_ge(o_small, 16 * 5)
                    dt = tokc[:, 32 * a + 8 * g:32 * a + 8 * g + 8].unsqueeze(2).to_broadcast([128, 8, HD])
                    release(dve, v.tensor_tensor(xd[:, a, 512 * g:512 * g + 512].rearrange("p (h d) -> p h d", h=8),
                                                 ps.rearrange("p (h d) -> p h d", h=8), dt, ALU.mult), j)
                elif k == "cb":
                    ps = filled(dve, j)
                    release(dve, v.tensor_tensor(cbm, ps.rearrange("p (g k) -> p g k", g=SG),
                                                 triu[:].unsqueeze(1).to_broadcast([128, SG, 128]), ALU.mult), j)
                elif k == "ab":
                    ps, a, b = filled(dve, j), j[1], j[2]
                    if a == 0 and b == 0:
                        dve.wait_ge(bs_out, 16)
                    for i in range(4):
                        h = 4 * b + i
                        if i == 0 and a == 1:
                            dve.wait_ge(et_ready, b + 1)
                        ins = v.tensor_scalar(wd[:, b % 2, 128 * i:128 * i + 128], ps[:, 128 * i:128 * i + 128],
                                              tokc[:, 64 + 32 * a + h:65 + 32 * a + h], 0.0, ALU.subtract, ALU.min)
                    release(dve, ins, j)
                    if b:
                        weigh(a, b - 1)
                elif k == "y":
                    a, b = j[1], j[2]
                    if b == 7:
                        weigh(a, 7)
                    ps = filled(dve, j)
                    for q in range(2):
                        hp, tk = 2 * b + q, slice(128 * a, 128 * a + 128)
                        ins = v.scalar_tensor_tensor(yT[:, hp, tk], u[:, hp, tk], exo[:, hp, 16:17],
                                                     ps[:, 128 * q:128 * q + 128], ALU.mult, ALU.add)
                    release(dve, ins, j)
                elif k == "z":
                    i = j[1]
                    read_out(dve, j)
                    v.tensor_copy(zsS[:, i, :], zs[:, i % 2, NP:T])
                    link(v.tensor_tensor(yT[:, i, 0:NP], yT[:, i, 0:NP], zs[:, i % 2, 0:NP], ALU.mult), zg_done)
                elif k == "ssm":
                    i, b, hf = j[1], j[1] // 2, j[1] % 2
                    dve.wait_ge(st_dec, i + 1)
                    dve.wait_ge(bc_full, 16 * (b + 1))
                    for c in range(8):
                        s = sst[:, i % 2, 128 * c:128 * c + 128]
                        gg = 2 * hf + c // 4
                        ins = v.scalar_tensor_tensor(s, bc[:, 128 * gg:128 * gg + 128], exo[:, 8 * hf + c, b:b + 1], s,
                                                     ALU.mult, ALU.add)
                    link(ins, st_new)
                    if i:
                        state_sum(i - 1)
                    if i == 2 * NS - 1:
                        state_sum(i)
                        dx = exo[:, :, 16:17].to_broadcast([128, NXB, NS])
                        link(v.tensor_tensor(exo[:, :, 0:NS], u[:, 0:NXB, NP:T], dx, ALU.mult))
                        link(v.tensor_tensor(yT[:, :, NP:T], yT[:, :, NP:T], exo[:, :, 0:NS], ALU.add))
                        link(v.tensor_tensor(yT[:, :, NP:T], yT[:, :, NP:T], zsS[:], ALU.mult))
                        link(v.tensor_tensor(u[:, 0:NXB, :], yT, yT, ALU.mult), y_sq)
                elif k == "yn":
                    g = j[1]
                    read_out(dve, j)
                    link(v.reciprocal(rs[:, g, :], rs[:, g, :]))
                    for c in range(4 * g, 4 * g + 4):
                        ins = v.scalar_tensor_tensor(yT[:, c, :], yT[:, c, :], vec[:, 64 + c:65 + c], rs[:, g, :],
                                                     ALU.mult, ALU.mult)
                    link(ins, y_ready)
                elif k == "pa":
                    ps, i = filled(dve, j), j[1]
                    read_out(dve, ("g", i))
                    release(dve, v.tensor_tensor(gT[:, i, :], gT[:, i, :], ps[:, 0:T], ALU.mult), j)
                elif k == "pb":
                    ps, i = filled(dve, j), j[1]
                    read_out(dve, ("g", 8 + i))
                    release(dve, v.tensor_tensor(gT[:, 8 + i, :], gT[:, 8 + i, :], ps[:, 0:T], ALU.mult), j)
                    link(v.tensor_tensor(gT[:, i, :], gT[:, i, :], gT[:, 8 + i, :], ALU.add), m_ready)
                elif k == "o":
                    ps, i = filled(dve, j), j[1]
                    v.scalar_tensor_tensor(xT[:, i, 0:NP], ps[:, 0:NP], modT[:, 16 + i, NS:NC], xT[:, i, 0:NP],
                                           ALU.mult, ALU.add)
                    release(dve, v.tensor_tensor(sm2[:, 16:24], ps[:, NP:T], modT[:, 16 + i, 0:NS], ALU.mult), j)
                    link(v.tensor_tensor(xT[:, i, NP:T], xT[:, i, NP:T], sm2[:, 16:24], ALU.add))
                    if i == KD - 1:
                        squares(1)
                elif k == "lr":
                    ps = filled(dve, j)
                    release(dve, v.tensor_scalar(lgT[0:NE, :], ps[0:NE, 0:T], brow[:], None, ALU.add), j)
                elif k == "lt":
                    link(v.memset(lg, 0.0))
                    ps = filled(dve, j)
                    v.tensor_copy(lg[:, 0:2, :], ps[:, 0:32].rearrange("p (a e) -> p a e", a=2))
                    release(dve, v.tensor_copy(lg[0:NS, 2, :], ps[0:NS, 32:48]), j)
                    route()
                elif k == "rk":
                    ps = filled(dve, j)
                    v.tensor_copy(rank, ps[:, 0:48].rearrange("p (a e) -> p a e", a=3))
                    release(dve, v.tensor_copy(cnt, ps[:, 48:64]), j)
                    link(v.tensor_reduce(rw[0][0:1, 0:1], cnt[0:1, :], AX.X, ALU.max))
                    link(v.tensor_scalar(rt[0][0:1, 0, :], thr[:], rw[0][0:1, 0:1], None, ALU.is_lt))
                    link(v.tensor_reduce(rw[1][0:1, 0:1], rt[0][0:1, 0, :], AX.X, ALU.add))
                    link(v.memset(Y[:], 0.0))
                    link(v.tensor_copy(xrd[:], rw[1][0:1, 0:1]), rk_ready)

            def experts(it, j):
                dve.wait_ge(gather_done, it + 1)
                dve.wait_ge(selT_done, it + 1)
                for w, m in enumerate((asg, cmb)):
                    for e in range(2):
                        for a in range(3):
                            col = bass.ds(j * 2 + e, 1)
                            ins = v.tensor_scalar(sel[:, w, a, BLK * e:BLK * e + BLK], iota[:], rank[:, a, col], m[:, a, col],
                                                  ALU.is_equal, ALU.mult)
                ins.then_inc(sel_ready, 1)
                dve.wait_ge(gather_done, it + 2)
                for q in range(2):
                    ins = v.tensor_copy(xg[:, 4 * q:4 * q + 4, :], banks[q][:].rearrange("p (k s) -> p k s", k=4))
                ins.then_inc(xg_ready, 1)
                dve.wait_ge(silu_ready, it + 1)
                dve.wait_ge(up_done, it + 2)
                v.tensor_tensor(hact, gact, banks[3][:], ALU.mult).then_inc(act_ready, 1)
                dve.wait_ge(comb_read, it * 8 + 1)
                for c in range(KD):
                    dve.wait_ge(comb_filled, it * 8 + (c + 2))
                    v.tensor_tensor(Y[:, c, :], Y[:, c, :], banks[6 + c % 2][:, 0:T], ALU.add).then_inc(comb_read, 1)

            with dve.Fori(0, NE // 2) as j:
                experts(j, j)
            dve.wait_ge(comb_read, 8 * KD + 1)
            extra = dve.value_load(xrd[0:1, 0:1], min_val=0, max_val=4)
            with dve.If(extra > 0):
                with dve.Fori(0, extra) as r:
                    v.tensor_scalar(rank, rank, -float(BLK), None, ALU.add).then_inc(rk_shift, 1)
                    with dve.Fori(0, NE // 2) as j:
                        dve.wait_ge(rk_shift, r + 1)
                        experts(r * 8 + (j + 8), j)
                    dve.wait_ge(comb_read, r * 64 + 129)
            for c in range(KD):
                v.scalar_tensor_tensor(xT[:, c, 0:NP], Y[:, c, 0:NP], modT[:, 40 + c, NS:NC], xT[:, c, 0:NP],
                                       ALU.mult, ALU.add)
            link(v.tensor_tensor(Y[:, :, NP:T], Y[:, :, NP:T], modT[:, 40:48, 0:NS], ALU.mult))
            link(v.tensor_tensor(xT[:, :, NP:T], xT[:, :, NP:T], Y[:, :, NP:T], ALU.add), yfin)

        @block.tensor
        def _(pe):
            mm, tr = nc.tensor.matmul, nc.tensor.transpose
            for s in (gather_done, selT_done, gate_done, up_done, down_done, comb_filled):
                pe.sem_inc(s, 1)

            def start(j):
                b, n = bank_of[j]
                if n > 1:
                    pe.wait_ge(bank_read[b], n - 1)
                return banks[b]

            def done(ins, j):
                ins.then_inc(bank_filled[bank_of[j][0]], 1)

            def landed(s):
                pe.wait_ge(slot_full[slot_at[s]], arrived_at[s])

            def flip(out, x):
                k = x.shape[0]
                return tr(out, x, ident[0:k, 0:k])

            for j in jobs:
                k = j[0]
                ps = start(j) if j in bank_of else None
                if k == "cT":
                    pe.wait_ge(consts, 1)
                    pe.wait_ge(cond_ready, 1)
                    for c in range(KD):
                        ins = flip(ps[:, NC * c:NC * c + NC], crow[0:NC, 128 * c:128 * c + 128])
                elif k == "vecs":
                    flip(ps[:, 0:104], vrow[0:104, 0, :])
                    ins = flip(ps[:, 104:200], vrow[0:96, 1, :])
                elif k == "mod":
                    read_out(pe, ("cT",))
                    for i in range(4):
                        landed(("mod", 4 * j[1] + i))
                    for c in range(KD):
                        for i in range(4):
                            ins = mm(ps[32 * i:32 * i + 32, 0:SW], cT[:, c, :], slot(("mod", 4 * j[1] + i))[:, c, :],
                                     start=c == 0, stop=c == KD - 1, tile_position=(0, 32 * i))
                elif k == "modt":
                    read_out(pe, ("mod", j[1]))
                    for q in range(2):
                        ins = flip(ps[:, 128 * q:128 * q + 128], mrow[:, 128 * q:128 * q + 128])
                elif k == "xt":
                    a, f, n = j[1], j[2], TOK[j[1]][1]
                    pe.wait_ge(x_in, 48)
                    for q in range(4):
                        c = 4 * f + q
                        ins = flip(ps[:, n * q:n * q + n], xin[0:n, a, 128 * c:128 * c + 128])
                elif k == "ssq":
                    pe.wait_ge(sq_ready, j[1] + 1)
                    pe.wait_ge(consts, 3)
                    for c in range(KD):
                        ins = mm(ps[:, 0:T], onesf[:], u[:, c, :], start=c == 0, stop=c == KD - 1)
                elif k == "cst":
                    pe.wait_ge(st_in, 16)
                    for q in range(12):
                        c = 12 * j[1] + q
                        ins = flip(ps[:, 24 * q:24 * q + 24], csin[0:24, 128 * c:128 * c + 128])
                elif k == "fd":
                    pe.wait_ge(h_ready, 1)
                    pe.wait_ge(late_in, 16 * 12)
                    for c in range(KD):
                        ins = mm(ps[0:HB, 0:T], wfd[:, c, :], hT[:, c, :], start=c == 0, stop=c == KD - 1)
                elif k == "ft":
                    pe.wait_ge(fd_e, 1)
                    for a, (t0, n) in enumerate(TOK):
                        ins = flip(ps[0:n, HB * a:HB * a + HB], fd[:, t0:t0 + n])
                    for i, x in enumerate((acsT[0:SH, 0:128], acsT[0:SH, 128:256], fdw[0:SH, 1, 0:128],
                                           fdw[0:SH, 1, 128:256], fdw[0:SH, 2, 0:128])):
                        ins = flip(ps[:, 144 + 32 * i:176 + 32 * i], x)
                elif k in ("q", "k", "v", "xbc", "z", "g"):
                    s, h = slots_of(j)[0], j[1] % 2
                    landed(s)
                    for c in range(KD):
                        w = slot(s)[:, c, 128 * h:128 * h + 128]
                        ins = mm(ps[:, 0:T], w, hT[:, c, :], start=c == 0, stop=c == KD - 1)
                elif k in ("kn", "qn"):
                    pe.wait_ge(qk_sq, 1 if k == "kn" else 2 + j[1] // 4)
                    ins = mm(ps[:, 0:T], blk[:], u[:, j[1] % 4, :], start=True, stop=True)
                elif k == "kt":
                    t0, n = TOK[j[1]]
                    pe.wait_ge(qk_ready, 1)
                    for m in range(4):
                        ins = flip(ps[0:n, 128 * m:128 * m + 128], qkT[:, 8 + m, t0:t0 + n])
                elif k == "vt":
                    t0, n = TOK[j[1]]
                    read_out(pe, ("v", 3))
                    for m in range(4):
                        ins = flip(ps[0:n, 128 * m:128 * m + 128], vT[:, m, t0:t0 + n])
                elif k == "s":
                    c, p = j[1], j[2]
                    m, s, r = c // 2, c % 2, slice(64 * p, 64 * p + 64)
                    h = 4 * m + 2 * p + s
                    pe.wait_ge(qk_ready, 3)
                    pe.wait_ge(fd_e, 1)
                    neg = nident[SH:HB, SH + h:SH + h + 1].to_broadcast([NH, 128])
                    for q0, lo, n in ((0, 0, 128), (128, 128, 256)):
                        mm(ps[:, lo:lo + n], qkT[r, c, q0:q0 + 128], qkT[r, 8 + m, 0:n], start=True, stop=False)
                        ins = mm(ps[:, lo:lo + n], neg, acsT[SH:HB, 0:n], start=False, stop=True)
                elif k == "pt":
                    p = j[2]
                    pe.wait_ge(p_ready, 2 * j[1] + p + 1)
                    for q in range(3):
                        ins = flip(ps[:, 128 * q:128 * q + 128], pb[:, p, 128 * q:128 * q + 128])
                elif k == "o2":
                    c = j[1]
                    for p in range(2):
                        read_out(pe, ("pt", c, p))
                        g = 2 * (c // 2) + p
                        vs = [vtok[:, a, 64 * g:64 * g + 64] for a in range(2)]
                        r = slice(64 * p, 64 * p + 64)
                        mm(ps[r, 0:128], vs[0], pT[:, p, 0:128], start=True, stop=True)
                        mm(ps[r, 128:256], vs[0], pT[:, p, 128:256], start=True, stop=False)
                        ins = mm(ps[r, 128:256], vs[1], pT[:, p, 256:384], start=False, stop=True)
                elif k == "sk":
                    b, q = j[1], j[2]
                    pe.wait_ge(kv_full[b % 4], 32 * (b // 4 + 1))
                    for m in range(4):
                        ins = flip(ps[:, 128 * m:128 * m + 128], kvr[:, b % 4, q, 128 * m:128 * m + 128])
                elif k == "ss":
                    b = j[1]
                    read_out(pe, ("sk", b, 0))
                    read_out(pe, ("sk", b, 1))
                    pe.wait_ge(kcol_ready, b + 1)
                    pe.wait_ge(qbd_ready, 2)
                    for m in range(4):
                        o = 128 * (4 * b + m)
                        mm(sbank[:, 0:257], qbd[:, o:o + 128], ktb[:, b % 2, m, :], start=b == 0 and m == 0, stop=False)
                    if b == NS - 1:
                        pe.wait_ge(lf_in, 16 * NS * NPG)
                        pe.wait_ge(lfn_ready, 1)
                        mm(sbank[:, 0:257], lfc[:, 0, :], ntri[:, 128:385], start=False, stop=False)
                        mm(sbank[:, 0:257], lfc[:, 1, :], ntri[:, 0:257], start=False, stop=False)
                        mm(sbank[:, 256:257], lfn[0:NS, :], ntri[0:NS, 384:385], start=False, stop=True)\
                            .then_inc(ss_done, 1)
                    continue
                elif k == "sp":
                    pe.wait_ge(sp_ready, 1)
                    for q in range(NPG):
                        flip(ps[:, 128 * q:128 * q + 128], ps_s[:, 128 * q:128 * q + 128])
                    ins = mm(ps[0:NS, 256:384], pnb, ident[:], start=True, stop=True)
                elif k == "so":
                    hf = j[1]
                    read_out(pe, ("sp",))
                    for b in range(4):
                        pe.wait_ge(kv_full[b], 96 + 32 * hf)
                    for q in range(NPG + 1):
                        for bb in range(4):
                            c = 16 * (4 * hf + bb)
                            w, x = ((psT[:, q, c:c + 32], kvr[:, bb, q, :]) if q < NPG else
                                    (pn[0:NS, c:c + 32], vtok[0:NS, 2, :]))
                            ins = mm(ps[32 * bb:32 * bb + 32, :], w, x, start=q == 0, stop=q == NPG,
                                     tile_position=(0, 32 * bb))
                elif k == "sx":
                    read_out(pe, ("so", j[1]))
                    for m in range(4):
                        ins = flip(ps[:, 128 * m:128 * m + 128], otok[:, 128 * m:128 * m + 128])
                elif k == "ct":
                    pe.wait_ge(conv_ready, NCB)
                    for q in range(4):
                        ins = flip(ps[0:27, 128 * q:128 * q + 128], tails[:, 4 * j[1] + q, :])
                elif k == "bs":
                    pe.wait_ge(u_ready, NCB)
                    for q in range(4):
                        ins = flip(ps[0:NS, 128 * q:128 * q + 128], u[:, NXB + 4 * j[1] + q, NP:T])
                elif k == "exp":
                    for c in range(NXB):
                        for h in range(2):
                            w = ident[0:SH, 2 * c + h:2 * c + h + 1].to_broadcast([SH, 64])
                            ins = mm(ps[64 * h:64 * h + 64, 17 * c:17 * c + 17], w, ex[:], start=True, stop=True)
                elif k == "bt":
                    for q in range(4):
                        ins = flip(ps[:, 128 * q:128 * q + 128], u[:, NXB + q, 128 * j[1]:128 * j[1] + 128])
                elif k == "xs":
                    a, g = j[1], j[2]
                    for q in range(4):
                        ins = flip(ps[:, 128 * q:128 * q + 128], u[:, 4 * g + q, 128 * a:128 * a + 128])
                elif k == "s1":
                    g = j[1]
                    read_out(pe, ("bt", 0))
                    pe.wait_ge(xe_ready, 1)
                    ins = mm(ps[:], btok[:, 0, 128 * g:128 * g + 128], xe[:, 0, 512 * g:512 * g + 512],
                             start=True, stop=True)
                elif k == "cb":
                    tk = slice(128 * j[1], 128 * j[1] + 128)
                    for g in range(SG):
                        ins = mm(ps[:, 128 * g:128 * g + 128], u[:, NXB + g, tk], u[:, NXB + SG + g, tk],
                                 start=True, stop=True)
                elif k == "ab":
                    a, b = j[1], j[2]
                    for i in range(4):
                        h = 4 * b + i
                        ins = mm(ps[:, 128 * i:128 * i + 128], ident[0:SH, h:h + 1].to_broadcast([SH, 128]),
                                 acsT[0:SH, 128 * a:128 * a + 128], start=True, stop=True)
                elif k == "y":
                    a, b = j[1], j[2]
                    pe.wait_ge(w_ready, 8 * a + b + 1)
                    read_out(pe, ("xs", a, b // 2))
                    if a == 1:
                        pe.wait_ge(ce_ready, b + 1)
                        read_out(pe, ("s1", 3))
                    for i in range(4):
                        h = 4 * b + i
                        o = ps[64 * (i % 2):64 * (i % 2) + 64, 128 * (i // 2):128 * (i // 2) + 128]
                        ins = mm(o, xd[:, a, 64 * h:64 * h + 64], wd[:, b % 2, 128 * i:128 * i + 128],
                                 start=True, stop=a == 0)
                        if a == 1:
                            ins = mm(o, s1T[:, 64 * h:64 * h + 64], ce[:, b % 2, 128 * i:128 * i + 128],
                                     start=False, stop=True)
                elif k == "fs":
                    i = j[1]
                    pe.wait_ge(xe_ready, 3)
                    read_out(pe, ("bt", 1))
                    for q in range(4):
                        c = 4 * i + q
                        for a in range(2):
                            ins = mm(ps[:, 128 * q:128 * q + 128], xe[:, a, 128 * c:128 * c + 128],
                                     btok[:, a, 128 * i:128 * i + 128], start=a == 0, stop=a == 1)
                elif k == "ssm":
                    continue
                elif k == "pa":
                    i = j[1]
                    s = slots_of(j)[0]
                    landed(s)
                    read_out(pe, ("o2", 7))
                    read_out(pe, ("sx", 1))
                    for c in range(KD):
                        ins = mm(ps[:, 0:T], slot(s)[:, c, 128 * (i % 2):128 * (i % 2) + 128], attT[:, c, :],
                                 start=c == 0, stop=c == KD - 1)
                elif k == "yn":
                    g = j[1]
                    pe.wait_ge(y_sq, 1)
                    for c in range(4):
                        ins = mm(ps[:, 0:T], onesf[:], u[:, 4 * g + c, :], start=c == 0, stop=c == 3)
                elif k == "pb":
                    i = j[1]
                    for s in slots_of(j):
                        landed(s)
                    for c in range(NXB):
                        if i == 0 and c % 4 == 0:
                            pe.wait_ge(y_ready, c // 4 + 1)
                        w = slot(("pb", i // 2, c // KD))[:, c % KD, 128 * (i % 2):128 * (i % 2) + 128]
                        ins = mm(ps[:, 0:T], w, yT[:, c, :], start=c == 0, stop=c == NXB - 1)
                elif k == "o":
                    i = j[1]
                    s = slots_of(j)[0]
                    landed(s)
                    for c in range(KD):
                        if i == 0:
                            pe.wait_ge(m_ready, c + 1)
                        ins = mm(ps[:, 0:T], slot(s)[:, c, 128 * (i % 2):128 * (i % 2) + 128], gT[:, c, :],
                                 start=c == 0, stop=c == KD - 1)
                elif k == "lr":
                    pe.wait_ge(h_ready, 2)
                    for c in range(KD):
                        ins = mm(ps[0:NE, 0:T], wr[:, c, :], hT[:, c, :], start=c == 0, stop=c == KD - 1)
                elif k == "lt":
                    read_out(pe, ("lr",))
                    for a, (t0, n) in enumerate(TOK):
                        ins = flip(ps[0:n, NE * a:NE * a + NE], lgT[0:NE, t0:t0 + n])
                elif k == "ht":
                    a, f, (t0, n) = j[1], j[2], TOK[j[1]]
                    for q in range(4):
                        ins = flip(ps[0:n, 128 * q:128 * q + 128], hT[:, 4 * f + q, t0:t0 + n])
                elif k == "rk":
                    pe.wait_ge(asg_ready, 2)
                    for a in range(4):
                        for b in range(min(a + 1, 3)):
                            ins = mm(ps[:, NE * a:NE * a + NE], striu[:] if a == b else onesb[:], asb[:, b, :],
                                     start=b == 0, stop=b == min(a, 2))
                done(ins, j)

            for b in range(NBANK):
                pe.wait_ge(bank_read[b], at_moe[b])
            pe.wait_ge(rk_ready, 1)

            def experts(it):
                pe.wait_ge(sel_ready, it + 1)
                pe.wait_ge(out_ready, it + 1)
                for c in range(KD):
                    for a, (t0, n) in enumerate(TOK):
                        ins = mm(banks[c // 4][:, 128 * (c % 4):128 * (c % 4) + 128], h2tok[0:n, a, 128 * c:128 * c + 128],
                                 sel[0:n, 0, a, :], start=a == 0, stop=a == 2)
                ins.then_inc(gather_done, 1)
                for a, (t0, n) in enumerate(TOK):
                    ins = flip(banks[4][:, t0:t0 + n], sel[0:n, 1, a, :])
                ins.then_inc(selT_done, 1)
                pe.wait_ge(xg_ready, it + 1)
                for i, sig in enumerate((gate_done, up_done)):
                    for e in range(2):
                        pe.wait_ge(moe_full[2 * i + e], (it + 1) * 16)
                    for c in range(KD):
                        for e in range(2):
                            r = slice(BLK * e, BLK * e + BLK)
                            w = mslot[2 * i + e].rearrange("p (k n) -> p k n", k=KD)
                            ins = mm(banks[2 + i][r, :], xg[:, c, r], w[:, c, :], start=c == 0, stop=c == KD - 1,
                                     tile_position=(0, BLK * e))
                    ins.then_inc(sig, 1)
                pe.wait_ge(act_ready, it + 2)
                for q in range(4):
                    ins = flip(banks[5][:, 128 * q:128 * q + 128], hact[:, 128 * q:128 * q + 128])
                ins.then_inc(actT_done, 1)
                pe.wait_ge(actT_ready, it + 1)
                for e in range(2):
                    pe.wait_ge(moe_full[4 + e], (it + 1) * 16)
                for q in range(2):
                    for c in range(4):
                        for e in range(2):
                            r = slice(BLK * e, BLK * e + BLK)
                            w = mslot[4 + e].rearrange("p (k n) -> p k n", k=4)
                            ins = mm(banks[q][r, :], aT[:, c, r], w[:, c, 512 * q:512 * q + 512], start=c == 0,
                                     stop=c == 3, tile_position=(0, BLK * e))
                ins.then_inc(down_done, 1)
                pe.wait_ge(out_ready, it + 2)
                pe.wait_ge(selT_ready, it + 1)
                for c in range(KD):
                    pe.wait_ge(comb_read, it * 8 + max(c, 1))
                    mm(banks[6 + c % 2][:, 0:T], outs[:, 128 * c:128 * c + 128], selT, start=True, stop=True)\
                        .then_inc(comb_filled, 1)

            with pe.Fori(0, NE // 2) as j:
                experts(j)
            extra = pe.value_load(xrd[0:1, 0:1], min_val=0, max_val=4)
            with pe.If(extra > 0):
                with pe.Fori(0, extra) as r:
                    with pe.Fori(0, NE // 2) as j:
                        experts(r * 8 + (j + 8))
            pe.wait_ge(yfin, 1)
            for j in late:
                a, f, (t0, n) = j[1], j[2], TOK[j[1]]
                ps = start(j)
                for q in range(4):
                    ins = flip(ps[0:n, 128 * q:128 * q + 128], xT[:, 4 * f + q, t0:t0 + n])
                done(ins, j)


OUTS = [("y_prompt", (1, NP, D)), ("y_sample", (NS, 1, D)), ("k_prompt", (1, 1, NP, NKV, HD)),
        ("v_prompt", (1, 1, NP, NKV, HD)), ("logf_prompt", (1, 1, NP, NH)), ("ssm_prompt", (1, 1, SH, HD, NST)),
        ("conv_prompt", (1, 1, 3, CD)), ("k_sample", (1, NS, 1, NKV, HD)), ("v_sample", (1, NS, 1, NKV, HD)),
        ("logf_sample", (1, NS, 1, NH)), ("ssm_sample", (1, NS, SH, HD, NST)), ("conv_sample", (1, NS, 3, CD))]


def kernel(**inputs):
    import numpy as np
    import concourse.bacc as bacc
    from concourse.bass_utils import run_bass_kernel_spmd

    nc = bacc.Bacc("TRN2", target_bir_lowering=False, num_devices=1)
    arrays, t = {}, {}
    for name, x in inputs.items():
        a = np.ascontiguousarray(x)
        arrays["in_" + name] = a
        t[name] = nc.dram_tensor("in_" + name, a.shape, mybir.dt.from_np(a.dtype), kind="ExternalInput").ap()
    for name, shape in OUTS:
        t[name] = nc.dram_tensor("out_" + name, shape, F32, kind="ExternalOutput").ap()
    t["bc_scratch"] = nc.dram_tensor("bc_scratch", (NS, 2 * SG * NST), F32, kind="Internal").ap()
    build(nc, t)
    r = run_bass_kernel_spmd(nc, [arrays], core_ids=[0])
    return tuple(r.results[0]["out_" + name] for name, _ in OUTS)
```

```python
import concourse.bass as bass
from concourse import mybir
from contextlib import ExitStack

F32 = mybir.dt.float32
BF16 = mybir.dt.bfloat16
I32 = mybir.dt.int32
ALU = mybir.AluOpType
ACT = mybir.ActivationFunctionType
AX = mybir.AxisListType

D = 1024
NP, NS = 256, 8
T = NP + NS
NC = NS + 1
KD = D // 128
NH, NKV, HD = 16, 8, 64
PAGE, NPG = 128, 2
KVW = NKV * HD
DI, SH, SG, NST = 2048, 32, 4, 128
CD = DI + 2 * SG * NST
NCB = CD // 128
NXB = DI // 128
HB = SH + NH
NE, EPG, NG, FF = 16, 4, 4, 512
EPS = 1e-6
COL_K, COL_V, COL_F = D, D + KVW, D + 2 * KVW
COL_Z = COL_F + NH
COL_X = COL_Z + DI
COL_DT = COL_X + CD
COL_G = COL_DT + SH
IN_DIM = COL_G + 2 * D
TOK = [(0, 128), (128, 128), (256, NS)]
SW = 256
SLOT = KD * SW
NSLOT = 6
NBANK = 7
BLK = 64
XW = 3 + NP + 4 * NS
XO = XW - 3


def build(nc, t):
    ctx = ExitStack()
    with ctx:
        def sb(name, shape, dt=F32):
            return ctx.enter_context(nc.sbuf_tensor(name, shape, dt))

        def sem(name):
            return ctx.enter_context(nc.semaphore(name))

        ring = sb("weight_ring", [128, NSLOT * SLOT])
        xT = sb("x_residual", [128, KD, T])
        hT = sb("h_normed", [128, KD, T])
        modT = sb("modulation", [128, 6 * KD, NC])
        gsc = sb("norm_gain", [128, KD, NC])
        ident = sb("identity", [128, 128])
        nident = sb("neg_identity", [HB, HB])
        ntri = sb("neg_triangle", [128, 3 * 128 + 1])
        cmask = sb("causal_mask", [128, 384])
        triu = sb("upper_triangle", [128, 128])
        onesf = sb("ones", [128, 128])
        blk = sb("head_blocks", [128, 128])
        striu = sb("strict_upper", [128, 128], BF16)
        onesb = sb("ones_bf", [128, 128], BF16)
        bm8 = sb("sample_rows", [NS, 128])
        bm2 = sb("sample_cols", [128, NS])
        iota = sb("slot_numbers", [128, BLK])
        w4 = sb("first_weights", [128, 4])
        thr = sb("round_limits", [1, 4])
        vm = sb("valid_rows", [128, 3])
        epsc = sb("eps_col", [128, 1])
        vec = sb("vectors", [128, 200])
        gqk = sb("qk_gain", [128, 2])
        hcol = sb("head_cols", [HB, 4])
        brow = sb("router_bias", [NE, 1])
        cT = sb("cond_T", [128, KD, 32])
        wfd = sb("w_forget_dt", [128, KD, HB])
        wr = sb("w_router_sb", [128, KD, NE])
        pgs = sb("pages", [1, NS * NPG], I32)
        rs = sb("rstd", [128, 4, T])
        attT = sb("att_T", [128, KD, T])
        u = sb("conv_out", [128, NCB, T])
        xa = sb("conv_in", [128, 2, XW])
        cacc = sb("conv_sum", [128, 2, XO])
        tails = sb("conv_tails", [128, NCB, 27])
        yq = sb("y_T", [128, 4228])
        yT = yq[:, 0:NXB * T].rearrange("p (c t) -> p c t", c=NXB)
        fd = sb("dt_logf", [HB, T])
        acsT = sb("cums", [HB, NP])
        ex = sb("expand_in", [SH, 2 * NS + 1])
        tokc = sb("token_cols", [128, 7 * 32])
        lft = sb("logf_tok", [128, 3, NH])
        exo = sb("expanded", [128, NXB, 2 * NS + 1])
        sm2 = sb("small", [128, 64])
        fdw = sb("head_work", [HB, 3, T])
        mrow = sb("mod_rows", [128, SW])
        stT = sb("conv_states", [128, NCB, 24])
        zsS = sb("z_samples", [128, NXB, NS])
        ARENA = 14352
        ar = sb("arena", [128, ARENA])
        at = [0]

        def part(n):
            o = at[0]
            at[0] += n
            assert at[0] <= ARENA, at[0]
            return ar[:, o:o + n]

        qkT = part(12 * T).rearrange("p (c t) -> p c t", c=12)
        vtok = part(3 * KVW).rearrange("p (a f) -> p a f", a=3)
        kvf = part(4 * NPG * KVW)
        kvr = kvf.rearrange("p (s g f) -> p s g f", s=4, g=NPG)
        ktb = part(2 * 4 * 257).rearrange("p (s m k) -> p s m k", s=2, m=4)
        pbT = part(4 * 384)
        pb = pbT[:, 0:768].rearrange("p (s k) -> p s k", s=2)
        pT = pbT[:, 768:1536].rearrange("p (s k) -> p s k", s=2)
        vT = pbT[:, 0:4 * T].rearrange("p (c t) -> p c t", c=4)
        ps_s = part(257)
        psT = part(NPG * 144).rearrange("p (g k) -> p g k", g=NPG)
        pn = part(144)
        otok = part(KVW)
        ktok = otok
        lfc = part(NPG * 128).rearrange("p (g k) -> p g k", g=NPG)
        lfn = part(128)
        pnb = part(NS)
        qbd = yq
        xin = kvf[:, 0:3 * D].rearrange("p (a d) -> p a d", a=3)
        vrow = otok[:, 0:256].rearrange("p (a k) -> p a k", a=2)
        crow = ar[:, 0:D]
        csin = ar[:, D:D + CD]
        at[0] = 0
        xd = part(2 * DI).rearrange("p (a f) -> p a f", a=2)
        xef = part(2 * DI)
        xe = xef.rearrange("p (a f) -> p a f", a=2)
        late0 = at[0]
        btok = part(2 * SG * NST).rearrange("p (a f) -> p a f", a=2)
        s1T = part(DI)
        cbm = part(SG * 128).rearrange("p (g k) -> p g k", g=SG)
        wdf = part(2 * 512)
        wd = wdf.rearrange("p (s k) -> p s k", s=2)
        ce = part(2 * 512).rearrange("p (s k) -> p s k", s=2)
        ctok = xef[:, 0:512]
        zb = ring[:, 4 * SLOT:6 * SLOT].rearrange("p (c t) -> p c t", c=NXB)
        at[0] = 16 * T
        sst = part(2 * NXB * NST).rearrange("p (s k) -> p s k", s=2)
        bc = part(2 * 2 * SG * NST).rearrange("p (s k) -> p s k", s=2)
        prod = part(NXB * NST)
        gT = ar[:, 0:16 * T].rearrange("p (c t) -> p c t", c=16)
        mslot = [ar[:, 4224 + i * 4096:4224 + (i + 1) * 4096] for i in range(2)] + [yq[:, 0:4096]] + \
                [ring[:, i * 4096:(i + 1) * 4096] for i in range(3)]

        def blocks(a, n):
            return u[:].rearrange("p c t -> p (c t)")[:, a:a + n]

        h2tok = blocks(0, 3 * D).rearrange("p (a d) -> p a d", a=3)
        xg = blocks(3 * D, 2 * D).rearrange("p (k s) -> p k s", k=KD)
        outs = blocks(5 * D, D)
        sel = ar[:, 0:1536].rearrange("p (w a s) -> p w a s", w=2, a=3)
        selT = ar[:, 1536:1536 + 2 * T].rearrange("p (e t) -> p e t", e=2)
        hact = ar[:, 2080:2592]
        gact = ar[:, 2592:3104]
        aT = ar[:, 3104:3616].rearrange("p (k s) -> p k s", k=4)
        mr = ar[:, 4224 + 2 * 4096:ARENA]
        lgT = mr[:, 0:T]

        def rows3(o, n=NE):
            return mr[:, o:o + 3 * n].rearrange("p (a e) -> p a e", a=3)

        lg, cmb, asg, rank, prg = (rows3(264 + 48 * i) for i in range(5))
        rt = [rows3(504 + 12 * i, 4) for i in range(12)]
        rw = [mr[:, 648 + 4 * i:651 + 4 * i] for i in range(10)]
        cnt = mr[:, 688:688 + NE]
        asb = sb("assigned_bf", [128, 3, NE], BF16)
        rounds_sb = sb("rounds", [1, 1], I32)
        Y = attT
        yout = yq[:, 0:3 * D].rearrange("p (a d) -> p a d", a=3)

        banks = [ctx.enter_context(nc.psum_tensor(f"bank{i}", [128, 512], F32)) for i in range(8)]
        sbank = banks[7]

        jobs = [("cT",), ("vecs",), ("mod", 0), ("modt", 0)]
        jobs += [("xt", a, f) for a in range(3) for f in range(2)]
        jobs += [("ssq", 0), ("mod", 1), ("modt", 1), ("cst", 0), ("cst", 1), ("fd",)]
        jobs += [("k", i) for i in range(4)] + [("ft",)] + [("kn", i) for i in range(4)]
        jobs += [("q", i) for i in range(4)] + [("qn", i) for i in range(4)]
        jobs += [("q", i) for i in range(4, 8)] + [("qn", i) for i in range(4, 8)]
        jobs += [("v", i) for i in range(4)]
        jobs += [("kt", a) for a in range(3)] + [("vt", a) for a in range(3)]
        for c in range(8):
            jobs += [("s", c, 0), ("s", c, 1), ("xbc", 3 * c), ("sk", c, 0), ("sk", c, 1),
                     ("xbc", 3 * c + 1), ("ss", c), ("xbc", 3 * c + 2),
                     ("pt", c, 0), ("pt", c, 1), ("o2", c)]
        jobs += [("mod", 2), ("modt", 2), ("sp",), ("mod", 3), ("modt", 3)]
        jobs += [("so", 0), ("sx", 0)] + [("z", i) for i in range(4)] + [("so", 1), ("sx", 1)]
        for i in range(6):
            jobs += [("ct", i), ("z", 4 + i)]
        jobs += [("bs", 0), ("bs", 1), ("exp",)]
        jobs += [("bt", a) for a in range(2)]
        fill = {(0, 2): [("z", 10)], (0, 4): [("z", 11)], (0, 6): [("z", 12)], (1, 0): [("z", 13)], (1, 1): [("z", 14)],
                (1, 2): [("z", 15)], (1, 4): [("mod", 4), ("modt", 4)], (1, 6): [("mod", 5), ("modt", 5)]}
        for a in range(2):
            jobs += [("xs", a, g) for g in range(4)]
            if a == 1:
                jobs += [("s1", g) for g in range(4)]
            jobs += [("cb", a)]
            for b in range(8):
                jobs += [("ab", a, b)] + fill.get((a, b), [])
                if b >= 1:
                    jobs += [("y", a, b - 1)]
            jobs += [("y", a, 7)]
        jobs += [("fs", i) for i in range(4)]
        merge = [("g", i) for i in range(16)] + [("pa", i) for i in range(8)]
        for i, j in enumerate(merge):
            if i % 3 == 2:
                jobs += [("ssm", i // 3)]
            jobs += [j]
        jobs += [("yn", g) for g in range(SG)]
        jobs += [("pb", i) for i in range(8)] + [("o", i) for i in range(8)]
        jobs += [("ssq", 1), ("lr",), ("lt",)] + [("ht", a, f) for a in range(3) for f in range(2)] + [("rk",)]
        late = [("yt", a, f) for a in range(3) for f in range(2)]
        NOBANK = {"ss", "ssm"}

        bank_of, at_bank = {}, [0] * NBANK
        for n, j in enumerate([j for j in jobs + late if j[0] not in NOBANK]):
            b = n % NBANK
            at_bank[b] += 1
            bank_of[j] = (b, at_bank[b])
        at_moe = [0] * NBANK
        for j in jobs:
            if j in bank_of:
                at_moe[bank_of[j][0]] += 1
        bank_filled = [sem(f"bank_filled{i}") for i in range(NBANK)]
        bank_read = [sem(f"bank_read{i}") for i in range(NBANK)]

        def slots_of(j):
            k = j[0]
            if k == "mod":
                return [("mod", 4 * j[1] + i) for i in range(4)]
            if k in ("q", "k", "v", "xbc", "z", "g"):
                base = {"q": 0, "k": COL_K, "v": COL_V, "xbc": COL_X, "z": COL_Z, "g": COL_G}[k]
                return [("in", base + SW * (j[1] // 2))]
            if k in ("pa", "o"):
                return [(k, j[1] // 2)]
            if k == "pb":
                return [(k, j[1] // 2, 0), (k, j[1] // 2, 1)]
            return []

        loads, last_user = [], {}
        for j in jobs:
            for s in slots_of(j):
                if s not in last_user:
                    loads.append(s)
                last_user[s] = j
        narrow = range(jobs.index(("z", 0)), jobs.index(("y", 1, 7)) + 1)
        slot_at, slot_count, arrived_at, held_by, before = {}, [0] * NSLOT, {}, {}, {}
        z_over = {}
        order = list(range(NSLOT))
        for s in loads:
            user = min(i for i, j in enumerate(jobs) if s in slots_of(j))
            r = next(r for r in order if r < 4 or user not in narrow)
            order = [i for i in order if i != r] + [r]
            slot_count[r] += 16 * (4 if s[0] == "pa" else 4 if s[0] == "in" and s[1] < D else 1)
            slot_at[s], arrived_at[s] = r, slot_count[r]
            before[s] = held_by.get(r)
            if r >= 4 and user < narrow[0]:
                z_over[r] = s
            held_by[r] = s
        slot_full = [sem(f"slot_full{i}") for i in range(NSLOT)]

        def slot(s):
            r = slot_at[s]
            return ring[:, r * SLOT:(r + 1) * SLOT].rearrange("p (k n) -> p k n", k=KD)

        small_in = sem("conditions_and_vectors_landed")
        x_in = sem("x_landed")
        st_in = sem("conv_states_landed")
        late_in = sem("small_weights_landed")
        pt_in = sem("page_table_landed")
        lf_in = sem("cached_logf_landed")
        consts = sem("constants_built")
        cond_ready = sem("condition_silu_done")
        sq_ready = sem("x_squared")
        h_ready = sem("h_ready")
        fd_exp = sem("exp_of_head_logits")
        fd_sp = sem("dt_logf_and_sums_ready")
        fd_e = sem("head_decays_ready")
        lfn_ready = sem("new_logf_spread")
        qk_sq = sem("qk_squared")
        qk_ready = sem("qk_normed")
        qbd_zero = sem("sample_queries_zeroed")
        qbd_ready = sem("sample_queries_placed")
        s_max = sem("scores_and_max_ready")
        s_exp = sem("scores_exponentiated")
        p_ready = sem("probs_ready")
        kcol_ready = sem("new_key_placed")
        ss_done = sem("sample_scores_summed")
        ss_max = sem("sample_max_ready")
        ss_exp = sem("sample_scores_exponentiated")
        sp_ready = sem("sample_probs_ready")
        conv_ready = sem("conv_summed")
        u_ready = sem("conv_silu_done")
        bs_out = sem("sample_bc_rows_stored")
        xds_ready = sem("sample_x_dt_ready")
        xe_ready = sem("decayed_xd_ready")
        seg_exp = sem("segment_decays_ready")
        et_ready = sem("exp_of_sums_ready")
        w_ready = sem("weighted_cb_ready")
        ce_ready = sem("decayed_c_ready")
        zg_done = sem("z_gate_applied")
        y_sq = sem("y_squared")
        y_ready = sem("y_normed")
        m_ready = sem("branches_merged")
        bc_full = [sem(f"sample_bc_rows_landed{i}") for i in range(2)]
        st_dec = sem("state_decayed")
        st_new = sem("state_updated")
        st_prod = sem("state_times_c_ready")
        st_red = sem("state_times_c_summed")
        o_small = sem("small_outputs_stored")
        o_k = sem("k_stored")
        o_tail = sem("conv_states_stored")
        o_y = sem("y_stored")
        asg_ready = sem("assignment_ready")
        rk_exp = sem("router_exp_ready")
        rk_ready = sem("ranks_ready")
        rk_shift = sem("ranks_shifted")
        sel_ready = sem("selection_ready")
        gath_filled = sem("gathered_bank_filled")
        selT_done = sem("selection_transposed")
        selT_ready = sem("selection_T_copied")
        xg_ready = sem("gathered_copied")
        gate_done = sem("gate_product_done")
        up_done = sem("up_product_done")
        silu_ready = sem("gate_silu_ready")
        act_ready = sem("expert_act_ready")
        actT_done = sem("expert_act_transposed")
        actT_ready = sem("expert_act_T_copied")
        down_done = sem("down_product_done")
        out_ready = sem("expert_out_copied")
        comb_filled = sem("combined_bank_filled")
        comb_read = sem("combined_bank_read")
        yfin = sem("y_final_ready")
        y_zero = sem("expert_sum_zeroed")
        dve_step = sem("dve_step")
        act_step = sem("act_step")
        pool_step = sem("pool_step")
        kv_full = [sem(f"cache_page_landed{i}") for i in range(4)]
        st_full = [sem(f"state_landed{i}") for i in range(2)]
        st_out = [sem(f"state_stored{i}") for i in range(2)]
        o_fs = [sem(f"ssm_prompt_stored{i}") for i in range(2)]
        moe_full = [sem(f"expert_matrix_landed{i}") for i in range(6)]

        def stepper(eng, own):
            n = {}

            def link(ins, s=own):
                n[s.name] = n.get(s.name, 0) + 1
                ins.then_inc(s, 1)
                eng.wait_ge(s, n[s.name])
            return link

        def filled(eng, j):
            b, n = bank_of[j]
            eng.wait_ge(bank_filled[b], n)
            return banks[b]

        def release(eng, ins, j):
            b, n = bank_of[j]
            ins.then_inc(bank_read[b], 1)
            eng.wait_ge(bank_read[b], n)

        def read_out(eng, j):
            b, n = bank_of[j]
            eng.wait_ge(bank_read[b], n)

        wmod = t["w_mod"].rearrange("o (k p) n -> p (o k) n", p=128)
        win = t["w_in"].rearrange("o (k p) n -> p (o k) n", p=128)
        wpa = t["w_pa"].rearrange("o (m h s d) n -> (o h) s d m n", h=2, s=2, d=HD)
        wpb = t["w_pb"].rearrange("o (k p) n -> p (o k) n", p=128)
        wo = t["w_o"].rearrange("o (k p) n -> p (o k) n", p=128)
        wg = t["w_gate"].rearrange("o e (k p) n -> (o e) p k n", p=128)
        wu = t["w_up"].rearrange("o e (k p) n -> (o e) p k n", p=128)
        wdn = t["w_down"].rearrange("o e (k p) n -> (o e) p k n", p=128)
        ck = t["cache_k"].rearrange("o g k h d -> (o g) k (h d)")
        cv = t["cache_v"].rearrange("o g k h d -> (o g) k (h d)")
        clf = t["cache_logf"].rearrange("o g k h -> (o g) k h")
        st_d = t["state_ssm"].rearrange("o b (c h) p n -> (o b) (h p) c n", h=2)
        so_d = t["ssm_sample"].rearrange("o b (c h) p n -> (o b) (h p) c n", h=2)
        fs_d = t["ssm_prompt"].rearrange("o b (c h) p n -> (o b) (h p) c n", h=2)
        bc_d = t["bc_scratch"]

        block = ctx.enter_context(nc.Block())

        @block.sync
        def _(sp):
            for s in loads:
                if before[s]:
                    b, use = bank_of[last_user[before[s]]]
                    sp.wait_ge(bank_filled[b], use)
                    if z_over.get(slot_at[s]) == before[s]:
                        sp.wait_ge(zg_done, NXB // 2)
                r, dst, c0 = slot_at[s], slot(s), SW * s[1]
                if s[0] == "mod":
                    sp.dma_start(dst, wmod[:, :, c0:c0 + SW]).then_inc(slot_full[r], 16)
                elif s[0] == "in" and s[1] < D:
                    for q in range(2):
                        for h in range(2):
                            o, c = HD * (2 * q + h), s[1] + HD * (2 * h + q)
                            sp.dma_start(dst[:, :, o:o + HD], win[:, :, c:c + HD]).then_inc(slot_full[r], 16)
                elif s[0] == "in":
                    sp.dma_start(dst, win[:, :, s[1]:s[1] + SW]).then_inc(slot_full[r], 16)
                elif s[0] == "o":
                    sp.dma_start(dst, wo[:, :, c0:c0 + SW]).then_inc(slot_full[r], 16)
                elif s[0] == "pb":
                    sp.dma_start(dst, wpb[:, KD * s[2]:KD * s[2] + KD, c0:c0 + SW]).then_inc(slot_full[r], 16)
                else:
                    dv = dst.rearrange("p (m s) n -> p s m n", s=2)
                    for h in range(2):
                        for q in range(2):
                            sp.dma_start(dv[64 * h:64 * h + 64, q], wpa[h, q, :, :, c0:c0 + SW])\
                              .then_inc(slot_full[r], 16)

            def experts(it, j):
                for i, w in enumerate((wg, wu, wdn)):
                    if it is not None:
                        sp.wait_ge((gate_done, up_done, down_done)[i], it * 2 + 1 if i == 2 else it + 1)
                    else:
                        if i == 0:
                            for q in range(2):
                                sp.wait_ge(st_out[q], 16 * (NS // 2))
                                sp.wait_ge(o_fs[q], 32)
                            sp.wait_ge(y_sq, 1)
                        bk, use = bank_of[("pb" if i == 1 else "o", 7)]
                        if i:
                            sp.wait_ge(bank_filled[bk], use)
                    for e in range(2):
                        s = 2 * i + e
                        if it is None and s == 3:
                            bk, use = bank_of[("o", 7)]
                            sp.wait_ge(bank_filled[bk], use)
                        sp.dma_start(mslot[s].rearrange("p (k n) -> p k n", k=KD if i < 2 else FF // 128),
                                     w[2 * j + e]).then_inc(moe_full[s], 16)

            experts(None, 0)
            with sp.Fori(1, NE // 2) as j:
                experts(j, j)
            sp.wait_ge(rk_ready, 1)
            rounds = sp.value_load(rounds_sb[0:1, 0:1], min_val=1, max_val=5)
            with sp.If(rounds > 1):
                with sp.Fori(1, rounds) as r:
                    with sp.Fori(0, NE // 2) as j:
                        experts(r * 8 + j, j)
            for a, (t0, n) in enumerate(TOK):
                read_out(sp, ("yt", a, 1))
                if a < 2:
                    dst = t["y_prompt"].rearrange("o q d -> (o q) d")[t0:t0 + n, :]
                else:
                    dst = t["y_sample"].rearrange("b o d -> (b o) d")
                sp.dma_start(dst, yout[0:n, a, :]).then_inc(o_y, 16)
            sp.wait_ge(o_y, 48)
            sp.wait_ge(o_small, 16 * 5)
            sp.wait_ge(o_k, 48)
            sp.wait_ge(o_tail, 16 * 12)

        @block.gpsimd
        def _(pool):
            link = stepper(pool, pool_step)
            g = nc.gpsimd
            link(g.memset(ident[:], 0.0))
            link(g.affine_select(out=ident[:], in_=ident[:], compare_op=ALU.not_equal, fill=1.0, base=0,
                                 pattern=[[-1, 128]], channel_multiplier=1), consts)
            link(g.memset(cT[:], 0.0), consts)
            link(g.memset(onesf[:], 1.0))
            link(g.memset(epsc[:], EPS))
            link(g.memset(blk[:], 0.0))
            link(g.memset(blk[0:64, 0:64], 1.0))
            link(g.memset(blk[64:128, 64:128], 1.0), consts)
            link(g.memset(qbd[:], 0.0), qbd_zero)
            link(g.memset(ntri[:], -1.0))
            link(g.affine_select(out=ntri[:], in_=ntri[:], compare_op=ALU.is_ge, fill=0.0, base=-128,
                                 pattern=[[1, 385]], channel_multiplier=-1))
            link(g.memset(cmask[:], 0.0))
            for o in (0, 256):
                link(g.affine_select(out=cmask[:, o:o + 128], in_=cmask[:, o:o + 128], compare_op=ALU.is_ge,
                                     fill=-1e30, base=0, pattern=[[-1, 128]], channel_multiplier=1))
            link(g.affine_select(out=triu[:], in_=onesf[:], compare_op=ALU.is_ge, fill=0.0, base=0,
                                 pattern=[[1, 128]], channel_multiplier=-1))
            link(g.affine_select(out=bm8[:].rearrange("p (b h) -> p b h", h=NH),
                                 in_=onesf[0:NS, :].rearrange("p (b h) -> p b h", h=NH),
                                 compare_op=ALU.is_equal, fill=0.0, base=0,
                                 pattern=[[1, NS], [0, NH]], channel_multiplier=-1))
            link(g.affine_select(out=bm2[:], in_=onesf[:, 0:NS], compare_op=ALU.is_ge, fill=0.0, base=0,
                                 pattern=[[-NH, NS]], channel_multiplier=1))
            link(g.affine_select(out=bm2[:], in_=bm2[:], compare_op=ALU.is_ge, fill=0.0, base=NH - 1,
                                 pattern=[[NH, NS]], channel_multiplier=-1))
            link(g.memset(onesb[:], 1.0))
            link(g.affine_select(out=striu[:], in_=onesb[:], compare_op=ALU.is_ge, fill=0.0, base=-1,
                                 pattern=[[1, 128]], channel_multiplier=-1))
            link(g.iota(iota[:], pattern=[[1, BLK]], base=0, channel_multiplier=0,
                        allow_small_or_imprecise_dtypes=True))
            link(g.iota(w4[:], pattern=[[-1, 4]], base=4, channel_multiplier=0,
                        allow_small_or_imprecise_dtypes=True))
            link(g.iota(thr[:], pattern=[[BLK, 4]], base=BLK, channel_multiplier=0,
                        allow_small_or_imprecise_dtypes=True))
            link(g.memset(vm[:], 1.0))
            link(g.affine_select(out=vm[:, 2:3], in_=vm[:, 2:3], compare_op=ALU.is_ge, fill=0.0, base=NS - 1,
                                 pattern=[[0, 1]], channel_multiplier=-1))
            link(g.memset(xa[:, :, 0:3], 0.0))
            link(g.memset(psT[:], 0.0))
            link(g.memset(pn[:], 0.0), consts)

            pool.wait_ge(pt_in, 16)

            def page(i):
                return pool.value_load(pgs[0:1, bass.ds(i, 1)], min_val=0, max_val=ck.shape[0] - 1)

            with pool.Fori(0, NS) as b:
                for q in range(NPG):
                    pool.dma_start(lfc[:, q, bass.ds(b * NH, NH)], clf[page(b * NPG + q)]).then_inc(lf_in, 16)
            bk, use = bank_of[("xt", 2, 1)]
            pool.wait_ge(bank_filled[bk], use)
            for kind, cache in enumerate((ck, cv)):
                for b in range(NS):
                    if kind == 1 or b >= 4:
                        bk, use = bank_of[("sk", b - 4, 1) if kind == 0 else ("sk", b + 4, 1) if b < 4 else ("so", 0)]
                        pool.wait_ge(bank_filled[bk], use)
                    with pool.Fori(0, NPG) as q:
                        pool.dma_start(kvr[:, b % 4, bass.ds(q, 1), :].rearrange("p o f -> p (o f)"),
                                       cache[page(q + b * NPG)]).then_inc(kv_full[b % 4], 16)

            for a in range(2):
                read_out(pool, ("xs", a, 3))
                if a == 0:
                    pool.wait_ge(o_tail, 16 * 12)
                e = tokc[:, (4 + a) * 32:(5 + a) * 32]
                link(g.tensor_tensor(xe[:, a, :].rearrange("p (h d) -> p h d", d=HD),
                                     xd[:, a, :].rearrange("p (h d) -> p h d", d=HD),
                                     e.unsqueeze(2).to_broadcast([128, SH, HD]), ALU.mult), xe_ready)
            bk, use = bank_of[("s1", 3)]
            pool.wait_ge(bank_filled[bk], use)
            x3 = xe[:, 0, :].rearrange("p (h d) -> p h d", d=HD)
            link(g.tensor_tensor(x3, x3, tokc[:, 192:224].unsqueeze(2).to_broadcast([128, SH, HD]), ALU.mult), xe_ready)
            for b in range(8):
                pool.wait_ge(et_ready, b + 1)
                c3 = ce[:, b % 2, :].rearrange("p (h k) -> p h k", h=4)
                cv3 = u[:, 20 + b // 2, 128:256].unsqueeze(1).to_broadcast([128, 4, 128])
                link(g.tensor_tensor(c3, c3, cv3, ALU.mult), ce_ready)

            bk, use = bank_of[("fs", 3)]
            pool.wait_ge(bank_filled[bk], use)
            for i in range(2):
                pool.wait_ge(o_fs[i], 32)
            pool.wait_ge(bs_out, 16)
            pool.wait_ge(xds_ready, 1)

            def load_state(b):
                if b >= 2:
                    pool.wait_ge(st_out[b % 2], 16 * (b // 2))
                    pool.wait_ge(st_prod, b - 1)
                pool.dma_start(sst[:, b % 2, :].rearrange("p (c n) -> p c n", c=NXB), st_d[b]).then_inc(st_full[b % 2], 16)
                pool.dma_start(bc[:, b % 2, :], bc_d[b:b + 1, :].to_broadcast([128, 2 * SG * NST]))\
                    .then_inc(bc_full[b % 2], 16)

            load_state(0)
            load_state(1)
            for b in range(NS):
                pool.wait_ge(st_new, b + 1)
                pool.dma_start(so_d[b], sst[:, b % 2, :].rearrange("p (c n) -> p c n", c=NXB)).then_inc(st_out[b % 2], 16)
                if b:
                    pool.wait_ge(st_red, b)
                s4 = sst[:, b % 2, :].rearrange("p (g c n) -> p g c n", g=SG, c=4)
                p4 = prod.rearrange("p (g c n) -> p g c n", g=SG, c=4)
                for q in range(SG):
                    cr = bc[:, b % 2, (SG + q) * NST:(SG + q + 1) * NST]
                    ins = g.tensor_tensor(p4[:, q], s4[:, q], cr.unsqueeze(1).to_broadcast([128, 4, NST]), ALU.mult)
                ins.then_inc(st_prod, 1)
                if b + 2 < NS:
                    load_state(b + 2)
            bk, use = bank_of[("pa", 7)]
            pool.wait_ge(bank_filled[bk], use)
            g.memset(Y[:], 0.0).then_inc(y_zero, 1)

        @block.scalar
        def _(act):
            link = stepper(act, act_step)
            fn = nc.scalar.activation
            act.sem_inc(silu_ready, 1)
            act.dma_start(crow[0:NS, :], t["c_sample"]).then_inc(small_in, 16)
            act.dma_start(crow[NS:NC, :], t["c_prompt"]).then_inc(small_in, 16)
            o = 0
            for name, n in (("b_mod", 48), ("g_norm1", 8), ("g_norm2", 8), ("g_ssm", 16), ("conv_b", 24)):
                act.dma_start(vrow[o:o + n, 0, :], t[name].rearrange("o (k p) -> (o k) p", p=128)).then_inc(small_in, 16)
                o += n
            act.dma_start(vrow[0:96, 1, :], t["conv_w"].rearrange("o w (k p) -> (o w k) p", p=128)).then_inc(small_in, 16)
            xp = t["x_prompt"].rearrange("o q d -> (o q) d")
            act.dma_start(xin[:, 0, :], xp[0:128, :]).then_inc(x_in, 16)
            act.dma_start(xin[:, 1, :], xp[128:256, :]).then_inc(x_in, 16)
            act.dma_start(xin[0:NS, 2, :], t["x_sample"].rearrange("b o d -> (b o) d")).then_inc(x_in, 16)
            act.dma_start(csin[0:24, :], t["state_conv"].rearrange("o b w c -> (o b w) c")).then_inc(st_in, 16)
            act.dma_start(pgs[:], t["page_table"].rearrange("(o b) g -> o (b g)", o=1)).then_inc(pt_in, 16)
            act.dma_start(wfd[:, :, 0:SH], win[:, :, COL_DT:COL_DT + SH]).then_inc(late_in, 16)
            act.dma_start(wfd[:, :, SH:HB], win[:, :, COL_F:COL_F + NH]).then_inc(late_in, 16)
            act.dma_start(wr[:], t["w_router"].rearrange("(k p) e -> p k e", p=128)).then_inc(late_in, 16)
            for h in range(2):
                act.dma_start(gqk[64 * h:64 * h + 64, 0:1], t["g_q"].rearrange("o d -> d o")).then_inc(late_in, 16)
                act.dma_start(gqk[64 * h:64 * h + 64, 1:2], t["g_k"].rearrange("o d -> d o")).then_inc(late_in, 16)
            act.dma_start(hcol[0:SH, 0:1], t["dt_bias"].rearrange("o d -> d o")).then_inc(late_in, 16)
            act.dma_start(hcol[SH:HB, 0:1], t["b_f"].rearrange("o d -> d o")).then_inc(late_in, 16)
            act.dma_start(hcol[0:SH, 1:2], t["a_log"].rearrange("o d -> d o")).then_inc(late_in, 16)
            act.dma_start(hcol[0:SH, 2:3], t["d_skip"].rearrange("o d -> d o")).then_inc(late_in, 16)
            act.dma_start(brow[:], t["b_router"].rearrange("(d o) -> d o", o=1)).then_inc(late_in, 16)
            act.wait_ge(small_in, 16 * 8)
            link(fn(crow[0:NC, :], crow[0:NC, :], ACT.Silu), cond_ready)

            def conv_silu(i):
                act.wait_ge(conv_ready, i + 1)
                link(fn(u[:, i, 0:NP], cacc[:, i % 2, 0:NP], ACT.Silu))
                link(fn(u[:, i, NP:T], cacc[:, i % 2, NP + 3:XO:4], ACT.Silu), u_ready)

            for j in jobs:
                k = j[0]
                if k == "sp":
                    act.wait_ge(ss_max, 1)
                    link(fn(ps_s, sbank[:, 0:257], ACT.Exp, bias=sm2[:, 8:9], accum_out=sm2[:, 9:10]), ss_exp)
                if k == "lt":
                    act.wait_ge(asg_ready, 1)
                    link(fn(lg, lg, ACT.Exp), rk_exp)
                ps = filled(act, j) if k in ("mod", "ssq", "q", "k", "qn", "kn", "v", "kt", "vt", "pt", "o2", "xbc",
                                             "sk", "sp", "so", "ct", "bs", "bt", "s1", "fs", "z", "g", "yn",
                                             "ht") else None
                if k == "mod":
                    if j[1] == 2:
                        conv_silu(NCB - 1)
                    release(act, fn(mrow[:], ps[:, 0:SW], ACT.Copy), j)
                elif k == "ssq":
                    act.wait_ge(consts, 3)
                    release(act, fn(rs[:, 0, :], ps[:, 0:T], ACT.Sqrt, bias=epsc[:], scale=1.0 / D), j)
                elif k == "fd":
                    read_out(act, j)
                    link(fn(fdw[:, 0, :], fd[:], ACT.Abs))
                    link(fn(hcol[0:SH, 1:2], hcol[0:SH, 1:2], ACT.Exp))
                    link(fn(fdw[:, 0, :], fdw[:, 0, :], ACT.Exp, scale=-1.0), fd_exp)
                    act.wait_ge(fd_sp, 1)
                    for c in range(2):
                        cols = slice(128 * c, 128 * c + 128)
                        link(fn(fdw[0:SH, 1, cols], acsT[0:SH, cols], ACT.Exp,
                                bias=acsT[0:SH, 128 * c + 127:128 * c + 128], scale=-1.0))
                    link(fn(fdw[0:SH, 2, 0:128], fdw[0:SH, 2, 0:128], ACT.Exp))
                    link(fn(ex[:, NS:2 * NS], ex[:, NS:2 * NS], ACT.Exp), fd_e)
                elif k == "ft":
                    read_out(act, j)
                    act.dma_start(t["logf_prompt"].rearrange("o b (a p) h -> p (o b a) h", p=128),
                                  lft[:, 0:2, :]).then_inc(o_small, 16)
                    act.dma_start(t["logf_sample"].rearrange("o b q h -> (o b q) h"), lft[0:NS, 2, :])\
                       .then_inc(o_small, 16)
                elif k in ("q", "k"):
                    release(act, fn(qkT[:, j[1] + (8 if k == "k" else 0), :], ps[:, 0:T], ACT.Copy), j)
                elif k in ("qn", "kn"):
                    if k == "qn":
                        act.wait_ge(qk_ready, 1 + j[1] // 4)
                    release(act, fn(rs[:, j[1] % 4, :], ps[:, 0:T], ACT.Sqrt, bias=epsc[:], scale=1.0 / HD), j)
                elif k == "v":
                    release(act, fn(vT[:, j[1], :], ps[:, 0:T], ACT.Copy), j)
                elif k in ("kt", "vt"):
                    a, (t0, n) = j[1], TOK[j[1]]
                    o, kind = (ktok[0:n, :], "k") if k == "kt" else (vtok[0:n, a, :], "v")
                    if k == "kt" and a:
                        act.wait_ge(o_k, 16 * a)
                    release(act, fn(o, ps[0:n, :], ACT.Copy), j)
                    dst = t[f"{kind}_prompt" if a < 2 else f"{kind}_sample"].rearrange("o b q h d -> (o b q) (h d)")
                    act.dma_start(dst[t0:t0 + n, :] if a < 2 else dst, o).then_inc(o_k if k == "kt" else o_small, 16)
                elif k == "s":
                    p = j[2]
                    act.wait_ge(s_max, 2 * j[1] + p + 1)
                    for q, (lo, hi) in enumerate(((0, 128), (128, 384))):
                        link(fn(pb[:, p, lo:hi], pb[:, p, lo:hi], ACT.Exp, bias=sm2[:, 4 * p + q:4 * p + q + 1],
                                accum_out=sm2[:, 4 * p + 2 + q:4 * p + 3 + q]), s_exp if q else act_step)
                elif k == "pt":
                    release(act, fn(pT[:, j[2], :], ps[:, 0:384], ACT.Copy), j)
                elif k == "o2":
                    release(act, fn(attT[:, j[1], 0:NP], ps[:, 0:NP], ACT.Copy), j)
                elif k == "xbc":
                    i = j[1]
                    if i >= 2:
                        act.wait_ge(conv_ready, i - 1)
                    link(fn(xa[:, i % 2, 3:3 + NP], ps[:, 0:NP], ACT.Copy))
                    release(act, fn(xa[:, i % 2, 3 + NP + 3:XW:4], ps[:, NP:T], ACT.Copy), j)
                    if i:
                        conv_silu(i - 1)
                elif k == "sk":
                    b, q = j[1], j[2]
                    release(act, fn(ktb[:, b % 2, :, 128 * q:128 * q + 128],
                                    ps.rearrange("p (m k) -> p m k", m=4), ACT.Copy), j)
                elif k == "sp":
                    for q in range(NPG):
                        link(fn(psT[:, q, 0:128], ps[:, 128 * q:128 * q + 128], ACT.Copy))
                    release(act, fn(pn[0:NS, 0:128], ps[0:NS, 256:384], ACT.Copy), j)
                elif k == "so":
                    act.wait_ge(o_k, 48)
                    release(act, fn(otok[:], ps[:], ACT.Copy), j)
                elif k == "ct":
                    i = j[1]
                    act.wait_ge(*((o_tail, 32 * i) if i else (o_small, 16 * 5)))
                    release(act, fn(ctok[0:27, :], ps[0:27, :], ACT.Copy), j)
                    act.dma_start(t["conv_sample"].rearrange("o b w c -> (o b w) c")[:, 512 * i:512 * i + 512],
                                  ctok[0:24, :]).then_inc(o_tail, 16)
                    act.dma_start(t["conv_prompt"].rearrange("o b w c -> (o b w) c")[:, 512 * i:512 * i + 512],
                                  ctok[24:27, :]).then_inc(o_tail, 16)
                elif k == "bs":
                    release(act, fn(wdf[0:NS, 512 * j[1]:512 * j[1] + 512], ps[0:NS, :], ACT.Copy), j)
                    if j[1]:
                        act.dma_start(bc_d, wdf[0:NS, :]).then_inc(bs_out, 16)
                elif k == "bt":
                    release(act, fn(btok[:, j[1], :], ps[:], ACT.Copy), j)
                elif k == "s1":
                    release(act, fn(s1T[:, 512 * j[1]:512 * j[1] + 512], ps[:], ACT.Copy), j)
                elif k == "ab":
                    a, b = j[1], j[2]
                    if a == 1:
                        filled(act, j)
                        if b >= 2:
                            filled(act, ("y", 1, b - 2))
                        link(fn(ce[:, b % 2, :], banks[bank_of[j][0]][:], ACT.Exp), et_ready)
                    read_out(act, j)
                    link(fn(wd[:, b % 2, :], wd[:, b % 2, :], ACT.Exp), seg_exp)
                elif k == "fs":
                    i = j[1]
                    if i >= 2:
                        act.wait_ge(o_fs[i % 2], 16)
                    release(act, fn(wd[:, i % 2, :], ps[:], ACT.Copy), j)
                    act.dma_start(fs_d[0, :, 4 * i:4 * i + 4, :], wd[:, i % 2, :].rearrange("p (c n) -> p c n", c=4))\
                       .then_inc(o_fs[i % 2], 16)
                elif k == "z":
                    i = j[1]
                    if i == 0:
                        for w in z_over.values():
                            filled(act, last_user[w])
                    link(fn(zb[:, i, :], ps[:, 0:NP], ACT.Silu))
                    release(act, fn(zsS[:, i, :], ps[:, NP:T], ACT.Silu), j)
                elif k == "ssm":
                    b = j[1]
                    act.wait_ge(st_full[b % 2], 16 * (b // 2 + 1))
                    for c in range(NXB):
                        x = sst[:, b % 2, NST * c:NST * c + NST]
                        ins = fn(x, x, ACT.Copy, scale=exo[:, c, NS + b:NS + b + 1])
                    link(ins, st_dec)
                elif k == "g":
                    release(act, fn(gT[:, j[1], :], ps[:, 0:T], ACT.Sigmoid), j)
                elif k == "yn":
                    release(act, fn(rs[:, j[1], :], ps[:, 0:T], ACT.Sqrt, bias=epsc[:], scale=SG / DI), j)
                elif k == "ht":
                    a, f, n = j[1], j[2], TOK[j[1]][1]
                    release(act, fn(h2tok[0:n, a, 512 * f:512 * f + 512], ps[0:n, :], ACT.Copy), j)

            def pair(it, t, p):
                act.wait_ge(gate_done, it + 2)
                act.wait_ge(act_ready, it + 1)
                fn(gact, banks[0][:], ACT.Silu).then_inc(silu_ready, 1)
                if p == 0:
                    act.wait_ge(selT_done, t + 2)
                    fn(selT[:, 0, :], banks[2][:, 0:T], ACT.Copy)
                    fn(selT[:, 1, :], banks[3][:, 0:T], ACT.Copy).then_inc(selT_ready, 1)
                act.wait_ge(actT_done, it + 1)
                fn(aT.rearrange("p k s -> p (k s)"), banks[4][:], ACT.Copy).then_inc(actT_ready, 1)
                for q in range(2):
                    act.wait_ge(down_done, it * 2 + (q + 2))
                    fn(outs[:, 512 * q:512 * q + 512], banks[2 + q][:], ACT.Copy).then_inc(out_ready, 1)

            act.wait_ge(rk_ready, 1)
            rounds = act.value_load(rounds_sb[0:1, 0:1], min_val=1, max_val=5)
            with act.Fori(0, rounds) as r:
                with act.Fori(0, NE // 4) as q:
                    for p in range(2):
                        pair(r * 8 + (q * 2 + p), r * 4 + q, p)
            for j in late:
                ps, (a, f), n = filled(act, j), j[1:], TOK[j[1]][1]
                release(act, fn(yout[0:n, a, 512 * f:512 * f + 512], ps[0:n, :], ACT.Copy), j)

        @block.vector
        def _(dve):
            link = stepper(dve, dve_step)
            v = nc.vector
            for s in (act_ready, comb_read, rk_shift):
                dve.sem_inc(s, 1)
            dve.sem_inc(xg_ready, 2)
            norm_of = ((48, 8, 0), (56, 32, 24))

            def squares(i):
                link(v.tensor_tensor(u[:, 0:KD, :], xT[:], xT[:], ALU.mult), sq_ready)

            def normed(i):
                gv, sc, sh = norm_of[i]
                link(v.reciprocal(rs[:, 0, :], rs[:, 0, :]))
                link(v.tensor_tensor(u[:, 0:KD, :], xT[:], rs[:, 0:1, :].to_broadcast([128, KD, T]), ALU.mult))
                link(v.scalar_tensor_tensor(gsc[:], modT[:, sc:sc + KD, :], 1.0,
                                            vec[:, gv:gv + KD].unsqueeze(2).to_broadcast([128, KD, NC]),
                                            ALU.add, ALU.mult))
                for c in range(KD):
                    v.tensor_scalar(hT[:, c, 0:NP], u[:, c, 0:NP], gsc[:, c, NS:NC], modT[:, sh + c, NS:NC],
                                    ALU.mult, ALU.add)
                link(v.tensor_tensor(hT[:, :, NP:T], u[:, 0:KD, NP:T], gsc[:, :, 0:NS], ALU.mult))
                link(v.tensor_tensor(hT[:, :, NP:T], hT[:, :, NP:T], modT[:, sh:sh + KD, 0:NS], ALU.add), h_ready)

            def weigh(a, b):
                dve.wait_ge(seg_exp, 8 * a + b + 1)
                w3 = wd[:, b % 2, :].rearrange("p (h k) -> p h k", h=4)
                link(v.tensor_tensor(w3, w3, cbm[:, b // 2:b // 2 + 1, :].to_broadcast([128, 4, 128]), ALU.mult), w_ready)

            def state_sum(b):
                dve.wait_ge(st_prod, b + 1)
                link(v.tensor_reduce(yT[:, :, NP + b], prod.rearrange("p (c n) -> p c n", c=NXB), AX.X, ALU.add), st_red)

            def first_max(src, m, best, tmp):
                m3 = m.unsqueeze(2).to_broadcast([128, 3, 4])
                link(v.tensor_reduce(m, src, AX.X, ALU.max))
                link(v.tensor_tensor(best, src, m3, ALU.is_equal))
                link(v.tensor_tensor(best, best, w4[:].unsqueeze(1).to_broadcast([128, 3, 4]), ALU.mult))
                link(v.tensor_reduce(tmp, best, AX.X, ALU.max))
                link(v.tensor_tensor(best, best, tmp.unsqueeze(2).to_broadcast([128, 3, 4]), ALU.is_equal))

            def route():
                m16 = rw[0].unsqueeze(2).to_broadcast([128, 3, NE])
                link(v.tensor_reduce(rw[0], lg, AX.X, ALU.max))
                link(v.tensor_tensor(lg, lg, m16, ALU.subtract), asg_ready)
                dve.wait_ge(rk_exp, 1)
                link(v.tensor_reduce(rw[1], lg, AX.X, ALU.add))
                link(v.reciprocal(rw[1], rw[1]))
                link(v.tensor_tensor(lg, lg, rw[1].unsqueeze(2).to_broadcast([128, 3, NE]), ALU.mult))
                lg4 = lg.rearrange("p a (g e) -> p a g e", g=NG)
                gm, og, pin, o1, o2, we = rt[0], rt[1], rt[2], rt[3], rt[4], rt[5]
                link(v.tensor_reduce(gm, lg4, AX.X, ALU.max))
                first_max(gm, rw[2], og, rw[3])
                pg4 = prg.rearrange("p a (g e) -> p a g e", g=NG)
                og4 = og.unsqueeze(3).to_broadcast([128, 3, NG, EPG])
                link(v.tensor_tensor(pg4, lg4, og4, ALU.mult))
                link(v.tensor_reduce(pin, prg.rearrange("p a (g e) -> p a e g", g=NG), AX.X, ALU.add))
                first_max(pin, rw[4], o1, rw[3])
                link(v.scalar_tensor_tensor(pin, o1, -4.0, pin, ALU.mult, ALU.add))
                first_max(pin, rw[5], o2, rw[3])
                link(v.tensor_tensor(rw[6], rw[4], rw[5], ALU.add))
                link(v.reciprocal(rw[6], rw[6]))
                link(v.tensor_tensor(rw[4], rw[4], rw[6], ALU.mult))
                link(v.tensor_tensor(rw[5], rw[5], rw[6], ALU.mult))
                link(v.tensor_tensor(we, o1, rw[4].unsqueeze(2).to_broadcast([128, 3, 4]), ALU.mult))
                link(v.tensor_tensor(pin, o2, rw[5].unsqueeze(2).to_broadcast([128, 3, 4]), ALU.mult))
                link(v.tensor_tensor(we, we, pin, ALU.add))
                link(v.tensor_tensor(o1, o1, o2, ALU.add))
                link(v.tensor_tensor(o1, o1, vm[:].unsqueeze(2).to_broadcast([128, 3, 4]), ALU.mult))
                link(v.tensor_tensor(we, we, vm[:].unsqueeze(2).to_broadcast([128, 3, 4]), ALU.mult))
                for dst, e4 in ((cmb, we), (asg, o1)):
                    for a in range(3):
                        link(v.tensor_tensor(dst[:, a, :].rearrange("p (g e) -> p g e", g=NG),
                                             og[:, a, :].unsqueeze(2).to_broadcast([128, NG, EPG]),
                                             e4[:, a, :].unsqueeze(1).to_broadcast([128, NG, EPG]), ALU.mult))
                link(v.tensor_copy(asb[:], asg), asg_ready)

            for j in jobs:
                k = j[0]
                if k == "cT":
                    ps = filled(dve, j)
                    dve.wait_ge(consts, 2)
                    release(dve, v.tensor_copy(cT[:, :, 0:NC], ps[:, 0:KD * NC].rearrange("p (k c) -> p k c", k=KD)), j)
                elif k == "vecs":
                    ps = filled(dve, j)
                    release(dve, v.tensor_copy(vec[:], ps[:, 0:200]), j)
                elif k == "modt":
                    ps, o = filled(dve, j), KD * j[1]
                    for q in range(2):
                        ins = v.tensor_tensor(modT[:, o + q:o + KD:2, :],
                                              ps[:, 128 * q:128 * q + 128].rearrange("p (i c) -> p i c", i=4)[:, :, 0:NC],
                                              vec[:, o + q:o + KD:2].unsqueeze(2).to_broadcast([128, 4, NC]), ALU.add)
                        if q:
                            release(dve, ins, j)
                        else:
                            link(ins)
                    if j[1] == 1:
                        normed(0)
                elif k == "xt":
                    ps, a, f, (t0, n) = filled(dve, j), j[1], j[2], TOK[j[1]]
                    release(dve, v.tensor_copy(xT[:, 4 * f:4 * f + 4, t0:t0 + n],
                                               ps[:, 0:4 * n].rearrange("p (q t) -> p q t", q=4)), j)
                    if a == 2 and f == 1:
                        squares(0)
                elif k == "ssq":
                    read_out(dve, j)
                    if j[1] == 1:
                        normed(1)
                elif k == "cst":
                    ps = filled(dve, j)
                    release(dve, v.tensor_copy(stT[:, 12 * j[1]:12 * j[1] + 12, :],
                                               ps[:, 0:288].rearrange("p (c s) -> p c s", c=12)), j)
                elif k == "fd":
                    ps = filled(dve, j)
                    dve.wait_ge(late_in, 16 * 12)
                    w0, w1, w2 = fdw[:, 0, :], fdw[:, 1, :], fdw[:, 2, :]
                    release(dve, v.tensor_scalar(fd[:], ps[0:HB, 0:T], hcol[:, 0:1], None, ALU.add), j)
                    link(v.tensor_scalar(gqk[:, 0:1], gqk[:, 0:1], HD ** -0.5, None, ALU.mult))
                    link(v.tensor_scalar(nident[:], ident[0:HB, 0:HB], -1.0, None, ALU.mult))
                    dve.wait_ge(fd_exp, 1)
                    link(v.tensor_scalar(w1, w0, 2.0, None, ALU.add))
                    link(v.reciprocal(w1, w1))
                    link(v.tensor_tensor(w0, w0, w1, ALU.mult))
                    link(v.tensor_tensor(w1, w0, w0, ALU.mult))
                    link(v.tensor_scalar(w2, w1, 1.0 / 15, None, ALU.mult))
                    for c in (13, 11, 9, 7, 5, 3):
                        link(v.scalar_tensor_tensor(w2, w2, 1.0 / c, w1, ALU.add, ALU.mult))
                    link(v.scalar_tensor_tensor(w2, w2, 1.0, w0, ALU.add, ALU.mult))
                    link(v.tensor_scalar(w1[0:SH], fd[0:SH, :], 0.0, None, ALU.max))
                    link(v.scalar_tensor_tensor(fd[0:SH, :], w2[0:SH], 2.0, w1[0:SH], ALU.mult, ALU.add))
                    link(v.tensor_scalar(w1[SH:HB], fd[SH:HB, :], 0.0, None, ALU.min))
                    link(v.scalar_tensor_tensor(fd[SH:HB, :], w2[SH:HB], -2.0, w1[SH:HB], ALU.mult, ALU.add))
                    link(v.tensor_scalar(hcol[0:SH, 1:2], hcol[0:SH, 1:2], -1.0, None, ALU.mult))
                    link(v.tensor_scalar(w0[0:SH], fd[0:SH, :], hcol[0:SH, 1:2], None, ALU.mult))
                    for c in range(2):
                        cols = slice(128 * c, 128 * c + 128)
                        link(v.tensor_tensor_scan(acsT[0:SH, cols], onesf[0:SH, :], w0[0:SH, cols], 0.0,
                                                  ALU.mult, ALU.add))
                        link(v.tensor_tensor_scan(acsT[SH:HB, cols], onesf[SH:HB, :], fd[SH:HB, cols],
                                                  acsT[SH:HB, 127:128] if c else 0.0, ALU.mult, ALU.add))
                    link(v.tensor_scalar(w2[0:SH, 0:128], onesf[0:SH, :], acsT[0:SH, 255:256], None, ALU.mult))
                    link(v.tensor_copy(ex[:, 0:NS], fd[0:SH, NP:T]))
                    link(v.tensor_copy(ex[:, 2 * NS:2 * NS + 1], hcol[0:SH, 2:3]))
                    link(v.tensor_copy(ex[:, NS:2 * NS], w0[0:SH, NP:T]), fd_sp)
                elif k == "ft":
                    ps = filled(dve, j)
                    v.tensor_copy(tokc[:, 0:64].rearrange("p (a h) -> p a h", a=2),
                                  ps[:, 0:96].rearrange("p (a h) -> p a h", a=2)[:, :, 0:SH])
                    v.tensor_copy(tokc[:, 64:224], ps[:, 144:304])
                    v.tensor_copy(lft[:, 0:2, :], ps[:, 0:96].rearrange("p (a h) -> p a h", a=2)[:, :, SH:HB])
                    release(dve, v.tensor_copy(lft[0:NS, 2, :], ps[0:NS, 96 + SH:96 + HB]), j)
                    dve.wait_ge(consts, 4)
                    link(v.tensor_tensor(lfn[0:NS, :].rearrange("p (b h) -> p b h", b=NS),
                                         lft[0:NS, 2:3, :].to_broadcast([NS, NS, NH]),
                                         bm8[:].rearrange("p (b h) -> p b h", b=NS), ALU.mult), lfn_ready)
                elif k in ("kn", "qn"):
                    c0 = 8 if k == "kn" else 4 * (j[1] // 4)
                    base = j[1] - j[1] % 4
                    if j[1] % 4 == 0:
                        for i in range(4):
                            read_out(dve, (k[0], base + i))
                        link(v.tensor_tensor(u[:, 0:4, :], qkT[:, c0:c0 + 4, :], qkT[:, c0:c0 + 4, :], ALU.mult), qk_sq)
                    elif j[1] % 4 == 3:
                        for i in range(4):
                            read_out(dve, (k, base + i))
                        link(v.reciprocal(rs[:], rs[:]))
                        col = gqk[:, 1:2] if k == "kn" else gqk[:, 0:1]
                        link(v.scalar_tensor_tensor(qkT[:, c0:c0 + 4, :], qkT[:, c0:c0 + 4, :], col, rs[:],
                                                    ALU.mult, ALU.mult), qk_ready)
                        if j == ("qn", 7):
                            dve.wait_ge(qbd_zero, 1)
                            for h in range(2):
                                dst = qbd[64 * h:64 * h + 64, 2 * h:2 * h + 4224]\
                                    .rearrange("p (b m x) -> p b m x", b=NS, m=4)[:, :, :, 0:2]
                                qs = qkT[64 * h:64 * h + 64, 0:8, NP:T].rearrange("p (m s) b -> p b m s", s=2)
                                link(v.tensor_copy(dst, qs), qbd_ready)
                elif k == "s":
                    ps, p = filled(dve, j), j[2]
                    release(dve, v.tensor_tensor(pb[:, p, :], ps[:, 0:384], cmask[:], ALU.add), j)
                    for q, (lo, hi) in enumerate(((0, 128), (128, 384))):
                        link(v.tensor_reduce(sm2[:, 4 * p + q:4 * p + q + 1], pb[:, p, lo:hi], AX.X, ALU.max, negate=True),
                             s_max if q else dve_step)
                elif k == "pt":
                    p = j[2]
                    dve.wait_ge(s_exp, 2 * j[1] + p + 1)
                    link(v.reciprocal(sm2[:, 4 * p + 2:4 * p + 4], sm2[:, 4 * p + 2:4 * p + 4]))
                    for q, (lo, hi) in enumerate(((0, 128), (128, 384))):
                        link(v.tensor_scalar(pb[:, p, lo:hi], pb[:, p, lo:hi], sm2[:, 4 * p + 2 + q:4 * p + 3 + q], None,
                                             ALU.mult), p_ready if q else dve_step)
                elif k == "xbc":
                    i, x = j[1], xa[:, j[1] % 2, :]
                    read_out(dve, j)
                    xs4 = x[:, 3 + NP:XW].rearrange("p (b w) -> p b w", w=4)
                    link(v.tensor_copy(xs4[:, :, 0:3], stT[:, i, :].rearrange("p (b w) -> p b w", w=3)))
                    link(v.tensor_copy(tails[:, i, 0:24].rearrange("p (b w) -> p b w", w=3), xs4[:, :, 1:4]))
                    link(v.tensor_copy(tails[:, i, 24:27], x[:, NP:NP + 3]))
                    if i >= 2:
                        dve.wait_ge(u_ready, i - 1)
                    acc = cacc[:, i % 2, :]
                    link(v.tensor_scalar(acc, x[:, 0:XO], vec[:, 104 + i:105 + i], vec[:, 80 + i:81 + i], ALU.mult, ALU.add))
                    for w in range(1, 4):
                        link(v.scalar_tensor_tensor(acc, x[:, w:w + XO], vec[:, 104 + 24 * w + i:105 + 24 * w + i], acc,
                                                    ALU.mult, ALU.add), conv_ready if w == 3 else dve_step)
                elif k == "sk" and j[2] == 1:
                    filled(dve, j)
                    link(v.tensor_copy(ktb[:, j[1] % 2, :, 256], qkT[:, 8:12, NP + j[1]]), kcol_ready)
                elif k == "sp":
                    dve.wait_ge(ss_done, 1)
                    link(v.tensor_reduce(sm2[:, 8:9], sbank[:, 0:257], AX.X, ALU.max, negate=True), ss_max)
                    dve.wait_ge(ss_exp, 1)
                    link(v.reciprocal(sm2[:, 9:10], sm2[:, 9:10]))
                    link(v.tensor_scalar(ps_s, ps_s, sm2[:, 9:10], None, ALU.mult))
                    link(v.tensor_scalar(pnb, bm2[:], ps_s[:, 256:257], None, ALU.mult), sp_ready)
                elif k == "sx":
                    ps, hf = filled(dve, j), j[1]
                    for m in range(4):
                        for h in range(2):
                            x = 4 * m + 2 * h
                            ins = v.tensor_copy(
                                attT[64 * h:64 * h + 64, 2 * m:2 * m + 2, NP + 4 * hf:NP + 4 * hf + 4].rearrange("p s b -> p b s"),
                                ps[64 * h:64 * h + 64, 128 * m:128 * m + 128].rearrange("p (b x) -> p b x", b=4)[:, :, x:x + 2])
                    release(dve, ins, j)
                elif k == "exp":
                    ps = filled(dve, j)
                    release(dve, v.tensor_copy(exo[:], ps[:, 0:NXB * 17].rearrange("p (c k) -> p c k", c=NXB)), j)
                    link(v.tensor_tensor(exo[:, :, 0:NS], exo[:, :, 0:NS], u[:, 0:NXB, NP:T], ALU.mult), xds_ready)
                elif k == "xs":
                    ps, a, g = filled(dve, j), j[1], j[2]
                    dve.wait_ge(o_small, 16 * 5)
                    dt = tokc[:, 32 * a + 8 * g:32 * a + 8 * g + 8].unsqueeze(2).to_broadcast([128, 8, HD])
                    release(dve, v.tensor_tensor(xd[:, a, 512 * g:512 * g + 512].rearrange("p (h d) -> p h d", h=8),
                                                 ps.rearrange("p (h d) -> p h d", h=8), dt, ALU.mult), j)
                elif k == "cb":
                    ps = filled(dve, j)
                    release(dve, v.tensor_tensor(cbm, ps.rearrange("p (g k) -> p g k", g=SG),
                                                 triu[:].unsqueeze(1).to_broadcast([128, SG, 128]), ALU.mult), j)
                elif k == "ab":
                    ps, a, b = filled(dve, j), j[1], j[2]
                    if a == 0 and b == 0:
                        dve.wait_ge(bs_out, 16)
                    for i in range(4):
                        h = 4 * b + i
                        if i == 0 and a == 1:
                            dve.wait_ge(et_ready, b + 1)
                        ins = v.tensor_scalar(wd[:, b % 2, 128 * i:128 * i + 128], ps[:, 128 * i:128 * i + 128],
                                              tokc[:, 64 + 32 * a + h:65 + 32 * a + h], 0.0, ALU.subtract, ALU.min)
                    release(dve, ins, j)
                    if b:
                        weigh(a, b - 1)
                elif k == "y":
                    a, b = j[1], j[2]
                    if b == 7:
                        weigh(a, 7)
                    ps = filled(dve, j)
                    for q in range(2):
                        hp, tk = 2 * b + q, slice(128 * a, 128 * a + 128)
                        ins = v.scalar_tensor_tensor(yT[:, hp, tk], u[:, hp, tk], exo[:, hp, 16:17],
                                                     ps[:, 128 * q:128 * q + 128], ALU.mult, ALU.add)
                    release(dve, ins, j)
                    if a == 1:
                        read_out(dve, ("z", 2 * b))
                        read_out(dve, ("z", 2 * b + 1))
                        hp = slice(2 * b, 2 * b + 2)
                        link(v.tensor_tensor(yT[:, hp, 0:NP], yT[:, hp, 0:NP], zb[:, hp, :], ALU.mult), zg_done)
                        v.tensor_tensor(u[:, hp, 0:NP], yT[:, hp, 0:NP], yT[:, hp, 0:NP], ALU.mult)
                elif k == "ssm":
                    b = j[1]
                    dve.wait_ge(st_dec, b + 1)
                    dve.wait_ge(bc_full[b % 2], 16 * (b // 2 + 1))
                    for c in range(NXB):
                        s = sst[:, b % 2, NST * c:NST * c + NST]
                        ins = v.scalar_tensor_tensor(s, bc[:, b % 2, NST * (c // 4):NST * (c // 4) + NST], exo[:, c, b:b + 1], s,
                                                     ALU.mult, ALU.add)
                    link(ins, st_new)
                    if b:
                        state_sum(b - 1)
                    if b == NS - 1:
                        state_sum(b)
                        dx = exo[:, :, 16:17].to_broadcast([128, NXB, NS])
                        ys = yT[:, :, NP:T]
                        link(v.tensor_tensor(exo[:, :, 0:NS], u[:, 0:NXB, NP:T], dx, ALU.mult))
                        link(v.tensor_tensor(ys, ys, exo[:, :, 0:NS], ALU.add))
                        link(v.tensor_tensor(ys, ys, zsS[:], ALU.mult))
                        link(v.tensor_tensor(u[:, 0:NXB, NP:T], ys, ys, ALU.mult), y_sq)
                elif k == "yn":
                    g = j[1]
                    read_out(dve, j)
                    link(v.reciprocal(rs[:, g, :], rs[:, g, :]))
                    for c in range(4 * g, 4 * g + 4):
                        ins = v.scalar_tensor_tensor(yT[:, c, :], yT[:, c, :], vec[:, 64 + c:65 + c], rs[:, g, :],
                                                     ALU.mult, ALU.mult)
                    link(ins, y_ready)
                elif k == "pa":
                    ps, i = filled(dve, j), j[1]
                    read_out(dve, ("g", i))
                    release(dve, v.tensor_tensor(gT[:, i, :], gT[:, i, :], ps[:, 0:T], ALU.mult), j)
                elif k == "pb":
                    ps, i = filled(dve, j), j[1]
                    read_out(dve, ("g", 8 + i))
                    release(dve, v.tensor_tensor(gT[:, 8 + i, :], gT[:, 8 + i, :], ps[:, 0:T], ALU.mult), j)
                    link(v.tensor_tensor(gT[:, i, :], gT[:, i, :], gT[:, 8 + i, :], ALU.add), m_ready)
                elif k == "o":
                    ps, i = filled(dve, j), j[1]
                    v.scalar_tensor_tensor(xT[:, i, 0:NP], ps[:, 0:NP], modT[:, 16 + i, NS:NC], xT[:, i, 0:NP],
                                           ALU.mult, ALU.add)
                    release(dve, v.tensor_tensor(sm2[:, 16:24], ps[:, NP:T], modT[:, 16 + i, 0:NS], ALU.mult), j)
                    link(v.tensor_tensor(xT[:, i, NP:T], xT[:, i, NP:T], sm2[:, 16:24], ALU.add))
                    if i == KD - 1:
                        squares(1)
                elif k == "lr":
                    ps = filled(dve, j)
                    release(dve, v.tensor_scalar(lgT[0:NE, :], ps[0:NE, 0:T], brow[:], None, ALU.add), j)
                elif k == "lt":
                    link(v.memset(lg, 0.0))
                    ps = filled(dve, j)
                    v.tensor_copy(lg[:, 0:2, :], ps[:, 0:32].rearrange("p (a e) -> p a e", a=2))
                    release(dve, v.tensor_copy(lg[0:NS, 2, :], ps[0:NS, 32:48]), j)
                    route()
                elif k == "rk":
                    ps = filled(dve, j)
                    v.tensor_copy(rank, ps[:, 0:48].rearrange("p (a e) -> p a e", a=3))
                    release(dve, v.tensor_copy(cnt, ps[:, 48:64]), j)
                    link(v.tensor_reduce(rw[0][0:1, 0:1], cnt[0:1, :], AX.X, ALU.max))
                    link(v.tensor_scalar(rt[0][0:1, 0, :], thr[:], rw[0][0:1, 0:1], None, ALU.is_lt))
                    link(v.tensor_reduce(rw[1][0:1, 0:1], rt[0][0:1, 0, :], AX.X, ALU.add))
                    link(v.tensor_scalar(rounds_sb[:], rw[1][0:1, 0:1], 1.0, None, ALU.add), rk_ready)

            def select(t, q):
                dve.wait_ge(selT_done, t + 1)
                for w, m in enumerate((asg, cmb)):
                    for e in range(4):
                        for a in range(3):
                            col = bass.ds(q * 4 + e, 1)
                            ins = v.tensor_scalar(sel[:, w, a, BLK * e:BLK * e + BLK], iota[:], rank[:, a, col], m[:, a, col],
                                                  ALU.is_equal, ALU.mult)
                ins.then_inc(sel_ready, 1)

            def gathered(t):
                for s in range(4):
                    dve.wait_ge(gath_filled, t * 4 + (s + 1))
                    v.tensor_copy(xg[:, 2 * s:2 * s + 2, :], banks[(7, 4)[s % 2]][:].rearrange("p (k s) -> p k s", k=2))\
                        .then_inc(xg_ready, 1)

            def multiply(it):
                dve.wait_ge(silu_ready, it + 2)
                dve.wait_ge(up_done, it + 2)
                v.tensor_tensor(hact, gact, banks[1][:], ALU.mult).then_inc(act_ready, 1)

            def combined(it):
                dve.wait_ge(comb_read, it * 8 + 1)
                for c in range(KD):
                    dve.wait_ge(comb_filled, it * 8 + (c + 1))
                    v.tensor_tensor(Y[:, c, :], Y[:, c, :], banks[5 + c % 2][:, 0:T], ALU.add).then_inc(comb_read, 1)

            def four(r, q, last):
                it = r * 8 + q * 2
                multiply(it)
                if not last:
                    select(r * 4 + (q + 1), q + 1)
                multiply(it + 1)
                combined(it)
                if not last:
                    gathered(r * 4 + (q + 1))
                combined(it + 1)

            rounds = dve.value_load(rounds_sb[0:1, 0:1], min_val=1, max_val=5)
            dve.wait_ge(y_zero, 1)
            with dve.Fori(0, rounds) as r:
                dve.wait_ge(rk_shift, r + 1)
                select(r * 4, 0)
                gathered(r * 4)
                with dve.Fori(0, NE // 4 - 1) as q:
                    four(r, q, False)
                four(r, NE // 4 - 1, True)
                dve.wait_ge(comb_read, r * 64 + 65)
                v.tensor_scalar(rank, rank, -float(BLK), None, ALU.add).then_inc(rk_shift, 1)
            for c in range(KD):
                v.scalar_tensor_tensor(xT[:, c, 0:NP], Y[:, c, 0:NP], modT[:, 40 + c, NS:NC], xT[:, c, 0:NP],
                                       ALU.mult, ALU.add)
            link(v.tensor_tensor(Y[:, :, NP:T], Y[:, :, NP:T], modT[:, 40:48, 0:NS], ALU.mult))
            link(v.tensor_tensor(xT[:, :, NP:T], xT[:, :, NP:T], Y[:, :, NP:T], ALU.add), yfin)

        @block.tensor
        def _(pe):
            mm, tr = nc.tensor.matmul, nc.tensor.transpose
            for s in (selT_done, gate_done, up_done, down_done):
                pe.sem_inc(s, 1)

            def start(j):
                b, n = bank_of[j]
                if n > 1:
                    pe.wait_ge(bank_read[b], n - 1)
                return banks[b]

            def done(ins, j):
                ins.then_inc(bank_filled[bank_of[j][0]], 1)

            def landed(s):
                pe.wait_ge(slot_full[slot_at[s]], arrived_at[s])

            def flip(out, x):
                k = x.shape[0]
                return tr(out, x, ident[0:k, 0:k])

            for j in jobs:
                k = j[0]
                ps = start(j) if j in bank_of else None
                if k == "cT":
                    pe.wait_ge(consts, 1)
                    pe.wait_ge(cond_ready, 1)
                    for c in range(KD):
                        ins = flip(ps[:, NC * c:NC * c + NC], crow[0:NC, 128 * c:128 * c + 128])
                elif k == "vecs":
                    flip(ps[:, 0:104], vrow[0:104, 0, :])
                    ins = flip(ps[:, 104:200], vrow[0:96, 1, :])
                elif k == "mod":
                    read_out(pe, ("cT",))
                    for i in range(4):
                        landed(("mod", 4 * j[1] + i))
                    for c in range(KD):
                        for i in range(4):
                            ins = mm(ps[32 * i:32 * i + 32, 0:SW], cT[:, c, :], slot(("mod", 4 * j[1] + i))[:, c, :],
                                     start=c == 0, stop=c == KD - 1, tile_position=(0, 32 * i))
                elif k == "modt":
                    read_out(pe, ("mod", j[1]))
                    for q in range(2):
                        ins = flip(ps[:, 128 * q:128 * q + 128], mrow[:, 128 * q:128 * q + 128])
                elif k == "xt":
                    a, f, n = j[1], j[2], TOK[j[1]][1]
                    pe.wait_ge(x_in, 48)
                    for q in range(4):
                        c = 4 * f + q
                        ins = flip(ps[:, n * q:n * q + n], xin[0:n, a, 128 * c:128 * c + 128])
                elif k == "ssq":
                    pe.wait_ge(sq_ready, j[1] + 1)
                    pe.wait_ge(consts, 3)
                    for c in range(KD):
                        ins = mm(ps[:, 0:T], onesf[:], u[:, c, :], start=c == 0, stop=c == KD - 1)
                elif k == "cst":
                    pe.wait_ge(st_in, 16)
                    for q in range(12):
                        c = 12 * j[1] + q
                        ins = flip(ps[:, 24 * q:24 * q + 24], csin[0:24, 128 * c:128 * c + 128])
                elif k == "fd":
                    pe.wait_ge(h_ready, 1)
                    pe.wait_ge(late_in, 16 * 12)
                    for c in range(KD):
                        ins = mm(ps[0:HB, 0:T], wfd[:, c, :], hT[:, c, :], start=c == 0, stop=c == KD - 1)
                elif k == "ft":
                    pe.wait_ge(fd_e, 1)
                    for a, (t0, n) in enumerate(TOK):
                        ins = flip(ps[0:n, HB * a:HB * a + HB], fd[:, t0:t0 + n])
                    for i, x in enumerate((acsT[0:SH, 0:128], acsT[0:SH, 128:256], fdw[0:SH, 1, 0:128],
                                           fdw[0:SH, 1, 128:256], fdw[0:SH, 2, 0:128])):
                        ins = flip(ps[:, 144 + 32 * i:176 + 32 * i], x)
                elif k in ("q", "k", "v", "xbc", "z", "g"):
                    s, h = slots_of(j)[0], j[1] % 2
                    landed(s)
                    for c in range(KD):
                        w = slot(s)[:, c, 128 * h:128 * h + 128]
                        ins = mm(ps[:, 0:T], w, hT[:, c, :], start=c == 0, stop=c == KD - 1)
                elif k in ("kn", "qn"):
                    pe.wait_ge(qk_sq, 1 if k == "kn" else 2 + j[1] // 4)
                    ins = mm(ps[:, 0:T], blk[:], u[:, j[1] % 4, :], start=True, stop=True)
                elif k == "kt":
                    t0, n = TOK[j[1]]
                    pe.wait_ge(qk_ready, 1)
                    for m in range(4):
                        ins = flip(ps[0:n, 128 * m:128 * m + 128], qkT[:, 8 + m, t0:t0 + n])
                elif k == "vt":
                    t0, n = TOK[j[1]]
                    read_out(pe, ("v", 3))
                    for m in range(4):
                        ins = flip(ps[0:n, 128 * m:128 * m + 128], vT[:, m, t0:t0 + n])
                elif k == "s":
                    c, p = j[1], j[2]
                    m, s, r = c // 2, c % 2, slice(64 * p, 64 * p + 64)
                    h = 4 * m + 2 * p + s
                    pe.wait_ge(qk_ready, 3)
                    pe.wait_ge(fd_e, 1)
                    neg = nident[SH:HB, SH + h:SH + h + 1].to_broadcast([NH, 128])
                    for q0, lo, n in ((0, 0, 128), (128, 128, 256)):
                        mm(ps[:, lo:lo + n], qkT[r, c, q0:q0 + 128], qkT[r, 8 + m, 0:n], start=True, stop=False)
                        ins = mm(ps[:, lo:lo + n], neg, acsT[SH:HB, 0:n], start=False, stop=True)
                elif k == "pt":
                    p = j[2]
                    pe.wait_ge(p_ready, 2 * j[1] + p + 1)
                    for q in range(3):
                        ins = flip(ps[:, 128 * q:128 * q + 128], pb[:, p, 128 * q:128 * q + 128])
                elif k == "o2":
                    c = j[1]
                    for p in range(2):
                        read_out(pe, ("pt", c, p))
                        g = 2 * (c // 2) + p
                        vs = [vtok[:, a, 64 * g:64 * g + 64] for a in range(2)]
                        r = slice(64 * p, 64 * p + 64)
                        mm(ps[r, 0:128], vs[0], pT[:, p, 0:128], start=True, stop=True)
                        mm(ps[r, 128:256], vs[0], pT[:, p, 128:256], start=True, stop=False)
                        ins = mm(ps[r, 128:256], vs[1], pT[:, p, 256:384], start=False, stop=True)
                elif k == "sk":
                    b, q = j[1], j[2]
                    pe.wait_ge(kv_full[b % 4], 32 * (b // 4 + 1))
                    for m in range(4):
                        ins = flip(ps[:, 128 * m:128 * m + 128], kvr[:, b % 4, q, 128 * m:128 * m + 128])
                elif k == "ss":
                    b = j[1]
                    read_out(pe, ("sk", b, 0))
                    read_out(pe, ("sk", b, 1))
                    pe.wait_ge(kcol_ready, b + 1)
                    pe.wait_ge(qbd_ready, 2)
                    for m in range(4):
                        o = 128 * (4 * b + m)
                        mm(sbank[:, 0:257], qbd[:, o:o + 128], ktb[:, b % 2, m, :], start=b == 0 and m == 0, stop=False)
                    if b == NS - 1:
                        pe.wait_ge(lf_in, 16 * NS * NPG)
                        pe.wait_ge(lfn_ready, 1)
                        mm(sbank[:, 0:257], lfc[:, 0, :], ntri[:, 128:385], start=False, stop=False)
                        mm(sbank[:, 0:257], lfc[:, 1, :], ntri[:, 0:257], start=False, stop=False)
                        mm(sbank[:, 256:257], lfn[0:NS, :], ntri[0:NS, 384:385], start=False, stop=True)\
                            .then_inc(ss_done, 1)
                    continue
                elif k == "sp":
                    pe.wait_ge(sp_ready, 1)
                    for q in range(NPG):
                        flip(ps[:, 128 * q:128 * q + 128], ps_s[:, 128 * q:128 * q + 128])
                    ins = mm(ps[0:NS, 256:384], pnb, ident[:], start=True, stop=True)
                elif k == "so":
                    hf = j[1]
                    read_out(pe, ("sp",))
                    for b in range(4):
                        pe.wait_ge(kv_full[b], 96 + 32 * hf)
                    for q in range(NPG + 1):
                        for bb in range(4):
                            c = 16 * (4 * hf + bb)
                            w, x = ((psT[:, q, c:c + 32], kvr[:, bb, q, :]) if q < NPG else
                                    (pn[0:NS, c:c + 32], vtok[0:NS, 2, :]))
                            ins = mm(ps[32 * bb:32 * bb + 32, :], w, x, start=q == 0, stop=q == NPG,
                                     tile_position=(0, 32 * bb))
                elif k == "sx":
                    read_out(pe, ("so", j[1]))
                    for m in range(4):
                        ins = flip(ps[:, 128 * m:128 * m + 128], otok[:, 128 * m:128 * m + 128])
                elif k == "ct":
                    pe.wait_ge(conv_ready, NCB)
                    for q in range(4):
                        ins = flip(ps[0:27, 128 * q:128 * q + 128], tails[:, 4 * j[1] + q, :])
                elif k == "bs":
                    pe.wait_ge(u_ready, NCB)
                    for q in range(4):
                        ins = flip(ps[0:NS, 128 * q:128 * q + 128], u[:, NXB + 4 * j[1] + q, NP:T])
                elif k == "exp":
                    for c in range(NXB):
                        for h in range(2):
                            w = ident[0:SH, 2 * c + h:2 * c + h + 1].to_broadcast([SH, 64])
                            ins = mm(ps[64 * h:64 * h + 64, 17 * c:17 * c + 17], w, ex[:], start=True, stop=True)
                elif k == "bt":
                    for q in range(4):
                        ins = flip(ps[:, 128 * q:128 * q + 128], u[:, NXB + q, 128 * j[1]:128 * j[1] + 128])
                elif k == "xs":
                    a, g = j[1], j[2]
                    for q in range(4):
                        ins = flip(ps[:, 128 * q:128 * q + 128], u[:, 4 * g + q, 128 * a:128 * a + 128])
                elif k == "s1":
                    g = j[1]
                    read_out(pe, ("bt", 0))
                    pe.wait_ge(xe_ready, 1)
                    ins = mm(ps[:], btok[:, 0, 128 * g:128 * g + 128], xe[:, 0, 512 * g:512 * g + 512],
                             start=True, stop=True)
                elif k == "cb":
                    tk = slice(128 * j[1], 128 * j[1] + 128)
                    for g in range(SG):
                        ins = mm(ps[:, 128 * g:128 * g + 128], u[:, NXB + g, tk], u[:, NXB + SG + g, tk],
                                 start=True, stop=True)
                elif k == "ab":
                    a, b = j[1], j[2]
                    for i in range(4):
                        h = 4 * b + i
                        ins = mm(ps[:, 128 * i:128 * i + 128], ident[0:SH, h:h + 1].to_broadcast([SH, 128]),
                                 acsT[0:SH, 128 * a:128 * a + 128], start=True, stop=True)
                elif k == "y":
                    a, b = j[1], j[2]
                    pe.wait_ge(w_ready, 8 * a + b + 1)
                    read_out(pe, ("xs", a, b // 2))
                    if a == 1:
                        pe.wait_ge(ce_ready, b + 1)
                        read_out(pe, ("s1", 3))
                    for i in range(4):
                        h = 4 * b + i
                        o = ps[64 * (i % 2):64 * (i % 2) + 64, 128 * (i // 2):128 * (i // 2) + 128]
                        ins = mm(o, xd[:, a, 64 * h:64 * h + 64], wd[:, b % 2, 128 * i:128 * i + 128],
                                 start=True, stop=a == 0)
                        if a == 1:
                            ins = mm(o, s1T[:, 64 * h:64 * h + 64], ce[:, b % 2, 128 * i:128 * i + 128],
                                     start=False, stop=True)
                elif k == "fs":
                    i = j[1]
                    pe.wait_ge(xe_ready, 3)
                    read_out(pe, ("bt", 1))
                    for q in range(4):
                        c = 4 * i + q
                        for a in range(2):
                            ins = mm(ps[:, 128 * q:128 * q + 128], xe[:, a, 128 * c:128 * c + 128],
                                     btok[:, a, 128 * i:128 * i + 128], start=a == 0, stop=a == 1)
                elif k == "ssm":
                    continue
                elif k == "pa":
                    i = j[1]
                    s = slots_of(j)[0]
                    landed(s)
                    read_out(pe, ("o2", 7))
                    read_out(pe, ("sx", 1))
                    for c in range(KD):
                        ins = mm(ps[:, 0:T], slot(s)[:, c, 128 * (i % 2):128 * (i % 2) + 128], attT[:, c, :],
                                 start=c == 0, stop=c == KD - 1)
                elif k == "yn":
                    g = j[1]
                    pe.wait_ge(y_sq, 1)
                    for c in range(4):
                        ins = mm(ps[:, 0:T], onesf[:], u[:, 4 * g + c, :], start=c == 0, stop=c == 3)
                elif k == "pb":
                    i = j[1]
                    for s in slots_of(j):
                        landed(s)
                    for c in range(NXB):
                        if i == 0 and c % 4 == 0:
                            pe.wait_ge(y_ready, c // 4 + 1)
                        w = slot(("pb", i // 2, c // KD))[:, c % KD, 128 * (i % 2):128 * (i % 2) + 128]
                        ins = mm(ps[:, 0:T], w, yT[:, c, :], start=c == 0, stop=c == NXB - 1)
                elif k == "o":
                    i = j[1]
                    s = slots_of(j)[0]
                    landed(s)
                    for c in range(KD):
                        if i == 0:
                            pe.wait_ge(m_ready, c + 1)
                        ins = mm(ps[:, 0:T], slot(s)[:, c, 128 * (i % 2):128 * (i % 2) + 128], gT[:, c, :],
                                 start=c == 0, stop=c == KD - 1)
                elif k == "lr":
                    pe.wait_ge(h_ready, 2)
                    for c in range(KD):
                        ins = mm(ps[0:NE, 0:T], wr[:, c, :], hT[:, c, :], start=c == 0, stop=c == KD - 1)
                elif k == "lt":
                    read_out(pe, ("lr",))
                    for a, (t0, n) in enumerate(TOK):
                        ins = flip(ps[0:n, NE * a:NE * a + NE], lgT[0:NE, t0:t0 + n])
                elif k == "ht":
                    a, f, (t0, n) = j[1], j[2], TOK[j[1]]
                    for q in range(4):
                        ins = flip(ps[0:n, 128 * q:128 * q + 128], hT[:, 4 * f + q, t0:t0 + n])
                elif k == "rk":
                    pe.wait_ge(asg_ready, 2)
                    for a in range(4):
                        for b in range(min(a + 1, 3)):
                            ins = mm(ps[:, NE * a:NE * a + NE], striu[:] if a == b else onesb[:], asb[:, b, :],
                                     start=b == 0, stop=b == min(a, 2))
                done(ins, j)

            for b in range(NBANK):
                pe.wait_ge(bank_read[b], at_moe[b])
            pe.wait_ge(rk_ready, 1)

            def gather(t):
                pe.wait_ge(sel_ready, t + 1)
                for s in range(4):
                    pe.wait_ge(xg_ready, t * 4 + (s + 1))
                    for k in range(2):
                        c = 2 * s + k
                        for a, (t0, n) in enumerate(TOK):
                            ins = mm(banks[(7, 4)[s % 2]][:, 256 * k:256 * k + 256], h2tok[0:n, a, 128 * c:128 * c + 128],
                                     sel[0:n, 0, a, :], start=a == 0, stop=a == 2)
                    ins.then_inc(gath_filled, 1)

            def gate_up(it, p):
                for i, sig in enumerate((gate_done, up_done)):
                    for e in range(2):
                        pe.wait_ge(moe_full[2 * i + e], (it + 1) * 16)
                    for c in range(KD):
                        for e in range(2):
                            w = mslot[2 * i + e].rearrange("p (k n) -> p k n", k=KD)
                            ins = mm(banks[i][BLK * e:BLK * e + BLK, :], xg[:, c, BLK * (2 * p + e):BLK * (2 * p + e + 1)],
                                     w[:, c, :], start=c == 0, stop=c == KD - 1, tile_position=(0, BLK * e))
                    ins.then_inc(sig, 1)

            def down(it):
                pe.wait_ge(act_ready, it + 2)
                for q in range(4):
                    ins = flip(banks[4][:, 128 * q:128 * q + 128], hact[:, 128 * q:128 * q + 128])
                ins.then_inc(actT_done, 1)
                for e in range(2):
                    pe.wait_ge(moe_full[4 + e], (it + 1) * 16)
                pe.wait_ge(actT_ready, it + 1)
                for q in range(2):
                    for c in range(4):
                        for e in range(2):
                            r = slice(BLK * e, BLK * e + BLK)
                            w = mslot[4 + e].rearrange("p (k n) -> p k n", k=4)
                            ins = mm(banks[2 + q][r, :], aT[:, c, r], w[:, c, 512 * q:512 * q + 512], start=c == 0,
                                     stop=c == 3, tile_position=(0, BLK * e))
                    ins.then_inc(down_done, 1)

            def combine(it, p):
                for c in range(KD):
                    if c % 4 == 0:
                        pe.wait_ge(out_ready, it * 2 + (c // 4 + 1))
                    pe.wait_ge(comb_read, it * 8 + max(c, 1))
                    mm(banks[5 + c % 2][:, 0:T], outs[:, 128 * c:128 * c + 128], selT[:, p, :], start=True, stop=True)\
                        .then_inc(comb_filled, 1)

            def four(r, q, last):
                t, it = r * 4 + q, r * 8 + q * 2
                pe.wait_ge(xg_ready, t * 4 + 6)
                gate_up(it, 0)
                for p in range(2):
                    for a, (t0, n) in enumerate(TOK):
                        ins = flip(banks[2 + p][:, t0:t0 + n], sel[0:n, 1, a, 128 * p:128 * p + 128])
                ins.then_inc(selT_done, 1)
                pe.wait_ge(selT_ready, t + 1)
                down(it)
                gate_up(it + 1, 1)
                combine(it, 0)
                down(it + 1)
                if not last:
                    gather(t + 1)
                combine(it + 1, 1)

            rounds = pe.value_load(rounds_sb[0:1, 0:1], min_val=1, max_val=5)
            with pe.Fori(0, rounds) as r:
                gather(r * 4)
                with pe.Fori(0, NE // 4 - 1) as q:
                    four(r, q, False)
                four(r, NE // 4 - 1, True)
            pe.wait_ge(yfin, 1)
            for j in late:
                a, f, (t0, n) = j[1], j[2], TOK[j[1]]
                ps = start(j)
                for q in range(4):
                    ins = flip(ps[0:n, 128 * q:128 * q + 128], xT[:, 4 * f + q, t0:t0 + n])
                done(ins, j)


OUTS = [("y_prompt", (1, NP, D)), ("y_sample", (NS, 1, D)), ("k_prompt", (1, 1, NP, NKV, HD)),
        ("v_prompt", (1, 1, NP, NKV, HD)), ("logf_prompt", (1, 1, NP, NH)), ("ssm_prompt", (1, 1, SH, HD, NST)),
        ("conv_prompt", (1, 1, 3, CD)), ("k_sample", (1, NS, 1, NKV, HD)), ("v_sample", (1, NS, 1, NKV, HD)),
        ("logf_sample", (1, NS, 1, NH)), ("ssm_sample", (1, NS, SH, HD, NST)), ("conv_sample", (1, NS, 3, CD))]


def kernel(**inputs):
    import numpy as np
    import concourse.bacc as bacc
    from concourse.bass_utils import run_bass_kernel_spmd

    nc = bacc.Bacc("TRN2", target_bir_lowering=False, num_devices=1)
    arrays, t = {}, {}
    for name, x in inputs.items():
        a = np.ascontiguousarray(x)
        arrays["in_" + name] = a
        t[name] = nc.dram_tensor("in_" + name, a.shape, mybir.dt.from_np(a.dtype), kind="ExternalInput").ap()
    for name, shape in OUTS:
        t[name] = nc.dram_tensor("out_" + name, shape, F32, kind="ExternalOutput").ap()
    t["bc_scratch"] = nc.dram_tensor("bc_scratch", (NS, 2 * SG * NST), F32, kind="Internal").ap()
    build(nc, t)
    r = run_bass_kernel_spmd(nc, [arrays], core_ids=[0])
    return tuple(r.results[0]["out_" + name] for name, _ in OUTS)
```

```python
import concourse.bass as bass
from concourse import mybir
from contextlib import ExitStack

F32 = mybir.dt.float32
BF16 = mybir.dt.bfloat16
I32 = mybir.dt.int32
ALU = mybir.AluOpType
ACT = mybir.ActivationFunctionType
AX = mybir.AxisListType

D = 1024
NP, NS = 256, 8
T = NP + NS
NC = NS + 1
KD = D // 128
NH, NKV, HD = 16, 8, 64
PAGE, NPG = 128, 2
KVW = NKV * HD
DI, SH, SG, NST = 2048, 32, 4, 128
CD = DI + 2 * SG * NST
NCB = CD // 128
NXB = DI // 128
HB = SH + NH
NE, EPG, NG, FF = 16, 4, 4, 512
EPS = 1e-6
COL_K, COL_V, COL_F = D, D + KVW, D + 2 * KVW
COL_Z = COL_F + NH
COL_X = COL_Z + DI
COL_DT = COL_X + CD
COL_G = COL_DT + SH
IN_DIM = COL_G + 2 * D
TOK = [(0, 128), (128, 128), (256, NS)]
SW = 256
SLOT = KD * SW
NSLOT = 6
NBANK = 7
BLK = 64
XW = 3 + NP + 4 * NS
XO = XW - 3


def build(nc, t):
    ctx = ExitStack()
    with ctx:
        def sb(name, shape, dt=F32):
            return ctx.enter_context(nc.sbuf_tensor(name, shape, dt))

        def sem(name):
            return ctx.enter_context(nc.semaphore(name))

        ring = sb("weight_ring", [128, NSLOT * SLOT])
        xT = sb("x_residual", [128, KD, T])
        hT = sb("h_normed", [128, KD, T])
        modT = sb("modulation", [128, 6 * KD, NC])
        gsc = sb("norm_gain", [128, KD, NC])
        ident = sb("identity", [128, 128])
        nident = sb("neg_identity", [HB, HB])
        ntri = sb("neg_triangle", [128, 3 * 128 + 1])
        cmask = sb("causal_mask", [128, 384])
        triu = sb("upper_triangle", [128, 128])
        onesf = sb("ones", [128, 128])
        blk = sb("head_blocks", [128, 128])
        striu = sb("strict_upper", [128, 128], BF16)
        onesb = sb("ones_bf", [128, 128], BF16)
        bm8 = sb("sample_rows", [NS, 128])
        bm2 = sb("sample_cols", [128, NS])
        iota = sb("slot_numbers", [128, BLK])
        w4 = sb("first_weights", [128, 4])
        thr = sb("round_limits", [1, 4])
        epsc = sb("eps_col", [128, 1])
        vec = sb("vectors", [128, 200])
        gqk = sb("qk_gain", [128, 2])
        hcol = sb("head_cols", [HB, 4])
        brow = sb("router_bias", [NE, 1])
        cT = sb("cond_T", [128, KD, 32])
        wfd = sb("w_forget_dt", [128, KD, HB])
        wr = sb("w_router_sb", [128, KD, NE])
        pgs = sb("pages", [1, NS * NPG], I32)
        rs = sb("rstd", [128, 4, T])
        attT = sb("att_T", [128, KD, T])
        u = sb("conv_out", [128, NCB, T])
        xa = sb("conv_in", [128, 2, XW])
        cacc = sb("conv_sum", [128, 2, XO])
        tails = sb("conv_tails", [128, NCB, 27])
        yq = sb("y_T", [128, 4228])
        yT = yq[:, 0:NXB * T].rearrange("p (c t) -> p c t", c=NXB)
        fd = sb("dt_logf", [HB, T])
        acsT = sb("cums", [HB, NP])
        ex = sb("expand_in", [SH, 2 * NS + 1])
        tokc = sb("token_cols", [128, 7 * 32])
        lft = sb("logf_tok", [128, 3, NH])
        exo = sb("expanded", [128, NXB, 2 * NS + 1])
        sm2 = sb("small", [128, 64])
        fdw = sb("head_work", [HB, 3, T])
        mrow = sb("mod_rows", [128, SW])
        stT = sb("conv_states", [128, NCB, 24])
        zsS = sb("z_samples", [128, NXB, NS])
        ARENA = 14848
        ar = sb("arena", [128, ARENA])
        at = [0]

        def part(n):
            o = at[0]
            at[0] += n
            assert at[0] <= ARENA, at[0]
            return ar[:, o:o + n]

        qkT = part(12 * T).rearrange("p (c t) -> p c t", c=12)
        vtok = part(3 * KVW).rearrange("p (a f) -> p a f", a=3)
        kvf = part(4 * NPG * KVW)
        kvr = kvf.rearrange("p (s g f) -> p s g f", s=4, g=NPG)
        ktb = part(2 * 4 * 257).rearrange("p (s m k) -> p s m k", s=2, m=4)
        pbT = part(4 * 384)
        pb = pbT[:, 0:768].rearrange("p (s k) -> p s k", s=2)
        pT = pbT[:, 768:1536].rearrange("p (s k) -> p s k", s=2)
        vT = pbT[:, 0:4 * T].rearrange("p (c t) -> p c t", c=4)
        ps_s = part(257)
        psT = part(NPG * 144).rearrange("p (g k) -> p g k", g=NPG)
        pn = part(144)
        otok = part(KVW)
        ktok = otok
        lfc = part(NPG * 128).rearrange("p (g k) -> p g k", g=NPG)
        lfn = part(128)
        pnb = part(NS)
        qbd = yq
        xin = kvf[:, 0:3 * D].rearrange("p (a d) -> p a d", a=3)
        vrow = otok[:, 0:256].rearrange("p (a k) -> p a k", a=2)
        crow = ar[:, 0:D]
        csin = ar[:, D:D + CD]
        at[0] = 0
        xd = part(2 * DI).rearrange("p (a f) -> p a f", a=2)
        xef = part(2 * DI)
        xe = xef.rearrange("p (a f) -> p a f", a=2)
        btok = part(2 * SG * NST).rearrange("p (a f) -> p a f", a=2)
        s1T = part(DI)
        cbm = part(SG * 128).rearrange("p (g k) -> p g k", g=SG)
        wdf = part(3 * 512)
        wd = wdf.rearrange("p (s k) -> p s k", s=3)
        ce = part(3 * 512).rearrange("p (s k) -> p s k", s=3)
        ctok = cacc[:].rearrange("p s k -> p (s k)")[:, 0:512]
        zb = ring[:, 4 * SLOT:6 * SLOT].rearrange("p (c t) -> p c t", c=NXB)
        at[0] = 16 * T
        s_odd, bc_odd, prod = part(NXB * NST), part(2 * SG * NST), part(NXB * NST)
        s_even, bc_even, bx = part(NXB * NST), part(2 * SG * NST), part(NXB * NST)
        sst, bc = (s_even, s_odd), (bc_even, bc_odd)
        fso = ar[:, 8 * T:8 * T + DI].rearrange("p (s k) -> p s k", s=4)
        gT = ar[:, 0:16 * T].rearrange("p (c t) -> p c t", c=16)
        mslot = [ar[:, 4224 + i * 4096:4224 + (i + 1) * 4096] for i in range(2)] + [yq[:, 0:4096]] + \
                [ring[:, i * 4096:(i + 1) * 4096] for i in range(3)]

        def blocks(a, n):
            return u[:].rearrange("p c t -> p (c t)")[:, a:a + n]

        h2tok = blocks(0, 3 * D).rearrange("p (a d) -> p a d", a=3)
        xg = blocks(3 * D, 2 * D).rearrange("p (k s) -> p k s", k=KD)
        outs = blocks(5 * D, D)
        sel = ar[:, 0:1536].rearrange("p (w a s) -> p w a s", w=2, a=3)
        selT = ar[:, 1536:1536 + 2 * T].rearrange("p (e t) -> p e t", e=2)
        hact = ar[:, 2080:2592]
        gact = ar[:, 2592:3104]
        aT = ar[:, 3104:3616].rearrange("p (k s) -> p k s", k=4)
        mr = ar[:, 4224 + 2 * 4096:ARENA]
        lgT = mr[:, 0:T]

        def rows3(o, n=NE):
            return mr[:, o:o + 3 * n].rearrange("p (a e) -> p a e", a=3)

        lg, cmb, asg, rank, prg = (rows3(264 + 48 * i) for i in range(5))
        rt = [rows3(504 + 12 * i, 4) for i in range(12)]
        rw = [mr[:, 648 + 4 * i:651 + 4 * i] for i in range(10)]
        cnt = mr[:, 688:688 + NE]
        asb = sb("assigned_bf", [128, 3, NE], BF16)
        rounds_sb = sb("rounds", [1, 1], I32)
        Y = attT
        yout = yq[:, 0:3 * D].rearrange("p (a d) -> p a d", a=3)

        banks = [ctx.enter_context(nc.psum_tensor(f"bank{i}", [128, 512], F32)) for i in range(8)]
        sbank = banks[7]

        jobs = [("cT",), ("vecs",)] + [("xt", a, f) for a in range(3) for f in range(2)]
        jobs += [("ssq", 0), ("mod", 0), ("modt", 0), ("cst", 0), ("cst", 1), ("mod", 1), ("modt", 1), ("fd",)]
        jobs += [("k", i) for i in range(4)] + [("ft",)] + [("kn", i) for i in range(4)]
        jobs += [("q", i) for i in range(4)] + [("qn", i) for i in range(4)]
        jobs += [("q", i) for i in range(4, 8)] + [("qn", i) for i in range(4, 8)]
        jobs += [("v", i) for i in range(4)]
        jobs += [("kt", a) for a in range(3)] + [("vt", a) for a in range(3)]
        for c in range(8):
            jobs += [("s", c, 0), ("s", c, 1), ("xbc", 3 * c), ("sc", c, 0), ("sc", c, 1), ("sk", c, 0), ("sk", c, 1),
                     ("xbc", 3 * c + 1), ("ss", c), ("xbc", 3 * c + 2),
                     ("pt", c, 0), ("pt", c, 1), ("o2", c)]
            if c % 2:
                jobs += [("mod", 2 + c // 2), ("modt", 2 + c // 2)]
        jobs += [("sp",), ("so", 0), ("sx", 0)] + [("z", i) for i in range(4)] + [("so", 1), ("sx", 1)]
        jobs += [("bs", 0), ("bs", 1), ("exp",)]
        jobs += [("bt", a) for a in range(2)]
        fill = {(0, 1): [("z", 4)], (0, 2): [("z", 5)], (0, 3): [("z", 6), ("ct", 0)], (0, 4): [("z", 7), ("ct", 1)],
                (0, 5): [("z", 8), ("ct", 2)], (0, 6): [("z", 9), ("ct", 3)], (0, 7): [("z", 10)], (1, 0): [("z", 11)],
                (1, 1): [("z", 12)], (1, 2): [("ct", 4)], (1, 3): [("z", 13)], (1, 4): [("z", 14)], (1, 5): [("ct", 5)],
                (1, 6): [("z", 15)]}
        for a in range(2):
            jobs += [("xs", a, g) for g in range(4)]
            if a == 1:
                jobs += [("s1", g) for g in range(4)]
            jobs += [("cb", a)]
            for b in range(8):
                jobs += [("ab", a, b)] + fill.get((a, b), [])
                if b >= 2:
                    jobs += [("y", a, b - 2)]
            jobs += [("y", a, 6), ("y", a, 7)]
        jobs += [("fs", i) for i in range(4)]
        merge = [("g", i) for i in range(16)] + [("pa", i) for i in range(8)]
        for g in range(SG):
            merge.insert(1 + 3 * g, ("yp", g))
        for i, j in enumerate(merge):
            if i % 3 == 2 and i // 3 < NS:
                jobs += [("ssm", i // 3)]
            jobs += [j]
        jobs += [("yn",)]
        jobs += [("pb", i) for i in range(8)] + [("o", i) for i in range(8)]
        jobs += [("ssq", 1), ("lr",), ("lt",)] + [("ht", a, f) for a in range(3) for f in range(2)] + [("rk",)]
        late = [("yt", a, f) for f in range(2) for a in range(3)]
        NOBANK = {"ss", "ssm", "sc"}

        bank_of, at_bank = {}, [0] * NBANK
        for n, j in enumerate([j for j in jobs + late if j[0] not in NOBANK]):
            b = n % NBANK
            at_bank[b] += 1
            bank_of[j] = (b, at_bank[b])
        at_moe = [0] * NBANK
        for j in jobs:
            if j in bank_of:
                at_moe[bank_of[j][0]] += 1
        bank_filled = [sem(f"bank_filled{i}") for i in range(NBANK)]
        bank_read = [sem(f"bank_read{i}") for i in range(NBANK)]

        def slots_of(j):
            k = j[0]
            if k == "mod":
                return [("mod", 4 * j[1] + i) for i in range(4)]
            if k in ("q", "k", "v", "xbc", "z", "g"):
                base = {"q": 0, "k": COL_K, "v": COL_V, "xbc": COL_X, "z": COL_Z, "g": COL_G}[k]
                return [("in", base + SW * (j[1] // 2))]
            if k in ("pa", "o"):
                return [(k, j[1] // 2)]
            if k == "pb":
                return [(k, j[1] // 2, 0), (k, j[1] // 2, 1)]
            return []

        loads, last_user = [], {}
        for j in jobs:
            for s in slots_of(j):
                if s not in last_user:
                    loads.append(s)
                last_user[s] = j
        narrow = range(jobs.index(("z", 0)), jobs.index(("y", 1, 7)) + 1)
        slot_at, slot_count, arrived_at, held_by, before = {}, [0] * NSLOT, {}, {}, {}
        z_over = {}
        order = list(range(NSLOT))
        for s in loads:
            user = min(i for i, j in enumerate(jobs) if s in slots_of(j))
            r = next(r for r in order if r < 4 or user not in narrow)
            order = [i for i in order if i != r] + [r]
            if user in narrow:
                order = [i for i in order if i < 4] + [4, 5]
            slot_count[r] += 16 * (4 if s[0] == "pa" else 4 if s[0] == "in" and s[1] < D else 1)
            slot_at[s], arrived_at[s] = r, slot_count[r]
            before[s] = held_by.get(r)
            if r >= 4 and user < narrow[0]:
                z_over[r] = s
            held_by[r] = s
        slot_full = [sem(f"slot_full{i}") for i in range(NSLOT)]

        def slot(s):
            r = slot_at[s]
            return ring[:, r * SLOT:(r + 1) * SLOT].rearrange("p (k n) -> p k n", k=KD)

        small_in = sem("conditions_and_vectors_landed")
        x_in = sem("x_landed")
        st_in = sem("conv_states_landed")
        late_in = sem("small_weights_landed")
        pt_in = sem("page_table_landed")
        lf_in = sem("cached_logf_landed")
        consts = sem("constants_built")
        cond_ready = sem("condition_silu_done")
        sq_ready = sem("x_squared")
        hs_ready = sem("h_scaled")
        h_ready = sem("h_prompt_block_ready")
        h_samples = sem("h_samples_ready")
        fd_exp = sem("exp_of_head_logits")
        fd_sp = sem("dt_logf_and_sums_ready")
        fd_e = sem("head_decays_ready")
        lfn_ready = sem("new_logf_spread")
        qk_sq = sem("qk_squared")
        qk_ready = sem("qk_normed")
        qbd_zero = sem("sample_queries_zeroed")
        qbd_ready = sem("sample_queries_placed")
        s_max = sem("scores_and_max_ready")
        s_exp = sem("scores_exponentiated")
        p_ready = sem("probs_ready")
        kcol_ready = sem("new_key_placed")
        ss_done = sem("sample_scores_summed")
        ss_max = sem("sample_max_ready")
        ss_exp = sem("sample_scores_exponentiated")
        sp_ready = sem("sample_probs_ready")
        conv_ready = sem("conv_summed")
        u_ready = sem("conv_silu_done")
        bs_out = sem("sample_bc_rows_stored")
        xds_ready = sem("sample_x_dt_ready")
        xe_ready = sem("decayed_xd_ready")
        seg_exp = sem("segment_decays_ready")
        et_ready = sem("exp_of_sums_ready")
        w_ready = sem("weighted_cb_ready")
        ce_ready = sem("decayed_c_ready")
        zg_done = sem("z_gate_applied")
        yp_sq = sem("y_prompt_squared")
        y_sq = sem("y_samples_squared")
        y_ready = sem("y_normed")
        m_ready = sem("branches_merged")
        bc_full = [sem(f"sample_bc_rows_landed{i}") for i in range(2)]
        bx_ready = sem("sample_x_dt_b_ready")
        st_new = sem("state_updated")
        st_prod = sem("state_times_c_ready")
        st_red = sem("state_times_c_summed")
        o_small = sem("small_outputs_stored")
        o_k = sem("k_stored")
        o_tail = sem("conv_states_stored")
        o_y = sem("y_stored")
        asg_ready = sem("assignment_ready")
        rk_exp = sem("router_exp_ready")
        rk_ready = sem("ranks_ready")
        rk_shift = sem("ranks_shifted")
        sel_ready = sem("selection_ready")
        selw_ready = sem("weighted_selection_ready")
        gath_filled = sem("gathered_bank_filled")
        selT_done = sem("selection_transposed")
        selT_ready = sem("selection_T_copied")
        xg_ready = sem("gathered_copied")
        gate_done = sem("gate_product_done")
        up_done = sem("up_product_done")
        silu_ready = sem("gate_silu_ready")
        act_ready = sem("expert_act_ready")
        actT_done = sem("expert_act_transposed")
        actT_ready = sem("expert_act_T_copied")
        down_done = sem("down_product_done")
        out_ready = sem("expert_out_copied")
        comb_filled = sem("combined_bank_filled")
        comb_read = sem("combined_bank_read")
        yfin = sem("y_final_ready")
        y_zero = sem("expert_sum_zeroed")
        dve_step = sem("dve_step")
        act_step = sem("act_step")
        pool_step = sem("pool_step")
        kv_full = [sem(f"cache_page_landed{i}") for i in range(4)]
        st_full = [sem(f"state_landed{i}") for i in range(2)]
        st_out = [sem(f"state_stored{i}") for i in range(2)]
        o_fs = sem("ssm_prompt_stored")
        moe_full = [sem(f"expert_matrix_landed{i}") for i in range(6)]

        def stepper(eng, own):
            n = {}

            def link(ins, s=own):
                n[s.name] = n.get(s.name, 0) + 1
                ins.then_inc(s, 1)
                eng.wait_ge(s, n[s.name])
            return link

        def filled(eng, j):
            b, n = bank_of[j]
            eng.wait_ge(bank_filled[b], n)
            return banks[b]

        def release(eng, ins, j):
            b, n = bank_of[j]
            ins.then_inc(bank_read[b], 1)
            eng.wait_ge(bank_read[b], n)

        def read_out(eng, j):
            b, n = bank_of[j]
            eng.wait_ge(bank_read[b], n)

        wmod = t["w_mod"].rearrange("o (k p) n -> p (o k) n", p=128)
        win = t["w_in"].rearrange("o (k p) n -> p (o k) n", p=128)
        wpa = t["w_pa"].rearrange("o (m h s d) n -> (o h) s d m n", h=2, s=2, d=HD)
        wpb = t["w_pb"].rearrange("o (k p) n -> p (o k) n", p=128)
        wo = t["w_o"].rearrange("o (k p) n -> p (o k) n", p=128)
        wg = t["w_gate"].rearrange("o e (k p) n -> (o e) p k n", p=128)
        wu = t["w_up"].rearrange("o e (k p) n -> (o e) p k n", p=128)
        wdn = t["w_down"].rearrange("o e (k p) n -> (o e) p k n", p=128)
        ck = t["cache_k"].rearrange("o g k h d -> (o g) k (h d)")
        cv = t["cache_v"].rearrange("o g k h d -> (o g) k (h d)")
        clf = t["cache_logf"].rearrange("o g k h -> (o g) k h")
        st_d = t["state_ssm"].rearrange("o b (c h) p n -> (o b) (h p) c n", h=2)
        so_d = t["ssm_sample"].rearrange("o b (c h) p n -> (o b) (h p) c n", h=2)
        fs_d = t["ssm_prompt"].rearrange("o b (c h) p n -> (o b) (h p) c n", h=2)
        bc_d = t["bc_scratch"]

        def down_slot(q):
            return mslot[4 + q].rearrange("p (e k n) -> p e k n", e=2, k=FF // 128)

        block = ctx.enter_context(nc.Block())

        @block.sync
        def _(sp):
            xp = t["x_prompt"].rearrange("o q d -> (o q) d")
            sp.dma_start(xin[:, 0, :], xp[0:128, :]).then_inc(x_in, 16)
            sp.dma_start(xin[:, 1, :], xp[128:256, :]).then_inc(x_in, 16)
            sp.dma_start(xin[0:NS, 2, :], t["x_sample"].rearrange("b o d -> (b o) d")).then_inc(x_in, 16)
            sp.dma_start(wfd[:, :, 0:SH], win[:, :, COL_DT:COL_DT + SH]).then_inc(late_in, 16)
            sp.dma_start(wfd[:, :, SH:HB], win[:, :, COL_F:COL_F + NH]).then_inc(late_in, 16)
            sp.dma_start(wr[:], t["w_router"].rearrange("(k p) e -> p k e", p=128)).then_inc(late_in, 16)
            for h in range(2):
                sp.dma_start(gqk[64 * h:64 * h + 64, 0:1], t["g_q"].rearrange("o d -> d o")).then_inc(late_in, 16)
                sp.dma_start(gqk[64 * h:64 * h + 64, 1:2], t["g_k"].rearrange("o d -> d o")).then_inc(late_in, 16)
            sp.dma_start(hcol[0:SH, 0:1], t["dt_bias"].rearrange("o d -> d o")).then_inc(late_in, 16)
            sp.dma_start(hcol[SH:HB, 0:1], t["b_f"].rearrange("o d -> d o")).then_inc(late_in, 16)
            sp.dma_start(hcol[0:SH, 1:2], t["a_log"].rearrange("o d -> d o")).then_inc(late_in, 16)
            sp.dma_start(hcol[0:SH, 2:3], t["d_skip"].rearrange("o d -> d o")).then_inc(late_in, 16)
            sp.dma_start(brow[:], t["b_router"].rearrange("(d o) -> d o", o=1)).then_inc(late_in, 16)
            sp.wait_ge(small_in, 16 * 8)
            stored = 0

            def store_states(n):
                nonlocal stored
                while stored < n:
                    sp.wait_ge(st_new, 2 * stored + 2)
                    sp.dma_start(so_d[stored], sst[stored % 2].rearrange("p (c n) -> p c n", c=NXB))\
                      .then_inc(st_out[stored % 2], 16)
                    stored += 1

            for s in loads:
                if s == ("pb", 0, 0):
                    store_states(NS - 2)
                    for i in range(2):
                        sp.wait_ge(st_full[i], 16 * (NS // 2))
                if before[s]:
                    done_jobs = jobs[:jobs.index(last_user[before[s]])]
                    store_states(sum(j[0] == "ssm" for j in done_jobs))
                    b, use = bank_of[last_user[before[s]]]
                    sp.wait_ge(bank_filled[b], use)
                    if z_over.get(slot_at[s]) == before[s]:
                        sp.wait_ge(zg_done, NXB // 2)
                r, dst, c0 = slot_at[s], slot(s), SW * s[1]
                if s[0] == "mod":
                    sp.dma_start(dst, wmod[:, :, c0:c0 + SW]).then_inc(slot_full[r], 16)
                elif s[0] == "in" and s[1] < D:
                    for q in range(2):
                        for h in range(2):
                            o, c = HD * (2 * q + h), s[1] + HD * (2 * h + q)
                            sp.dma_start(dst[:, :, o:o + HD], win[:, :, c:c + HD]).then_inc(slot_full[r], 16)
                elif s[0] == "in":
                    sp.dma_start(dst, win[:, :, s[1]:s[1] + SW]).then_inc(slot_full[r], 16)
                elif s[0] == "o":
                    sp.dma_start(dst, wo[:, :, c0:c0 + SW]).then_inc(slot_full[r], 16)
                elif s[0] == "pb":
                    sp.dma_start(dst, wpb[:, KD * s[2]:KD * s[2] + KD, c0:c0 + SW]).then_inc(slot_full[r], 16)
                else:
                    dv = dst.rearrange("p (m s) n -> p s m n", s=2)
                    for h in range(2):
                        for q in range(2):
                            sp.dma_start(dv[64 * h:64 * h + 64, q], wpa[h, q, :, :, c0:c0 + SW])\
                              .then_inc(slot_full[r], 16)

            def load_expert(kind, e, j):
                s = 2 * kind + e
                if kind < 2:
                    sp.dma_start(mslot[s].rearrange("p (k n) -> p k n", k=KD), (wg, wu)[kind][2 * j + e])\
                      .then_inc(moe_full[s], 16)
                else:
                    for x in range(2):
                        sp.dma_start(down_slot(e)[:, x], wdn[2 * j + x][:, :, 512 * e:512 * e + 512])\
                          .then_inc(moe_full[s], 16)

            def experts(it, j):
                for kind in range(3):
                    sp.wait_ge((gate_done, up_done, down_done)[kind], it * 2 + 1 if kind == 2 else it + 1)
                    for e in range(2):
                        load_expert(kind, e, j)

            store_states(NS)
            for i in range(2):
                sp.wait_ge(st_out[i], 16 * (NS // 2))
            sp.wait_ge(y_sq, 1)
            load_expert(0, 0, 0)
            load_expert(0, 1, 0)
            bk, use = bank_of[("pb", 7)]
            sp.wait_ge(bank_filled[bk], use)
            load_expert(1, 0, 0)
            bk, use = bank_of[("o", 7)]
            sp.wait_ge(bank_filled[bk], use)
            load_expert(1, 1, 0)
            load_expert(2, 0, 0)
            load_expert(2, 1, 0)
            with sp.Fori(1, NE // 2) as j:
                experts(j, j)
            sp.wait_ge(rk_ready, 1)
            rounds = sp.value_load(rounds_sb[0:1, 0:1], min_val=1, max_val=5)
            with sp.If(rounds > 1):
                with sp.Fori(1, rounds) as r:
                    with sp.Fori(0, NE // 2) as j:
                        experts(r * 8 + j, j)
            for j in late:
                a, f, (t0, n) = j[1], j[2], TOK[j[1]]
                read_out(sp, j)
                dst = t["y_prompt"].rearrange("o q d -> (o q) d")[t0:t0 + n] if a < 2 else \
                    t["y_sample"].rearrange("b o d -> (b o) d")
                sp.dma_start(dst[:, 512 * f:512 * f + 512], yout[0:n, a, 512 * f:512 * f + 512]).then_inc(o_y, 16)
            sp.wait_ge(o_y, 16 * 6)
            sp.wait_ge(o_fs, 64)
            sp.wait_ge(o_small, 16 * 5)
            sp.wait_ge(o_k, 48)
            sp.wait_ge(o_tail, 16 * 12)

        @block.gpsimd
        def _(pool):
            link = stepper(pool, pool_step)
            g = nc.gpsimd
            link(g.memset(ident[:], 0.0))
            link(g.affine_select(out=ident[:], in_=ident[:], compare_op=ALU.not_equal, fill=1.0, base=0,
                                 pattern=[[-1, 128]], channel_multiplier=1), consts)
            link(g.memset(cT[:], 0.0), consts)
            link(g.memset(onesf[:], 1.0))
            link(g.memset(epsc[:], EPS))
            link(g.memset(blk[:], 0.0))
            link(g.memset(blk[0:64, 0:64], 1.0))
            link(g.memset(blk[64:128, 64:128], 1.0), consts)
            link(g.memset(qbd[:], 0.0), qbd_zero)
            link(g.memset(ntri[:], -1.0))
            link(g.affine_select(out=ntri[:], in_=ntri[:], compare_op=ALU.is_ge, fill=0.0, base=-128,
                                 pattern=[[1, 385]], channel_multiplier=-1))
            link(g.memset(cmask[:], 0.0))
            for o in (0, 256):
                link(g.affine_select(out=cmask[:, o:o + 128], in_=cmask[:, o:o + 128], compare_op=ALU.is_ge,
                                     fill=-1e30, base=0, pattern=[[-1, 128]], channel_multiplier=1))
            link(g.affine_select(out=triu[:], in_=onesf[:], compare_op=ALU.is_ge, fill=0.0, base=0,
                                 pattern=[[1, 128]], channel_multiplier=-1))
            link(g.affine_select(out=bm8[:].rearrange("p (b h) -> p b h", h=NH),
                                 in_=onesf[0:NS, :].rearrange("p (b h) -> p b h", h=NH),
                                 compare_op=ALU.is_equal, fill=0.0, base=0,
                                 pattern=[[1, NS], [0, NH]], channel_multiplier=-1))
            link(g.affine_select(out=bm2[:], in_=onesf[:, 0:NS], compare_op=ALU.is_ge, fill=0.0, base=0,
                                 pattern=[[-NH, NS]], channel_multiplier=1))
            link(g.affine_select(out=bm2[:], in_=bm2[:], compare_op=ALU.is_ge, fill=0.0, base=NH - 1,
                                 pattern=[[NH, NS]], channel_multiplier=-1))
            link(g.memset(onesb[:], 1.0))
            link(g.affine_select(out=striu[:], in_=onesb[:], compare_op=ALU.is_ge, fill=0.0, base=-1,
                                 pattern=[[1, 128]], channel_multiplier=-1))
            link(g.iota(iota[:], pattern=[[1, BLK]], base=0, channel_multiplier=0,
                        allow_small_or_imprecise_dtypes=True))
            link(g.iota(w4[:], pattern=[[-1, 4]], base=4, channel_multiplier=0,
                        allow_small_or_imprecise_dtypes=True))
            link(g.iota(thr[:], pattern=[[BLK, 4]], base=BLK, channel_multiplier=0,
                        allow_small_or_imprecise_dtypes=True))
            link(g.memset(xa[:, :, 0:3], 0.0))
            link(g.memset(psT[:], 0.0))
            link(g.memset(pn[:], 0.0), consts)

            pool.wait_ge(pt_in, 16)

            def page(i):
                return pool.value_load(pgs[0:1, bass.ds(i, 1)], min_val=0, max_val=ck.shape[0] - 1)

            with pool.Fori(0, NS) as b:
                for q in range(NPG):
                    pool.dma_start(lfc[:, q, bass.ds(b * NH, NH)], clf[page(b * NPG + q)]).then_inc(lf_in, 16)
            bk, use = bank_of[("xt", 2, 1)]
            pool.wait_ge(bank_filled[bk], use)
            for kind, cache in enumerate((ck, cv)):
                for b in range(NS):
                    if kind == 1 or b >= 4:
                        bk, use = bank_of[("sk", b - 4, 1) if kind == 0 else ("sk", b + 4, 1) if b < 4 else ("so", 0)]
                        pool.wait_ge(bank_filled[bk], use)
                    with pool.Fori(0, NPG) as q:
                        pool.dma_start(kvr[:, b % 4, bass.ds(q, 1), :].rearrange("p o f -> p (o f)"),
                                       cache[page(q + b * NPG)]).then_inc(kv_full[b % 4], 16)

            for a in range(2):
                read_out(pool, ("xs", a, 3))
                e = tokc[:, (4 + a) * 32:(5 + a) * 32]
                link(g.tensor_tensor(xe[:, a, :].rearrange("p (h d) -> p h d", d=HD),
                                     xd[:, a, :].rearrange("p (h d) -> p h d", d=HD),
                                     e.unsqueeze(2).to_broadcast([128, SH, HD]), ALU.mult), xe_ready)
            bk, use = bank_of[("s1", 3)]
            pool.wait_ge(bank_filled[bk], use)
            x3 = xe[:, 0, :].rearrange("p (h d) -> p h d", d=HD)
            link(g.tensor_tensor(x3, x3, tokc[:, 192:224].unsqueeze(2).to_broadcast([128, SH, HD]), ALU.mult), xe_ready)
            for b in range(8):
                pool.wait_ge(et_ready, b + 1)
                c3 = ce[:, b % 3, :].rearrange("p (h k) -> p h k", h=4)
                cv3 = u[:, 20 + b // 2, 128:256].unsqueeze(1).to_broadcast([128, 4, 128])
                link(g.tensor_tensor(c3, c3, cv3, ALU.mult), ce_ready)

            pool.wait_ge(bs_out, 16)
            pool.wait_ge(xds_ready, 1)

            def load_state(b):
                if b >= 2:
                    pool.wait_ge(st_prod, b - 1)
                pool.dma_start(bc[b % 2], bc_d[b:b + 1, :].to_broadcast([128, 2 * SG * NST]))\
                    .then_inc(bc_full[b % 2], 16)
                if b >= 2:
                    pool.wait_ge(st_out[b % 2], 16 * (b // 2))
                pool.dma_start(sst[b % 2].rearrange("p (c n) -> p c n", c=NXB), st_d[b]).then_inc(st_full[b % 2], 16)

            for b, j in enumerate((("y", 1, 7), ("fs", 3))):
                bk, use = bank_of[j]
                pool.wait_ge(bank_filled[bk], use)
                load_state(b)
            for b in range(NS):
                pool.wait_ge(st_new, 2 * b + 2)
                if b:
                    pool.wait_ge(st_red, b)
                s4 = sst[b % 2].rearrange("p (g c n) -> p g c n", g=SG, c=4)
                p4 = prod.rearrange("p (g c n) -> p g c n", g=SG, c=4)
                for q in range(SG):
                    cr = bc[b % 2][:, (SG + q) * NST:(SG + q + 1) * NST]
                    ins = g.tensor_tensor(p4[:, q], s4[:, q], cr.unsqueeze(1).to_broadcast([128, 4, NST]), ALU.mult)
                ins.then_inc(st_prod, 1)
                if b + 2 < NS:
                    load_state(b + 2)
            bk, use = bank_of[("pa", 7)]
            pool.wait_ge(bank_filled[bk], use)
            g.memset(Y[:], 0.0).then_inc(y_zero, 1)

        @block.scalar
        def _(act):
            link = stepper(act, act_step)
            fn = nc.scalar.activation
            act.sem_inc(silu_ready, 1)
            act.dma_start(crow[0:NS, :], t["c_sample"]).then_inc(small_in, 16)
            act.dma_start(crow[NS:NC, :], t["c_prompt"]).then_inc(small_in, 16)
            o = 0
            for name, n in (("b_mod", 48), ("g_norm1", 8), ("g_norm2", 8), ("g_ssm", 16), ("conv_b", 24)):
                act.dma_start(vrow[o:o + n, 0, :], t[name].rearrange("o (k p) -> (o k) p", p=128)).then_inc(small_in, 16)
                o += n
            act.dma_start(vrow[0:96, 1, :], t["conv_w"].rearrange("o w (k p) -> (o w k) p", p=128)).then_inc(small_in, 16)
            act.dma_start(csin[0:24, :], t["state_conv"].rearrange("o b w c -> (o b w) c")).then_inc(st_in, 16)
            act.dma_start(pgs[:], t["page_table"].rearrange("(o b) g -> o (b g)", o=1)).then_inc(pt_in, 16)
            act.wait_ge(small_in, 16 * 8)
            link(fn(crow[0:NC, :], crow[0:NC, :], ACT.Silu), cond_ready)

            def shifted(i):
                for c in range(KD):
                    act.wait_ge(hs_ready, KD * i + c + 1)
                    fn(hT[:, c, 0:NP], u[:, c, 0:NP], ACT.Identity, bias=modT[:, 24 * i + c, NS:NC]).then_inc(h_ready, 1)

            def conv_silu(i):
                act.wait_ge(conv_ready, i + 1)
                link(fn(u[:, i, 0:NP], cacc[:, i % 2, 0:NP], ACT.Silu))
                link(fn(u[:, i, NP:T], cacc[:, i % 2, NP + 3:XO:4], ACT.Silu), u_ready)

            for j in jobs:
                k = j[0]
                if k == "sp":
                    conv_silu(NCB - 1)
                    act.wait_ge(ss_max, 1)
                    link(fn(ps_s, sbank[:, 0:257], ACT.Exp, bias=sm2[:, 8:9], accum_out=sm2[:, 9:10]), ss_exp)
                if k == "lt":
                    act.wait_ge(asg_ready, 1)
                    link(fn(lg, lg, ACT.Exp), rk_exp)
                ps = filled(act, j) if k in ("mod", "ssq", "q", "k", "qn", "kn", "v", "kt", "vt", "pt", "o2", "xbc",
                                             "sk", "sp", "so", "ct", "bs", "bt", "s1", "fs", "z", "g", "yp", "yn",
                                             "ht") else None
                if k == "mod":
                    release(act, fn(mrow[:], ps[:, 0:SW], ACT.Copy), j)
                elif k == "ssq":
                    act.wait_ge(consts, 3)
                    release(act, fn(rs[:, 0, :], ps[:, 0:T], ACT.Sqrt, bias=epsc[:], scale=1.0 / D), j)
                    if j[1] == 1:
                        shifted(1)
                        link(fn(sm2[:, 24:25], epsc[:], ACT.Exp))
                elif k == "fd":
                    shifted(0)
                    read_out(act, j)
                    link(fn(fdw[:, 0, :], fd[:], ACT.Abs))
                    link(fn(hcol[0:SH, 1:2], hcol[0:SH, 1:2], ACT.Exp))
                    link(fn(fdw[:, 0, :], fdw[:, 0, :], ACT.Exp, scale=-1.0), fd_exp)
                    act.wait_ge(fd_sp, 1)
                    for c in range(2):
                        cols = slice(128 * c, 128 * c + 128)
                        link(fn(fdw[0:SH, 1, cols], acsT[0:SH, cols], ACT.Exp,
                                bias=acsT[0:SH, 128 * c + 127:128 * c + 128], scale=-1.0))
                    link(fn(fdw[0:SH, 2, 0:128], fdw[0:SH, 2, 0:128], ACT.Exp))
                    link(fn(ex[:, NS:2 * NS], ex[:, NS:2 * NS], ACT.Exp), fd_e)
                elif k == "ft":
                    read_out(act, j)
                    act.dma_start(t["logf_prompt"].rearrange("o b (a p) h -> p (o b a) h", p=128),
                                  lft[:, 0:2, :]).then_inc(o_small, 16)
                    act.dma_start(t["logf_sample"].rearrange("o b q h -> (o b q) h"), lft[0:NS, 2, :])\
                       .then_inc(o_small, 16)
                elif k in ("q", "k"):
                    release(act, fn(qkT[:, j[1] + (8 if k == "k" else 0), :], ps[:, 0:T], ACT.Copy), j)
                elif k in ("qn", "kn"):
                    if k == "qn":
                        act.wait_ge(qk_ready, 1 + j[1] // 4)
                    release(act, fn(rs[:, j[1] % 4, :], ps[:, 0:T], ACT.Sqrt, bias=epsc[:], scale=1.0 / HD), j)
                elif k == "v":
                    release(act, fn(vT[:, j[1], :], ps[:, 0:T], ACT.Copy), j)
                elif k in ("kt", "vt"):
                    a, (t0, n) = j[1], TOK[j[1]]
                    o, kind = (ktok[0:n, :], "k") if k == "kt" else (vtok[0:n, a, :], "v")
                    if k == "kt" and a:
                        act.wait_ge(o_k, 16 * a)
                    release(act, fn(o, ps[0:n, :], ACT.Copy), j)
                    dst = t[f"{kind}_prompt" if a < 2 else f"{kind}_sample"].rearrange("o b q h d -> (o b q) (h d)")
                    act.dma_start(dst[t0:t0 + n, :] if a < 2 else dst, o).then_inc(o_k if k == "kt" else o_small, 16)
                elif k == "s":
                    p = j[2]
                    act.wait_ge(s_max, 2 * j[1] + p + 1)
                    for q, (lo, hi) in enumerate(((0, 128), (128, 384))):
                        link(fn(pb[:, p, lo:hi], pb[:, p, lo:hi], ACT.Exp, bias=sm2[:, 4 * p + q:4 * p + q + 1],
                                accum_out=sm2[:, 4 * p + 2 + q:4 * p + 3 + q]), s_exp if q else act_step)
                elif k == "pt":
                    release(act, fn(pT[:, j[2], :], ps[:, 0:384], ACT.Copy), j)
                elif k == "o2":
                    release(act, fn(attT[:, j[1], 0:NP], ps[:, 0:NP], ACT.Copy), j)
                elif k == "xbc":
                    i = j[1]
                    if i >= 2:
                        act.wait_ge(conv_ready, i - 1)
                    link(fn(xa[:, i % 2, 3:3 + NP], ps[:, 0:NP], ACT.Copy))
                    release(act, fn(xa[:, i % 2, 3 + NP + 3:XW:4], ps[:, NP:T], ACT.Copy), j)
                    if i:
                        conv_silu(i - 1)
                elif k == "sk":
                    b, q = j[1], j[2]
                    release(act, fn(ktb[:, b % 2, :, 128 * q:128 * q + 128],
                                    ps.rearrange("p (m k) -> p m k", m=4), ACT.Copy), j)
                elif k == "sp":
                    for q in range(NPG):
                        link(fn(psT[:, q, 0:128], ps[:, 128 * q:128 * q + 128], ACT.Copy))
                    release(act, fn(pn[0:NS, 0:128], ps[0:NS, 256:384], ACT.Copy), j)
                elif k == "so":
                    act.wait_ge(o_k, 48)
                    release(act, fn(otok[:], ps[:], ACT.Copy), j)
                elif k == "ct":
                    i = j[1]
                    if i:
                        act.wait_ge(o_tail, 32 * i)
                    release(act, fn(ctok[0:27, :], ps[0:27, :], ACT.Copy), j)
                    act.dma_start(t["conv_sample"].rearrange("o b w c -> (o b w) c")[:, 512 * i:512 * i + 512],
                                  ctok[0:24, :]).then_inc(o_tail, 16)
                    act.dma_start(t["conv_prompt"].rearrange("o b w c -> (o b w) c")[:, 512 * i:512 * i + 512],
                                  ctok[24:27, :]).then_inc(o_tail, 16)
                elif k == "bs":
                    release(act, fn(wdf[0:NS, 512 * j[1]:512 * j[1] + 512], ps[0:NS, :], ACT.Copy), j)
                    if j[1]:
                        act.dma_start(bc_d, wdf[0:NS, 0:2 * SG * NST]).then_inc(bs_out, 16)
                elif k == "bt":
                    release(act, fn(btok[:, j[1], :], ps[:], ACT.Copy), j)
                elif k == "s1":
                    release(act, fn(s1T[:, 512 * j[1]:512 * j[1] + 512], ps[:], ACT.Copy), j)
                elif k == "ab":
                    a, b = j[1], j[2]
                    if a == 1:
                        filled(act, j)
                        if b >= 3:
                            filled(act, ("y", 1, b - 3))
                        link(fn(ce[:, b % 3, :], banks[bank_of[j][0]][:], ACT.Exp), et_ready)
                    read_out(act, j)
                    link(fn(wd[:, b % 3, :], wd[:, b % 3, :], ACT.Exp), seg_exp)
                elif k == "fs":
                    i = j[1]
                    release(act, fn(fso[:, i, :], ps[:], ACT.Copy), j)
                    act.dma_start(fs_d[0, :, 4 * i:4 * i + 4, :], fso[:, i, :].rearrange("p (c n) -> p c n", c=4))\
                       .then_inc(o_fs, 16)
                elif k == "z":
                    i = j[1]
                    if i == 0:
                        for w in z_over.values():
                            filled(act, last_user[w])
                    link(fn(zb[:, i, :], ps[:, 0:NP], ACT.Silu))
                    release(act, fn(zsS[:, i, :], ps[:, NP:T], ACT.Silu), j)
                elif k == "ssm":
                    b = j[1]
                    if b == 0:
                        filled(act, ("fs", 3))
                    act.wait_ge(bc_full[b % 2], 16 * (b // 2 + 1))
                    for c in range(NXB):
                        if b and c % 8 == 0:
                            act.wait_ge(st_new, 2 * b - 1 + c // 8)
                        ins = fn(bx[:, NST * c:NST * c + NST], bc[b % 2][:, NST * (c // 4):NST * (c // 4) + NST], ACT.Copy,
                                 scale=exo[:, c, b:b + 1])
                        if c % 8 == 7:
                            ins.then_inc(bx_ready, 1)
                elif k == "g":
                    if j[1] == 8:
                        act.wait_ge(o_fs, 64)
                    release(act, fn(gT[:, j[1], :], ps[:, 0:T], ACT.Sigmoid), j)
                elif k == "yp":
                    release(act, fn(rs[:, j[1], 0:NP], ps[:, 0:NP], ACT.Sqrt, bias=epsc[:], scale=SG / DI), j)
                elif k == "yn":
                    release(act, fn(sm2[:, 32:64], ps[:, 0:32], ACT.Sqrt, bias=epsc[:], scale=SG / DI), j)
                elif k == "ht":
                    a, f, n = j[1], j[2], TOK[j[1]][1]
                    release(act, fn(h2tok[0:n, a, 512 * f:512 * f + 512], ps[0:n, :], ACT.Copy), j)

            def pair(it, t, p):
                act.wait_ge(gate_done, it + 2)
                act.wait_ge(act_ready, it + 1)
                fn(gact, banks[0][:], ACT.Silu).then_inc(silu_ready, 1)
                if p == 0:
                    act.wait_ge(selT_done, t + 2)
                    fn(selT[:, 0, :], banks[2][:, 0:T], ACT.Copy)
                    fn(selT[:, 1, :], banks[3][:, 0:T], ACT.Copy).then_inc(selT_ready, 1)
                act.wait_ge(actT_done, it + 1)
                fn(aT.rearrange("p k s -> p (k s)"), banks[4][:], ACT.Copy).then_inc(actT_ready, 1)
                for q in range(2):
                    act.wait_ge(down_done, it * 2 + (q + 2))
                    fn(outs[:, 512 * q:512 * q + 512], banks[2 + q][:], ACT.Copy).then_inc(out_ready, 1)

            act.wait_ge(rk_ready, 1)
            rounds = act.value_load(rounds_sb[0:1, 0:1], min_val=1, max_val=5)
            with act.Fori(0, rounds) as r:
                with act.Fori(0, NE // 4) as q:
                    for p in range(2):
                        pair(r * 8 + (q * 2 + p), r * 4 + q, p)
            for j in late:
                ps, (a, f), n = filled(act, j), j[1:], TOK[j[1]][1]
                release(act, fn(yout[0:n, a, 512 * f:512 * f + 512], ps[0:n, :], ACT.Copy), j)

        @block.vector
        def _(dve):
            link = stepper(dve, dve_step)
            v = nc.vector
            for s in (act_ready, comb_read, rk_shift):
                dve.sem_inc(s, 1)
            dve.sem_inc(xg_ready, 2)
            norm_of = ((48, 8, 0), (56, 32, 24))

            def square(c):
                v.tensor_tensor(u[:, c, :], xT[:, c, :], xT[:, c, :], ALU.mult).then_inc(sq_ready, 1)

            def normed(i):
                gv, sc, sh = norm_of[i]
                link(v.scalar_tensor_tensor(gsc[:], modT[:, sc:sc + KD, :], 1.0,
                                            vec[:, gv:gv + KD].unsqueeze(2).to_broadcast([128, KD, NC]),
                                            ALU.add, ALU.mult))
                for c in range(KD):
                    v.scalar_tensor_tensor(u[:, c, 0:NP], xT[:, c, 0:NP], gsc[:, c, NS:NC], rs[:, 0, 0:NP],
                                           ALU.mult, ALU.mult).then_inc(hs_ready, 1)
                hs = hT[:, :, NP:T]
                link(v.tensor_tensor(hs, xT[:, :, NP:T], gsc[:, :, 0:NS], ALU.mult))
                link(v.tensor_tensor(hs, hs, rs[:, 0:1, NP:T].to_broadcast([128, KD, NS]), ALU.mult))
                link(v.tensor_tensor(hs, hs, modT[:, sh:sh + KD, 0:NS], ALU.add), h_samples)

            def weigh(a, b):
                dve.wait_ge(seg_exp, 8 * a + b + 1)
                w3 = wd[:, b % 3, :].rearrange("p (h k) -> p h k", h=4)
                link(v.tensor_tensor(w3, w3, cbm[:, b // 2:b // 2 + 1, :].to_broadcast([128, 4, 128]), ALU.mult), w_ready)

            def state_sum(b):
                dve.wait_ge(st_prod, b + 1)
                link(v.tensor_reduce(yT[:, :, NP + b], prod.rearrange("p (c n) -> p c n", c=NXB), AX.X, ALU.add), st_red)

            def first_max(src, m, best, tmp):
                m3 = m.unsqueeze(2).to_broadcast([128, 3, 4])
                link(v.tensor_reduce(m, src, AX.X, ALU.max))
                link(v.tensor_tensor(best, src, m3, ALU.is_equal))
                link(v.tensor_tensor(best, best, w4[:].unsqueeze(1).to_broadcast([128, 3, 4]), ALU.mult))
                link(v.tensor_reduce(tmp, best, AX.X, ALU.max))
                link(v.tensor_tensor(best, best, tmp.unsqueeze(2).to_broadcast([128, 3, 4]), ALU.is_equal))

            def route():
                m16 = rw[0].unsqueeze(2).to_broadcast([128, 3, NE])
                link(v.tensor_reduce(rw[0], lg, AX.X, ALU.max))
                link(v.tensor_tensor(lg, lg, m16, ALU.subtract), asg_ready)
                dve.wait_ge(rk_exp, 1)
                link(v.tensor_reduce(rw[1], lg, AX.X, ALU.add))
                link(v.reciprocal(rw[1], rw[1]))
                link(v.tensor_tensor(lg, lg, rw[1].unsqueeze(2).to_broadcast([128, 3, NE]), ALU.mult))
                lg4 = lg.rearrange("p a (g e) -> p a g e", g=NG)
                gm, og, pin, o1, o2, we = rt[0], rt[1], rt[2], rt[3], rt[4], rt[5]
                link(v.tensor_reduce(gm, lg4, AX.X, ALU.max))
                first_max(gm, rw[2], og, rw[3])
                pg4 = prg.rearrange("p a (g e) -> p a g e", g=NG)
                og4 = og.unsqueeze(3).to_broadcast([128, 3, NG, EPG])
                link(v.tensor_tensor(pg4, lg4, og4, ALU.mult))
                link(v.tensor_reduce(pin, prg.rearrange("p a (g e) -> p a e g", g=NG), AX.X, ALU.add))
                first_max(pin, rw[4], o1, rw[3])
                link(v.scalar_tensor_tensor(pin, o1, -4.0, pin, ALU.mult, ALU.add))
                first_max(pin, rw[5], o2, rw[3])
                link(v.tensor_tensor(rw[6], rw[4], rw[5], ALU.add))
                link(v.reciprocal(rw[6], rw[6]))
                link(v.tensor_tensor(rw[4], rw[4], rw[6], ALU.mult))
                link(v.tensor_tensor(rw[5], rw[5], rw[6], ALU.mult))
                link(v.tensor_tensor(we, o1, rw[4].unsqueeze(2).to_broadcast([128, 3, 4]), ALU.mult))
                link(v.tensor_tensor(pin, o2, rw[5].unsqueeze(2).to_broadcast([128, 3, 4]), ALU.mult))
                link(v.tensor_tensor(we, we, pin, ALU.add))
                link(v.tensor_tensor(o1, o1, o2, ALU.add))
                for dst, e4 in ((asg, o1), (cmb, we)):
                    if dst is cmb:
                        link(v.tensor_copy(asb[:], asg), asg_ready)
                    for a in range(3):
                        link(v.tensor_tensor(dst[:, a, :].rearrange("p (g e) -> p g e", g=NG),
                                             og[:, a, :].unsqueeze(2).to_broadcast([128, NG, EPG]),
                                             e4[:, a, :].unsqueeze(1).to_broadcast([128, NG, EPG]), ALU.mult))

            for j in jobs:
                k = j[0]
                if k == "cT":
                    ps = filled(dve, j)
                    dve.wait_ge(consts, 2)
                    release(dve, v.tensor_copy(cT[:, :, 0:NC], ps[:, 0:KD * NC].rearrange("p (k c) -> p k c", k=KD)), j)
                elif k == "vecs":
                    ps = filled(dve, j)
                    release(dve, v.tensor_copy(vec[:], ps[:, 0:200]), j)
                elif k == "modt":
                    ps, o = filled(dve, j), KD * j[1]
                    for q in range(2):
                        ins = v.tensor_tensor(modT[:, o + q:o + KD:2, :],
                                              ps[:, 128 * q:128 * q + 128].rearrange("p (i c) -> p i c", i=4)[:, :, 0:NC],
                                              vec[:, o + q:o + KD:2].unsqueeze(2).to_broadcast([128, 4, NC]), ALU.add)
                        if q:
                            release(dve, ins, j)
                        else:
                            link(ins)
                    if j[1] == 1:
                        normed(0)
                elif k == "xt":
                    ps, a, f, (t0, n) = filled(dve, j), j[1], j[2], TOK[j[1]]
                    release(dve, v.tensor_copy(xT[:, 4 * f:4 * f + 4, t0:t0 + n],
                                               ps[:, 0:4 * n].rearrange("p (q t) -> p q t", q=4)), j)
                    if a == 2 and f == 1:
                        for c in range(KD):
                            square(c)
                elif k == "ssq":
                    read_out(dve, j)
                    dve.wait_ge(sq_ready, KD * (j[1] + 1))
                    link(v.reciprocal(rs[:, 0, :], rs[:, 0, :]))
                    if j[1] == 1:
                        normed(1)
                elif k == "cst":
                    ps = filled(dve, j)
                    release(dve, v.tensor_copy(stT[:, 12 * j[1]:12 * j[1] + 12, :],
                                               ps[:, 0:288].rearrange("p (c s) -> p c s", c=12)), j)
                elif k == "fd":
                    ps = filled(dve, j)
                    dve.wait_ge(late_in, 16 * 12)
                    w0, w1, w2 = fdw[:, 0, :], fdw[:, 1, :], fdw[:, 2, :]
                    release(dve, v.tensor_scalar(fd[:], ps[0:HB, 0:T], hcol[:, 0:1], None, ALU.add), j)
                    link(v.tensor_scalar(gqk[:, 0:1], gqk[:, 0:1], HD ** -0.5, None, ALU.mult))
                    link(v.tensor_scalar(nident[:], ident[0:HB, 0:HB], -1.0, None, ALU.mult))
                    dve.wait_ge(fd_exp, 1)
                    link(v.tensor_scalar(w1, w0, 2.0, None, ALU.add))
                    link(v.reciprocal(w1, w1))
                    link(v.tensor_tensor(w0, w0, w1, ALU.mult))
                    link(v.tensor_tensor(w1, w0, w0, ALU.mult))
                    link(v.tensor_scalar(w2, w1, 1.0 / 15, None, ALU.mult))
                    for c in (13, 11, 9, 7, 5, 3):
                        link(v.scalar_tensor_tensor(w2, w2, 1.0 / c, w1, ALU.add, ALU.mult))
                    link(v.scalar_tensor_tensor(w2, w2, 1.0, w0, ALU.add, ALU.mult))
                    link(v.tensor_scalar(w1[0:SH], fd[0:SH, :], 0.0, None, ALU.max))
                    link(v.scalar_tensor_tensor(fd[0:SH, :], w2[0:SH], 2.0, w1[0:SH], ALU.mult, ALU.add))
                    link(v.tensor_scalar(w1[SH:HB], fd[SH:HB, :], 0.0, None, ALU.min))
                    link(v.scalar_tensor_tensor(fd[SH:HB, :], w2[SH:HB], -2.0, w1[SH:HB], ALU.mult, ALU.add))
                    link(v.tensor_scalar(hcol[0:SH, 1:2], hcol[0:SH, 1:2], -1.0, None, ALU.mult))
                    link(v.tensor_scalar(w0[0:SH], fd[0:SH, :], hcol[0:SH, 1:2], None, ALU.mult))
                    for c in range(2):
                        cols = slice(128 * c, 128 * c + 128)
                        link(v.tensor_tensor_scan(acsT[0:SH, cols], onesf[0:SH, :], w0[0:SH, cols], 0.0,
                                                  ALU.mult, ALU.add))
                        link(v.tensor_tensor_scan(acsT[SH:HB, cols], onesf[SH:HB, :], fd[SH:HB, cols],
                                                  acsT[SH:HB, 127:128] if c else 0.0, ALU.mult, ALU.add))
                    link(v.tensor_scalar(w2[0:SH, 0:128], onesf[0:SH, :], acsT[0:SH, 255:256], None, ALU.mult))
                    link(v.tensor_copy(ex[:, 0:NS], fd[0:SH, NP:T]))
                    link(v.tensor_copy(ex[:, 2 * NS:2 * NS + 1], hcol[0:SH, 2:3]))
                    link(v.tensor_copy(ex[:, NS:2 * NS], w0[0:SH, NP:T]), fd_sp)
                elif k == "ft":
                    ps = filled(dve, j)
                    v.tensor_copy(tokc[:, 0:64].rearrange("p (a h) -> p a h", a=2),
                                  ps[:, 0:96].rearrange("p (a h) -> p a h", a=2)[:, :, 0:SH])
                    v.tensor_copy(tokc[:, 64:224], ps[:, 144:304])
                    v.tensor_copy(lft[:, 0:2, :], ps[:, 0:96].rearrange("p (a h) -> p a h", a=2)[:, :, SH:HB])
                    release(dve, v.tensor_copy(lft[0:NS, 2, :], ps[0:NS, 96 + SH:96 + HB]), j)
                    dve.wait_ge(consts, 4)
                    link(v.tensor_tensor(lfn[0:NS, :].rearrange("p (b h) -> p b h", b=NS),
                                         lft[0:NS, 2:3, :].to_broadcast([NS, NS, NH]),
                                         bm8[:].rearrange("p (b h) -> p b h", b=NS), ALU.mult), lfn_ready)
                elif k in ("kn", "qn"):
                    c0 = 8 if k == "kn" else 4 * (j[1] // 4)
                    base = j[1] - j[1] % 4
                    if j[1] % 4 == 0:
                        for i in range(4):
                            read_out(dve, (k[0], base + i))
                        link(v.tensor_tensor(u[:, 0:4, :], qkT[:, c0:c0 + 4, :], qkT[:, c0:c0 + 4, :], ALU.mult), qk_sq)
                    elif j[1] % 4 == 3:
                        for i in range(4):
                            read_out(dve, (k, base + i))
                        link(v.reciprocal(rs[:], rs[:]))
                        col = gqk[:, 1:2] if k == "kn" else gqk[:, 0:1]
                        link(v.scalar_tensor_tensor(qkT[:, c0:c0 + 4, :], qkT[:, c0:c0 + 4, :], col, rs[:],
                                                    ALU.mult, ALU.mult), qk_ready)
                        if j == ("qn", 7):
                            dve.wait_ge(qbd_zero, 1)
                            for h in range(2):
                                dst = qbd[64 * h:64 * h + 64, 2 * h:2 * h + 4224]\
                                    .rearrange("p (b m x) -> p b m x", b=NS, m=4)[:, :, :, 0:2]
                                qs = qkT[64 * h:64 * h + 64, 0:8, NP:T].rearrange("p (m s) b -> p b m s", s=2)
                                link(v.tensor_copy(dst, qs), qbd_ready)
                elif k == "s":
                    ps, p = filled(dve, j), j[2]
                    release(dve, v.tensor_tensor(pb[:, p, :], ps[:, 0:384], cmask[:], ALU.add), j)
                    for q, (lo, hi) in enumerate(((0, 128), (128, 384))):
                        link(v.tensor_reduce(sm2[:, 4 * p + q:4 * p + q + 1], pb[:, p, lo:hi], AX.X, ALU.max, negate=True),
                             s_max if q else dve_step)
                elif k == "sc":
                    p = j[2]
                    dve.wait_ge(s_exp, 2 * j[1] + p + 1)
                    link(v.reciprocal(sm2[:, 4 * p + 2:4 * p + 4], sm2[:, 4 * p + 2:4 * p + 4]))
                    for q, (lo, hi) in enumerate(((0, 128), (128, 384))):
                        link(v.tensor_scalar(pb[:, p, lo:hi], pb[:, p, lo:hi], sm2[:, 4 * p + 2 + q:4 * p + 3 + q], None,
                                             ALU.mult), p_ready if q else dve_step)
                elif k == "xbc":
                    i, x = j[1], xa[:, j[1] % 2, :]
                    read_out(dve, j)
                    xs4 = x[:, 3 + NP:XW].rearrange("p (b w) -> p b w", w=4)
                    link(v.tensor_copy(xs4[:, :, 0:3], stT[:, i, :].rearrange("p (b w) -> p b w", w=3)))
                    link(v.tensor_copy(tails[:, i, 0:24].rearrange("p (b w) -> p b w", w=3), xs4[:, :, 1:4]))
                    link(v.tensor_copy(tails[:, i, 24:27], x[:, NP:NP + 3]))
                    if i >= 2:
                        dve.wait_ge(u_ready, i - 1)
                    acc = cacc[:, i % 2, :]
                    link(v.tensor_scalar(acc, x[:, 0:XO], vec[:, 104 + i:105 + i], vec[:, 80 + i:81 + i], ALU.mult, ALU.add))
                    for w in range(1, 4):
                        link(v.scalar_tensor_tensor(acc, x[:, w:w + XO], vec[:, 104 + 24 * w + i:105 + 24 * w + i], acc,
                                                    ALU.mult, ALU.add), conv_ready if w == 3 else dve_step)
                elif k == "sk" and j[2] == 1:
                    filled(dve, j)
                    link(v.tensor_copy(ktb[:, j[1] % 2, :, 256], qkT[:, 8:12, NP + j[1]]), kcol_ready)
                elif k == "sp":
                    dve.wait_ge(ss_done, 1)
                    link(v.tensor_reduce(sm2[:, 8:9], sbank[:, 0:257], AX.X, ALU.max, negate=True), ss_max)
                    dve.wait_ge(ss_exp, 1)
                    link(v.reciprocal(sm2[:, 9:10], sm2[:, 9:10]))
                    link(v.tensor_scalar(ps_s, ps_s, sm2[:, 9:10], None, ALU.mult))
                    link(v.tensor_scalar(pnb, bm2[:], ps_s[:, 256:257], None, ALU.mult), sp_ready)
                elif k == "sx":
                    ps, hf = filled(dve, j), j[1]
                    for m in range(4):
                        for h in range(2):
                            x = 4 * m + 2 * h
                            ins = v.tensor_copy(
                                attT[64 * h:64 * h + 64, 2 * m:2 * m + 2, NP + 4 * hf:NP + 4 * hf + 4].rearrange("p s b -> p b s"),
                                ps[64 * h:64 * h + 64, 128 * m:128 * m + 128].rearrange("p (b x) -> p b x", b=4)[:, :, x:x + 2])
                    release(dve, ins, j)
                elif k == "exp":
                    ps = filled(dve, j)
                    release(dve, v.tensor_copy(exo[:], ps[:, 0:NXB * 17].rearrange("p (c k) -> p c k", c=NXB)), j)
                    link(v.tensor_tensor(exo[:, :, 0:NS], exo[:, :, 0:NS], u[:, 0:NXB, NP:T], ALU.mult), xds_ready)
                elif k == "xs":
                    ps, a, g = filled(dve, j), j[1], j[2]
                    dve.wait_ge(o_small, 16 * 5)
                    dt = tokc[:, 32 * a + 8 * g:32 * a + 8 * g + 8].unsqueeze(2).to_broadcast([128, 8, HD])
                    release(dve, v.tensor_tensor(xd[:, a, 512 * g:512 * g + 512].rearrange("p (h d) -> p h d", h=8),
                                                 ps.rearrange("p (h d) -> p h d", h=8), dt, ALU.mult), j)
                elif k == "cb":
                    ps = filled(dve, j)
                    release(dve, v.tensor_tensor(cbm, ps.rearrange("p (g k) -> p g k", g=SG),
                                                 triu[:].unsqueeze(1).to_broadcast([128, SG, 128]), ALU.mult), j)
                elif k == "ab":
                    ps, a, b = filled(dve, j), j[1], j[2]
                    if a == 0 and b == 0:
                        dve.wait_ge(bs_out, 16)
                    for i in range(4):
                        h = 4 * b + i
                        if i == 0 and a == 1:
                            dve.wait_ge(et_ready, b + 1)
                        ins = v.tensor_scalar(wd[:, b % 3, 128 * i:128 * i + 128], ps[:, 128 * i:128 * i + 128],
                                              tokc[:, 64 + 32 * a + h:65 + 32 * a + h], 0.0, ALU.subtract, ALU.min)
                    release(dve, ins, j)
                    if b:
                        weigh(a, b - 1)
                elif k == "y":
                    a, b = j[1], j[2]
                    if b == 6:
                        weigh(a, 7)
                    ps = filled(dve, j)
                    for q in range(2):
                        hp, tk = 2 * b + q, slice(128 * a, 128 * a + 128)
                        ins = v.scalar_tensor_tensor(yT[:, hp, tk], u[:, hp, tk], exo[:, hp, 16:17],
                                                     ps[:, 128 * q:128 * q + 128], ALU.mult, ALU.add)
                    release(dve, ins, j)
                    if a == 1:
                        read_out(dve, ("z", 2 * b))
                        read_out(dve, ("z", 2 * b + 1))
                        hp = slice(2 * b, 2 * b + 2)
                        link(v.tensor_tensor(yT[:, hp, 0:NP], yT[:, hp, 0:NP], zb[:, hp, :], ALU.mult), zg_done)
                        link(v.tensor_tensor(u[:, hp, 0:NP], yT[:, hp, 0:NP], yT[:, hp, 0:NP], ALU.mult))
                        v.tensor_tensor(u[:, 2 * b, 0:NP], u[:, 2 * b, 0:NP], u[:, 2 * b + 1, 0:NP], ALU.add)\
                            .then_inc(yp_sq, 1)
                elif k == "ssm":
                    b = j[1]
                    dve.wait_ge(st_full[b % 2], 16 * (b // 2 + 1))
                    for c in range(NXB):
                        if c % 8 == 0:
                            dve.wait_ge(bx_ready, 2 * b + 1 + c // 8)
                        x = sst[b % 2][:, NST * c:NST * c + NST]
                        ins = v.scalar_tensor_tensor(x, x, exo[:, c, NS + b:NS + b + 1], bx[:, NST * c:NST * c + NST],
                                                     ALU.mult, ALU.add)
                        if c % 8 == 7:
                            ins.then_inc(st_new, 1)
                    if b:
                        state_sum(b - 1)
                    if b == NS - 1:
                        state_sum(b)
                        dx = exo[:, :, 16:17].to_broadcast([128, NXB, NS])
                        ys = yT[:, :, NP:T]
                        link(v.tensor_tensor(exo[:, :, 0:NS], u[:, 0:NXB, NP:T], dx, ALU.mult))
                        link(v.tensor_tensor(ys, ys, exo[:, :, 0:NS], ALU.add))
                        link(v.tensor_tensor(ys, ys, zsS[:], ALU.mult))
                        link(v.tensor_tensor(exo[:, :, 0:NS], ys, ys, ALU.mult))
                        link(v.tensor_reduce(sm2[:, 0:32].rearrange("p (g b) -> p g b", g=SG),
                                             exo[:, :, 0:NS].rearrange("p (g c) b -> p g b c", g=SG), AX.X, ALU.add), y_sq)
                elif k == "yp":
                    g = j[1]
                    read_out(dve, j)
                    link(v.reciprocal(rs[:, g, 0:NP], rs[:, g, 0:NP]))
                    for c in range(4 * g, 4 * g + 4):
                        ins = v.scalar_tensor_tensor(yT[:, c, 0:NP], yT[:, c, 0:NP], vec[:, 64 + c:65 + c], rs[:, g, 0:NP],
                                                     ALU.mult, ALU.mult)
                    link(ins, y_ready)
                elif k == "yn":
                    read_out(dve, j)
                    link(v.reciprocal(sm2[:, 32:64], sm2[:, 32:64]))
                    link(v.tensor_tensor(yT[:, :, NP:T], yT[:, :, NP:T],
                                         vec[:, 64:64 + NXB].unsqueeze(2).to_broadcast([128, NXB, NS]), ALU.mult))
                    for g in range(SG):
                        y4 = yT[:, 4 * g:4 * g + 4, NP:T]
                        r4 = sm2[:, 32 + NS * g:40 + NS * g].unsqueeze(1).to_broadcast([128, 4, NS])
                        ins = v.tensor_tensor(y4, y4, r4, ALU.mult)
                    link(ins, y_ready)
                elif k == "pa":
                    ps, i = filled(dve, j), j[1]
                    read_out(dve, ("g", i))
                    release(dve, v.tensor_tensor(gT[:, i, :], gT[:, i, :], ps[:, 0:T], ALU.mult), j)
                elif k == "pb":
                    ps, i = filled(dve, j), j[1]
                    read_out(dve, ("g", 8 + i))
                    release(dve, v.tensor_tensor(gT[:, 8 + i, :], gT[:, 8 + i, :], ps[:, 0:T], ALU.mult), j)
                    link(v.tensor_tensor(gT[:, i, :], gT[:, i, :], gT[:, 8 + i, :], ALU.add), m_ready)
                elif k == "o":
                    ps, i = filled(dve, j), j[1]
                    v.scalar_tensor_tensor(xT[:, i, 0:NP], ps[:, 0:NP], modT[:, 16 + i, NS:NC], xT[:, i, 0:NP],
                                           ALU.mult, ALU.add)
                    release(dve, v.tensor_tensor(sm2[:, 16:24], ps[:, NP:T], modT[:, 16 + i, 0:NS], ALU.mult), j)
                    link(v.tensor_tensor(xT[:, i, NP:T], xT[:, i, NP:T], sm2[:, 16:24], ALU.add))
                    square(i)
                elif k == "lr":
                    ps = filled(dve, j)
                    release(dve, v.tensor_scalar(lgT[0:NE, :], ps[0:NE, 0:T], brow[:], None, ALU.add), j)
                elif k == "lt":
                    link(v.memset(lg, 0.0))
                    ps = filled(dve, j)
                    v.tensor_copy(lg[:, 0:2, :], ps[:, 0:32].rearrange("p (a e) -> p a e", a=2))
                    release(dve, v.tensor_copy(lg[0:NS, 2, :], ps[0:NS, 32:48]), j)
                    route()
                elif k == "rk":
                    ps = filled(dve, j)
                    v.tensor_copy(rank, ps[:, 0:48].rearrange("p (a e) -> p a e", a=3))
                    release(dve, v.tensor_copy(cnt, ps[:, 48:64]), j)
                    link(v.tensor_reduce(rw[0][0:1, 0:1], cnt[0:1, :], AX.X, ALU.max))
                    link(v.tensor_scalar(rt[0][0:1, 0, :], thr[:], rw[0][0:1, 0:1], None, ALU.is_lt))
                    link(v.tensor_reduce(rw[1][0:1, 0:1], rt[0][0:1, 0, :], AX.X, ALU.add))
                    link(v.tensor_scalar(rounds_sb[:], rw[1][0:1, 0:1], 1.0, None, ALU.add), rk_ready)

            def select(t, q):
                dve.wait_ge(selT_done, t + 1)
                for w, m in enumerate((asg, cmb)):
                    for e in range(4):
                        for a in range(3):
                            col = bass.ds(q * 4 + e, 1)
                            ins = v.tensor_scalar(sel[:, w, a, BLK * e:BLK * e + BLK], iota[:], rank[:, a, col], m[:, a, col],
                                                  ALU.is_equal, ALU.mult)
                    ins.then_inc((sel_ready, selw_ready)[w], 1)

            def gathered(t):
                for s in range(4):
                    dve.wait_ge(gath_filled, t * 4 + (s + 1))
                    v.tensor_copy(xg[:, 2 * s:2 * s + 2, :], banks[(7, 4)[s % 2]][:].rearrange("p (k s) -> p k s", k=2))\
                        .then_inc(xg_ready, 1)

            def multiply(it):
                dve.wait_ge(silu_ready, it + 2)
                dve.wait_ge(up_done, it + 2)
                v.tensor_tensor(hact, gact, banks[1][:], ALU.mult).then_inc(act_ready, 1)

            def combined(it):
                dve.wait_ge(comb_read, it * 8 + 1)
                for c in range(KD):
                    dve.wait_ge(comb_filled, it * 8 + (c + 1))
                    v.tensor_tensor(Y[:, c, :], Y[:, c, :], banks[5 + c % 2][:, 0:T], ALU.add).then_inc(comb_read, 1)

            def four(r, q, last):
                it = r * 8 + q * 2
                multiply(it)
                if not last:
                    select(r * 4 + (q + 1), q + 1)
                multiply(it + 1)
                combined(it)
                if not last:
                    gathered(r * 4 + (q + 1))
                combined(it + 1)

            rounds = dve.value_load(rounds_sb[0:1, 0:1], min_val=1, max_val=5)
            dve.wait_ge(y_zero, 1)
            with dve.Fori(0, rounds) as r:
                dve.wait_ge(rk_shift, r + 1)
                select(r * 4, 0)
                gathered(r * 4)
                with dve.Fori(0, NE // 4 - 1) as q:
                    four(r, q, False)
                four(r, NE // 4 - 1, True)
                dve.wait_ge(comb_read, r * 64 + 65)
                v.tensor_scalar(rank, rank, -float(BLK), None, ALU.add).then_inc(rk_shift, 1)
            link(v.tensor_tensor(Y[:, :, NP:T], Y[:, :, NP:T], modT[:, 40:48, 0:NS], ALU.mult))
            v.tensor_tensor(xT[:, :, NP:T], xT[:, :, NP:T], Y[:, :, NP:T], ALU.add).then_inc(yfin, 1)
            for c in range(KD):
                v.scalar_tensor_tensor(xT[:, c, 0:NP], Y[:, c, 0:NP], modT[:, 40 + c, NS:NC], xT[:, c, 0:NP],
                                       ALU.mult, ALU.add).then_inc(yfin, 1)

        @block.tensor
        def _(pe):
            mm, tr = nc.tensor.matmul, nc.tensor.transpose
            for s in (selT_done, gate_done, up_done, down_done):
                pe.sem_inc(s, 1)

            def start(j):
                b, n = bank_of[j]
                if n > 1:
                    pe.wait_ge(bank_read[b], n - 1)
                return banks[b]

            def done(ins, j):
                ins.then_inc(bank_filled[bank_of[j][0]], 1)

            def landed(s):
                pe.wait_ge(slot_full[slot_at[s]], arrived_at[s])

            def flip(out, x):
                k = x.shape[0]
                return tr(out, x, ident[0:k, 0:k])

            for j in jobs:
                k = j[0]
                ps = start(j) if j in bank_of else None
                if k == "cT":
                    pe.wait_ge(consts, 1)
                    pe.wait_ge(cond_ready, 1)
                    for c in range(KD):
                        ins = flip(ps[:, NC * c:NC * c + NC], crow[0:NC, 128 * c:128 * c + 128])
                elif k == "vecs":
                    flip(ps[:, 0:104], vrow[0:104, 0, :])
                    ins = flip(ps[:, 104:200], vrow[0:96, 1, :])
                elif k == "mod":
                    read_out(pe, ("cT",))
                    for i in range(4):
                        landed(("mod", 4 * j[1] + i))
                    for c in range(KD):
                        for i in range(4):
                            ins = mm(ps[32 * i:32 * i + 32, 0:SW], cT[:, c, :], slot(("mod", 4 * j[1] + i))[:, c, :],
                                     start=c == 0, stop=c == KD - 1, tile_position=(0, 32 * i))
                elif k == "modt":
                    read_out(pe, ("mod", j[1]))
                    for q in range(2):
                        ins = flip(ps[:, 128 * q:128 * q + 128], mrow[:, 128 * q:128 * q + 128])
                elif k == "xt":
                    a, f, n = j[1], j[2], TOK[j[1]][1]
                    pe.wait_ge(x_in, 48)
                    for q in range(4):
                        c = 4 * f + q
                        ins = flip(ps[:, n * q:n * q + n], xin[0:n, a, 128 * c:128 * c + 128])
                elif k == "ssq":
                    pe.wait_ge(consts, 3)
                    for c in range(KD):
                        pe.wait_ge(sq_ready, KD * j[1] + c + 1)
                        ins = mm(ps[:, 0:T], onesf[:], u[:, c, :], start=c == 0, stop=c == KD - 1)
                elif k == "cst":
                    pe.wait_ge(st_in, 16)
                    for q in range(12):
                        c = 12 * j[1] + q
                        ins = flip(ps[:, 24 * q:24 * q + 24], csin[0:24, 128 * c:128 * c + 128])
                elif k == "fd":
                    pe.wait_ge(late_in, 16 * 12)
                    pe.wait_ge(h_samples, 1)
                    for c in range(KD):
                        pe.wait_ge(h_ready, c + 1)
                        ins = mm(ps[0:HB, 0:T], wfd[:, c, :], hT[:, c, :], start=c == 0, stop=c == KD - 1)
                elif k == "ft":
                    pe.wait_ge(fd_e, 1)
                    for a, (t0, n) in enumerate(TOK):
                        ins = flip(ps[0:n, HB * a:HB * a + HB], fd[:, t0:t0 + n])
                    for i, x in enumerate((acsT[0:SH, 0:128], acsT[0:SH, 128:256], fdw[0:SH, 1, 0:128],
                                           fdw[0:SH, 1, 128:256], fdw[0:SH, 2, 0:128])):
                        ins = flip(ps[:, 144 + 32 * i:176 + 32 * i], x)
                elif k in ("q", "k", "v", "xbc", "z", "g"):
                    s, h = slots_of(j)[0], j[1] % 2
                    landed(s)
                    for c in range(KD):
                        w = slot(s)[:, c, 128 * h:128 * h + 128]
                        ins = mm(ps[:, 0:T], w, hT[:, c, :], start=c == 0, stop=c == KD - 1)
                elif k in ("kn", "qn"):
                    pe.wait_ge(qk_sq, 1 if k == "kn" else 2 + j[1] // 4)
                    ins = mm(ps[:, 0:T], blk[:], u[:, j[1] % 4, :], start=True, stop=True)
                elif k == "kt":
                    t0, n = TOK[j[1]]
                    pe.wait_ge(qk_ready, 1)
                    for m in range(4):
                        ins = flip(ps[0:n, 128 * m:128 * m + 128], qkT[:, 8 + m, t0:t0 + n])
                elif k == "vt":
                    t0, n = TOK[j[1]]
                    read_out(pe, ("v", 3))
                    for m in range(4):
                        ins = flip(ps[0:n, 128 * m:128 * m + 128], vT[:, m, t0:t0 + n])
                elif k == "s":
                    c, p = j[1], j[2]
                    m, s, r = c // 2, c % 2, slice(64 * p, 64 * p + 64)
                    h = 4 * m + 2 * p + s
                    pe.wait_ge(qk_ready, 3)
                    pe.wait_ge(fd_e, 1)
                    neg = nident[SH:HB, SH + h:SH + h + 1].to_broadcast([NH, 128])
                    for q0, lo, n in ((0, 0, 128), (128, 128, 256)):
                        mm(ps[:, lo:lo + n], qkT[r, c, q0:q0 + 128], qkT[r, 8 + m, 0:n], start=True, stop=False)
                        ins = mm(ps[:, lo:lo + n], neg, acsT[SH:HB, 0:n], start=False, stop=True)
                elif k == "pt":
                    p = j[2]
                    pe.wait_ge(p_ready, 2 * j[1] + p + 1)
                    for q in range(3):
                        ins = flip(ps[:, 128 * q:128 * q + 128], pb[:, p, 128 * q:128 * q + 128])
                elif k == "o2":
                    c = j[1]
                    for p in range(2):
                        read_out(pe, ("pt", c, p))
                        g = 2 * (c // 2) + p
                        vs = [vtok[:, a, 64 * g:64 * g + 64] for a in range(2)]
                        r = slice(64 * p, 64 * p + 64)
                        mm(ps[r, 0:128], vs[0], pT[:, p, 0:128], start=True, stop=True)
                        mm(ps[r, 128:256], vs[0], pT[:, p, 128:256], start=True, stop=False)
                        ins = mm(ps[r, 128:256], vs[1], pT[:, p, 256:384], start=False, stop=True)
                elif k == "sk":
                    b, q = j[1], j[2]
                    pe.wait_ge(kv_full[b % 4], 32 * (b // 4 + 1))
                    for m in range(4):
                        ins = flip(ps[:, 128 * m:128 * m + 128], kvr[:, b % 4, q, 128 * m:128 * m + 128])
                elif k == "ss":
                    b = j[1]
                    read_out(pe, ("sk", b, 0))
                    read_out(pe, ("sk", b, 1))
                    pe.wait_ge(kcol_ready, b + 1)
                    pe.wait_ge(qbd_ready, 2)
                    for m in range(4):
                        o = 128 * (4 * b + m)
                        mm(sbank[:, 0:257], qbd[:, o:o + 128], ktb[:, b % 2, m, :], start=b == 0 and m == 0, stop=False)
                    if b == NS - 1:
                        pe.wait_ge(lf_in, 16 * NS * NPG)
                        pe.wait_ge(lfn_ready, 1)
                        mm(sbank[:, 0:257], lfc[:, 0, :], ntri[:, 128:385], start=False, stop=False)
                        mm(sbank[:, 0:257], lfc[:, 1, :], ntri[:, 0:257], start=False, stop=False)
                        mm(sbank[:, 256:257], lfn[0:NS, :], ntri[0:NS, 384:385], start=False, stop=True)\
                            .then_inc(ss_done, 1)
                    continue
                elif k == "sp":
                    pe.wait_ge(sp_ready, 1)
                    for q in range(NPG):
                        flip(ps[:, 128 * q:128 * q + 128], ps_s[:, 128 * q:128 * q + 128])
                    ins = mm(ps[0:NS, 256:384], pnb, ident[:], start=True, stop=True)
                elif k == "so":
                    hf = j[1]
                    read_out(pe, ("sp",))
                    for b in range(4):
                        pe.wait_ge(kv_full[b], 96 + 32 * hf)
                    for q in range(NPG + 1):
                        for bb in range(4):
                            c = 16 * (4 * hf + bb)
                            w, x = ((psT[:, q, c:c + 32], kvr[:, bb, q, :]) if q < NPG else
                                    (pn[0:NS, c:c + 32], vtok[0:NS, 2, :]))
                            ins = mm(ps[32 * bb:32 * bb + 32, :], w, x, start=q == 0, stop=q == NPG,
                                     tile_position=(0, 32 * bb))
                elif k == "sx":
                    read_out(pe, ("so", j[1]))
                    for m in range(4):
                        ins = flip(ps[:, 128 * m:128 * m + 128], otok[:, 128 * m:128 * m + 128])
                elif k == "ct":
                    pe.wait_ge(conv_ready, NCB)
                    for q in range(4):
                        ins = flip(ps[0:27, 128 * q:128 * q + 128], tails[:, 4 * j[1] + q, :])
                elif k == "bs":
                    pe.wait_ge(u_ready, NCB)
                    for q in range(4):
                        ins = flip(ps[0:NS, 128 * q:128 * q + 128], u[:, NXB + 4 * j[1] + q, NP:T])
                elif k == "exp":
                    for c in range(NXB):
                        for h in range(2):
                            w = ident[0:SH, 2 * c + h:2 * c + h + 1].to_broadcast([SH, 64])
                            ins = mm(ps[64 * h:64 * h + 64, 17 * c:17 * c + 17], w, ex[:], start=True, stop=True)
                elif k == "bt":
                    for q in range(4):
                        ins = flip(ps[:, 128 * q:128 * q + 128], u[:, NXB + q, 128 * j[1]:128 * j[1] + 128])
                elif k == "xs":
                    a, g = j[1], j[2]
                    for q in range(4):
                        ins = flip(ps[:, 128 * q:128 * q + 128], u[:, 4 * g + q, 128 * a:128 * a + 128])
                elif k == "s1":
                    g = j[1]
                    read_out(pe, ("bt", 0))
                    pe.wait_ge(xe_ready, 1)
                    ins = mm(ps[:], btok[:, 0, 128 * g:128 * g + 128], xe[:, 0, 512 * g:512 * g + 512],
                             start=True, stop=True)
                elif k == "cb":
                    tk = slice(128 * j[1], 128 * j[1] + 128)
                    for g in range(SG):
                        ins = mm(ps[:, 128 * g:128 * g + 128], u[:, NXB + g, tk], u[:, NXB + SG + g, tk],
                                 start=True, stop=True)
                elif k == "ab":
                    a, b = j[1], j[2]
                    for i in range(4):
                        h = 4 * b + i
                        ins = mm(ps[:, 128 * i:128 * i + 128], ident[0:SH, h:h + 1].to_broadcast([SH, 128]),
                                 acsT[0:SH, 128 * a:128 * a + 128], start=True, stop=True)
                elif k == "y":
                    a, b = j[1], j[2]
                    pe.wait_ge(w_ready, 8 * a + b + 1)
                    read_out(pe, ("xs", a, b // 2))
                    if a == 1:
                        pe.wait_ge(ce_ready, b + 1)
                        read_out(pe, ("s1", 3))
                    for i in range(4):
                        h = 4 * b + i
                        o = ps[64 * (i % 2):64 * (i % 2) + 64, 128 * (i // 2):128 * (i // 2) + 128]
                        ins = mm(o, xd[:, a, 64 * h:64 * h + 64], wd[:, b % 3, 128 * i:128 * i + 128],
                                 start=True, stop=a == 0)
                        if a == 1:
                            ins = mm(o, s1T[:, 64 * h:64 * h + 64], ce[:, b % 3, 128 * i:128 * i + 128],
                                     start=False, stop=True)
                elif k == "fs":
                    i = j[1]
                    pe.wait_ge(xe_ready, 3)
                    read_out(pe, ("bt", 1))
                    for q in range(4):
                        c = 4 * i + q
                        for a in range(2):
                            ins = mm(ps[:, 128 * q:128 * q + 128], xe[:, a, 128 * c:128 * c + 128],
                                     btok[:, a, 128 * i:128 * i + 128], start=a == 0, stop=a == 1)
                elif k in ("ssm", "sc"):
                    continue
                elif k == "pa":
                    i = j[1]
                    s = slots_of(j)[0]
                    landed(s)
                    read_out(pe, ("o2", 7))
                    read_out(pe, ("sx", 1))
                    for c in range(KD):
                        ins = mm(ps[:, 0:T], slot(s)[:, c, 128 * (i % 2):128 * (i % 2) + 128], attT[:, c, :],
                                 start=c == 0, stop=c == KD - 1)
                elif k == "yp":
                    for q in range(2):
                        b = 2 * j[1] + q
                        pe.wait_ge(yp_sq, b + 1)
                        ins = mm(ps[:, 0:NP], onesf[:], u[:, 2 * b, 0:NP], start=q == 0, stop=q == 1)
                elif k == "yn":
                    pe.wait_ge(y_sq, 1)
                    ins = mm(ps[:, 0:32], onesf[:], sm2[:, 0:32], start=True, stop=True)
                elif k == "pb":
                    i = j[1]
                    for s in slots_of(j):
                        landed(s)
                    for c in range(NXB):
                        if i == 0 and c == 0:
                            pe.wait_ge(y_ready, SG + 1)
                        w = slot(("pb", i // 2, c // KD))[:, c % KD, 128 * (i % 2):128 * (i % 2) + 128]
                        ins = mm(ps[:, 0:T], w, yT[:, c, :], start=c == 0, stop=c == NXB - 1)
                elif k == "o":
                    i = j[1]
                    s = slots_of(j)[0]
                    landed(s)
                    for c in range(KD):
                        if i == 0:
                            pe.wait_ge(m_ready, c + 1)
                        ins = mm(ps[:, 0:T], slot(s)[:, c, 128 * (i % 2):128 * (i % 2) + 128], gT[:, c, :],
                                 start=c == 0, stop=c == KD - 1)
                elif k == "lr":
                    pe.wait_ge(h_samples, 2)
                    for c in range(KD):
                        pe.wait_ge(h_ready, KD + 1 + c)
                        ins = mm(ps[0:NE, 0:T], wr[:, c, :], hT[:, c, :], start=c == 0, stop=c == KD - 1)
                elif k == "lt":
                    read_out(pe, ("lr",))
                    for a, (t0, n) in enumerate(TOK):
                        ins = flip(ps[0:n, NE * a:NE * a + NE], lgT[0:NE, t0:t0 + n])
                elif k == "ht":
                    a, f, (t0, n) = j[1], j[2], TOK[j[1]]
                    for q in range(4):
                        ins = flip(ps[0:n, 128 * q:128 * q + 128], hT[:, 4 * f + q, t0:t0 + n])
                elif k == "rk":
                    pe.wait_ge(asg_ready, 2)
                    for a in range(4):
                        for b in range(min(a + 1, 3)):
                            n = TOK[b][1]
                            ins = mm(ps[:, NE * a:NE * a + NE], (striu if a == b else onesb)[0:n, :], asb[0:n, b, :],
                                     start=b == 0, stop=b == min(a, 2))
                done(ins, j)

            for b in range(NBANK):
                pe.wait_ge(bank_read[b], at_moe[b])
            pe.wait_ge(rk_ready, 1)

            def gather(t):
                pe.wait_ge(sel_ready, t + 1)
                for s in range(4):
                    pe.wait_ge(xg_ready, t * 4 + (s + 1))
                    for k in range(2):
                        c = 2 * s + k
                        for a, (t0, n) in enumerate(TOK):
                            ins = mm(banks[(7, 4)[s % 2]][:, 256 * k:256 * k + 256], h2tok[0:n, a, 128 * c:128 * c + 128],
                                     sel[0:n, 0, a, :], start=a == 0, stop=a == 2)
                    ins.then_inc(gath_filled, 1)

            def gate_up(it, p):
                for i, sig in enumerate((gate_done, up_done)):
                    for e in range(2):
                        pe.wait_ge(moe_full[2 * i + e], (it + 1) * 16)
                    for c in range(KD):
                        for e in range(2):
                            w = mslot[2 * i + e].rearrange("p (k n) -> p k n", k=KD)
                            ins = mm(banks[i][BLK * e:BLK * e + BLK, :], xg[:, c, BLK * (2 * p + e):BLK * (2 * p + e + 1)],
                                     w[:, c, :], start=c == 0, stop=c == KD - 1, tile_position=(0, BLK * e))
                    ins.then_inc(sig, 1)

            def down(it):
                pe.wait_ge(act_ready, it + 2)
                for q in range(4):
                    ins = flip(banks[4][:, 128 * q:128 * q + 128], hact[:, 128 * q:128 * q + 128])
                ins.then_inc(actT_done, 1)
                pe.wait_ge(actT_ready, it + 1)
                for q in range(2):
                    pe.wait_ge(moe_full[4 + q], (it + 1) * 32)
                    for c in range(4):
                        for e in range(2):
                            r = slice(BLK * e, BLK * e + BLK)
                            ins = mm(banks[2 + q][r, :], aT[:, c, r], down_slot(q)[:, e, c, :], start=c == 0,
                                     stop=c == 3, tile_position=(0, BLK * e))
                    ins.then_inc(down_done, 1)

            def combine(it, p):
                for c in range(KD):
                    if c % 4 == 0:
                        pe.wait_ge(out_ready, it * 2 + (c // 4 + 1))
                    pe.wait_ge(comb_read, it * 8 + max(c, 1))
                    mm(banks[5 + c % 2][:, 0:T], outs[:, 128 * c:128 * c + 128], selT[:, p, :], start=True, stop=True)\
                        .then_inc(comb_filled, 1)

            def four(r, q, last):
                t, it = r * 4 + q, r * 8 + q * 2
                pe.wait_ge(xg_ready, t * 4 + 6)
                gate_up(it, 0)
                pe.wait_ge(selw_ready, t + 1)
                for p in range(2):
                    for a, (t0, n) in enumerate(TOK):
                        ins = flip(banks[2 + p][:, t0:t0 + n], sel[0:n, 1, a, 128 * p:128 * p + 128])
                ins.then_inc(selT_done, 1)
                pe.wait_ge(selT_ready, t + 1)
                down(it)
                gate_up(it + 1, 1)
                combine(it, 0)
                down(it + 1)
                if not last:
                    gather(t + 1)
                combine(it + 1, 1)

            rounds = pe.value_load(rounds_sb[0:1, 0:1], min_val=1, max_val=5)
            with pe.Fori(0, rounds) as r:
                gather(r * 4)
                with pe.Fori(0, NE // 4 - 1) as q:
                    four(r, q, False)
                four(r, NE // 4 - 1, True)
            for j in late:
                a, f, (t0, n) = j[1], j[2], TOK[j[1]]
                pe.wait_ge(yfin, 4 * f + 5)
                ps = start(j)
                for q in range(4):
                    ins = flip(ps[0:n, 128 * q:128 * q + 128], xT[:, 4 * f + q, t0:t0 + n])
                done(ins, j)


OUTS = [("y_prompt", (1, NP, D)), ("y_sample", (NS, 1, D)), ("k_prompt", (1, 1, NP, NKV, HD)),
        ("v_prompt", (1, 1, NP, NKV, HD)), ("logf_prompt", (1, 1, NP, NH)), ("ssm_prompt", (1, 1, SH, HD, NST)),
        ("conv_prompt", (1, 1, 3, CD)), ("k_sample", (1, NS, 1, NKV, HD)), ("v_sample", (1, NS, 1, NKV, HD)),
        ("logf_sample", (1, NS, 1, NH)), ("ssm_sample", (1, NS, SH, HD, NST)), ("conv_sample", (1, NS, 3, CD))]


def kernel(**inputs):
    import numpy as np
    import concourse.bacc as bacc
    from concourse.bass_utils import run_bass_kernel_spmd

    nc = bacc.Bacc("TRN2", target_bir_lowering=False, num_devices=1)
    arrays, t = {}, {}
    for name, x in inputs.items():
        a = np.ascontiguousarray(x)
        arrays["in_" + name] = a
        t[name] = nc.dram_tensor("in_" + name, a.shape, mybir.dt.from_np(a.dtype), kind="ExternalInput").ap()
    for name, shape in OUTS:
        t[name] = nc.dram_tensor("out_" + name, shape, F32, kind="ExternalOutput").ap()
    t["bc_scratch"] = nc.dram_tensor("bc_scratch", (NS, 2 * SG * NST), F32, kind="Internal").ap()
    build(nc, t)
    r = run_bass_kernel_spmd(nc, [arrays], core_ids=[0])
    return tuple(r.results[0]["out_" + name] for name, _ in OUTS)
```
